# Optimizing a Trainium2 kernel written in Bass

```python
import jax, jax.numpy as jnp
from jax import lax
import numpy as np

'''Hybrid decoder trunk: DEPTH layers of
  h = h + W_o( sum_i sigmoid(G_i xn) * P_i(mixer_i(xn)) ),  xn = RMSNorm(h)
  h = h + HierMoE(RMSNorm(h))
with mixers: (A) native sparse attention (compressed / selected / sliding-window
branches, ALiBi), (B) causal multi-scale pooling, (C) short gated causal conv.
All mixers read one combined input projection of xn. Final RMSNorm.
Input x: (BATCH, SEQ, D_MODEL) float32. Output: (BATCH, SEQ, D_MODEL).
'''

D_MODEL = 1024
BATCH = 1
SEQ = 256
DEPTH = 1

HEAD_DIM = 64
NSA_HEADS = D_MODEL // 128
NSA_KV_HEADS = 2
NSA_GROUP = NSA_HEADS // NSA_KV_HEADS
CMP_LEN = 32
CMP_STRIDE = 16
CMP_HIDDEN = 4 * HEAD_DIM
SLC_BLOCK = 64
SLC_TOPN = 16
WINDOW = 512
Q_BLOCK = 128
NSA_BRANCHES = 3
POOL_WINDOWS = (2, 4, 8, 16)
POOL_WIDTH = D_MODEL // 4
POOL_GROUP_DIM = POOL_WIDTH // 4
CONV_WIDTH = D_MODEL // 4
CONV_K = 3
N_BRANCHES = 3
NSA_Q_DIM = NSA_HEADS * HEAD_DIM
NSA_KV_DIM = 6 * NSA_KV_HEADS * HEAD_DIM
NSA_GATE_DIM = NSA_HEADS * NSA_BRANCHES
MERGE_GATE_DIM = N_BRANCHES * D_MODEL
IN_SIZES = (NSA_Q_DIM, NSA_KV_DIM, NSA_GATE_DIM, POOL_WIDTH, CONV_WIDTH, CONV_WIDTH, CONV_WIDTH, MERGE_GATE_DIM)
IN_DIM = NSA_Q_DIM + NSA_KV_DIM + NSA_GATE_DIM + POOL_WIDTH + 3 * CONV_WIDTH + MERGE_GATE_DIM
N_EXPERT_GROUPS = 4
EXPERTS_PER_GROUP = 8
N_EXPERTS = N_EXPERT_GROUPS * EXPERTS_PER_GROUP
EXPERT_TOP_K = 2
D_EXPERT = D_MODEL // 4

RMS_EPS = 1e-6
NEG_INF = -1e30
FORCE_SCORE = 1e30

kernel_name = 'nsa_pool_conv_hier_moe_hybrid'

def rms_norm(x, g):
    xf = x.astype(jnp.float32)
    y = xf * lax.rsqrt(jnp.mean(xf * xf, axis=-1, keepdims=True) + RMS_EPS)
    return (y * g.astype(jnp.float32)).astype(x.dtype)

def alibi_slopes(n_heads):
    return jnp.exp2(-8.0 * jnp.arange(1, n_heads + 1, dtype=jnp.float32) / n_heads)

def masked_softmax(s, mask):
    s = jnp.where(mask, s, NEG_INF)
    return jnp.where(mask, jax.nn.softmax(s, axis=-1), 0.0)

def compress_tokens(k, pe, w1, w2):
    B, T, G, Dh = k.shape
    n_sub = CMP_LEN // CMP_STRIDE
    n_cmp = T // CMP_STRIDE - n_sub + 1
    chunks = k.reshape(B, T // CMP_STRIDE, CMP_STRIDE, G, Dh)
    blocks = jnp.concatenate([chunks[:, i:i + n_cmp] for i in range(n_sub)], axis=2)
    blocks = blocks + pe[None, None, :, None, :]
    flat = blocks.transpose(0, 1, 3, 2, 4).reshape(B, n_cmp, G, CMP_LEN * Dh)
    return jax.nn.gelu(flat @ w1) @ w2

def nsa_mixer(q, kv, gate_logits, cmp_pe, cmp_w1, cmp_w2):
    B, T, _ = q.shape
    G, R, Dh = NSA_KV_HEADS, NSA_GROUP, HEAD_DIM
    q = q.reshape(B, T, G, R, Dh)
    kv = kv.reshape(B, T, 6, G, Dh)
    k_cmp = compress_tokens(kv[:, :, 0], cmp_pe[0], cmp_w1[0], cmp_w2[0])
    v_cmp = compress_tokens(kv[:, :, 1], cmp_pe[1], cmp_w1[1], cmp_w2[1])
    n_cmp = k_cmp.shape[1]
    cmp_end = (jnp.arange(n_cmp) * CMP_STRIDE + CMP_LEN - 1).astype(jnp.float32)
    n_slc = T // SLC_BLOCK
    n_sel = min(SLC_TOPN, n_slc)
    ratio = SLC_BLOCK // CMP_STRIDE
    lead = CMP_LEN // CMP_STRIDE - 1
    to_blocks = lambda a: a.reshape(B, n_slc, SLC_BLOCK, G, Dh).transpose(0, 3, 1, 2, 4)
    k_slc, v_slc = to_blocks(kv[:, :, 2]), to_blocks(kv[:, :, 3])
    pad = ((0, 0), (WINDOW, 0), (0, 0), (0, 0))
    k_win, v_win = jnp.pad(kv[:, :, 4], pad), jnp.pad(kv[:, :, 5], pad)
    gates = jax.nn.sigmoid(gate_logits).reshape(B, T, G, R, NSA_BRANCHES)
    slopes = alibi_slopes(NSA_HEADS).reshape(G, R)
    scale = HEAD_DIM ** -0.5
    b_ix = jnp.arange(B)[:, None, None, None]
    g_ix = jnp.arange(G)[None, :, None, None]
    blk_ids = jnp.arange(n_slc)
    n_qb = T // Q_BLOCK

    def block(args):
        qb, qq, gg = args
        t = qb * Q_BLOCK + jnp.arange(Q_BLOCK)
        tf = t.astype(jnp.float32)
        d_c = tf[:, None] - cmp_end[None, :]
        s = jnp.einsum('bqgrd,bcgd->bgrqc', qq, k_cmp).astype(jnp.float32) * scale - slopes[:, :, None, None] * d_c
        p_c = masked_softmax(s, d_c >= 0)
        o_c = jnp.einsum('bgrqc,bcgd->bqgrd', p_c.astype(v_cmp.dtype), v_cmp)
        imp = jnp.pad(p_c.sum(axis=2), ((0, 0), (0, 0), (0, 0), (lead, ratio * n_slc - n_cmp)))
        imp = sum(imp[..., o:o + ratio * n_slc:ratio] for o in range(ratio + lead))
        cur = t // SLC_BLOCK
        valid = blk_ids[None, :] <= cur[:, None]
        forced = (blk_ids[None, :] == 0) | (blk_ids[None, :] == cur[:, None]) | (blk_ids[None, :] == cur[:, None] - 1)
        score = jnp.where(forced, FORCE_SCORE, jnp.where(valid, imp, NEG_INF))
        _, idx = lax.top_k(score, n_sel)
        kb = k_slc[b_ix, g_ix, idx].reshape(B, G, Q_BLOCK, n_sel * SLC_BLOCK, Dh)
        vb = v_slc[b_ix, g_ix, idx].reshape(B, G, Q_BLOCK, n_sel * SLC_BLOCK, Dh)
        pos = (idx[..., None] * SLC_BLOCK + jnp.arange(SLC_BLOCK)).reshape(B, G, Q_BLOCK, n_sel * SLC_BLOCK)
        d_s = (t[:, None] - pos).astype(jnp.float32)
        s = jnp.einsum('bqgrd,bgqkd->bgrqk', qq, kb).astype(jnp.float32) * scale - slopes[None, :, :, None, None] * d_s[:, :, None]
        p_s = masked_softmax(s, (d_s >= 0)[:, :, None])
        o_s = jnp.einsum('bgrqk,bgqkd->bqgrd', p_s.astype(vb.dtype), vb)
        start = qb * Q_BLOCK
        kw = lax.dynamic_slice_in_dim(k_win, start, WINDOW + Q_BLOCK, axis=1)
        vw = lax.dynamic_slice_in_dim(v_win, start, WINDOW + Q_BLOCK, axis=1)
        pos_w = start - WINDOW + jnp.arange(WINDOW + Q_BLOCK)
        d_w = t[:, None] - pos_w[None, :]
        m_w = (pos_w[None, :] >= 0) & (d_w >= 0) & (d_w < WINDOW)
        s = jnp.einsum('bqgrd,bkgd->bgrqk', qq, kw).astype(jnp.float32) * scale - slopes[:, :, None, None] * d_w.astype(jnp.float32)
        p_w = masked_softmax(s, m_w)
        o_w = jnp.einsum('bgrqk,bkgd->bqgrd', p_w.astype(vw.dtype), vw)
        o = gg[..., 0:1] * o_c + gg[..., 1:2] * o_s + gg[..., 2:3] * o_w
        return o.reshape(B, Q_BLOCK, NSA_HEADS * Dh)

    qs = jnp.moveaxis(q.reshape(B, n_qb, Q_BLOCK, G, R, Dh), 1, 0)
    gs = jnp.moveaxis(gates.reshape(B, n_qb, Q_BLOCK, G, R, NSA_BRANCHES), 1, 0)
    out = lax.map(block, (jnp.arange(n_qb), qs, gs))
    return jnp.moveaxis(out, 0, 1).reshape(B, T, NSA_HEADS * Dh)

def pool_mixer(u, w_grp, scale):
    B, T, _ = u.shape
    ug = u.reshape(B, T, len(POOL_WINDOWS), POOL_GROUP_DIM).astype(jnp.float32)
    cs = jnp.pad(jnp.cumsum(ug, axis=1), ((0, 0), (1, 0), (0, 0), (0, 0)))
    t = jnp.arange(T)
    outs = []
    for g, w in enumerate(POOL_WINDOWS):
        lo = jnp.maximum(t + 1 - w, 0)
        cg = cs[:, :, g]
        cnt = (t + 1 - lo).astype(jnp.float32)
        outs.append((cg[:, 1:] - cg[:, lo]) / cnt[None, :, None] - ug[:, :, g])
    pooled = jnp.stack(outs, axis=2).astype(u.dtype)
    mixed = jnp.einsum('btgc,gcd->btgd', pooled, w_grp)
    return mixed.reshape(B, T, POOL_WIDTH) * scale

def short_conv_mixer(h, b_gate, c_gate, conv_w):
    z = c_gate * h
    y = lax.conv_general_dilated(z, conv_w[:, None, :], window_strides=(1,), padding=[(CONV_K - 1, 0)],
                                 dimension_numbers=('NWC', 'WIO', 'NWC'), feature_group_count=z.shape[-1])
    return b_gate * y

def hier_moe(x, wg, bg, we, be, w1, w3, w2):
    B, T, D = x.shape
    n_tok = B * T
    xt = x.reshape(n_tok, D)
    tok = jnp.arange(n_tok)
    g_logits = (xt @ wg + bg).astype(jnp.float32)
    g_prob = jax.nn.softmax(g_logits, axis=-1)
    g_sel = jnp.argmax(g_logits, axis=-1)
    e_logits = (xt @ we + be).astype(jnp.float32).reshape(n_tok, N_EXPERT_GROUPS, EXPERTS_PER_GROUP)
    e_in = e_logits[tok, g_sel]
    top_v, top_i = lax.top_k(e_in, EXPERT_TOP_K)
    top_w = jax.nn.softmax(top_v, axis=-1) * g_prob[tok, g_sel][:, None]
    expert_id = g_sel[:, None] * EXPERTS_PER_GROUP + top_i
    combine = jnp.einsum('nk,nke->ne', top_w, jax.nn.one_hot(expert_id, N_EXPERTS, dtype=jnp.float32)).astype(x.dtype)
    out = jnp.zeros_like(xt)
    for e in range(N_EXPERTS):
        h = jax.nn.silu(xt @ w1[e]) * (xt @ w3[e])
        out = out + combine[:, e:e + 1] * (h @ w2[e])
    return out.reshape(B, T, D)

def setup_inputs(seed: int = 0) -> dict:
    key = jax.random.key(seed)
    ks = jax.random.split(key, 24)
    nrm = lambda k, shape, s: jax.random.normal(k, shape, jnp.float32) * s
    L, D = DEPTH, D_MODEL
    return {
        'x': nrm(ks[0], (BATCH, SEQ, D), 1.0),
        'norm1_g': 1.0 + nrm(ks[1], (L, D), 0.02),
        'w_in': nrm(ks[2], (L, D, IN_DIM), D ** -0.5),
        'cmp_pe': nrm(ks[3], (L, 2, CMP_LEN, HEAD_DIM), 0.1),
        'cmp_w1': nrm(ks[4], (L, 2, CMP_LEN * HEAD_DIM, CMP_HIDDEN), (CMP_LEN * HEAD_DIM) ** -0.5),
        'cmp_w2': nrm(ks[5], (L, 2, CMP_HIDDEN, HEAD_DIM), CMP_HIDDEN ** -0.5),
        'w_nsa_proj': nrm(ks[6], (L, NSA_Q_DIM, D), NSA_Q_DIM ** -0.5),
        'pool_w': nrm(ks[7], (L, len(POOL_WINDOWS), POOL_GROUP_DIM, POOL_GROUP_DIM), POOL_GROUP_DIM ** -0.5),
        'pool_scale': 1.0 + nrm(ks[8], (L, POOL_WIDTH), 0.02),
        'w_pool_proj': nrm(ks[9], (L, POOL_WIDTH, D), POOL_WIDTH ** -0.5),
        'conv_w': nrm(ks[10], (L, CONV_K, CONV_WIDTH), CONV_K ** -0.5),
        'w_conv_proj': nrm(ks[11], (L, CONV_WIDTH, D), CONV_WIDTH ** -0.5),
        'w_o': nrm(ks[12], (L, D, D), D ** -0.5),
        'norm2_g': 1.0 + nrm(ks[13], (L, D), 0.02),
        'router_group_w': nrm(ks[14], (L, D, N_EXPERT_GROUPS), D ** -0.5),
        'router_group_b': nrm(ks[15], (L, N_EXPERT_GROUPS), 0.01),
        'router_expert_w': nrm(ks[16], (L, D, N_EXPERTS), D ** -0.5),
        'router_expert_b': nrm(ks[17], (L, N_EXPERTS), 0.01),
        'expert_w1': nrm(ks[18], (L, N_EXPERTS, D, D_EXPERT), D ** -0.5),
        'expert_w3': nrm(ks[19], (L, N_EXPERTS, D, D_EXPERT), D ** -0.5),
        'expert_w2': nrm(ks[20], (L, N_EXPERTS, D_EXPERT, D), D_EXPERT ** -0.5),
        'final_norm_g': 1.0 + nrm(ks[21], (D,), 0.02),
    }

def reference(x, norm1_g, w_in, cmp_pe, cmp_w1, cmp_w2, w_nsa_proj, pool_w, pool_scale, w_pool_proj,
              conv_w, w_conv_proj, w_o, norm2_g, router_group_w, router_group_b, router_expert_w,
              router_expert_b, expert_w1, expert_w3, expert_w2, final_norm_g):
    B, T, D = x.shape
    split_at = np.cumsum(IN_SIZES)[:-1].tolist()
    h = x
    for l in range(DEPTH):
        xn = rms_norm(h, norm1_g[l])
        proj = xn @ w_in[l]
        q, kv, nsa_g, pool_u, conv_h, conv_b, conv_c, merge_g = jnp.split(proj, split_at, axis=-1)
        y_nsa = nsa_mixer(q, kv, nsa_g, cmp_pe[l], cmp_w1[l], cmp_w2[l]) @ w_nsa_proj[l]
        y_pool = pool_mixer(pool_u, pool_w[l], pool_scale[l]) @ w_pool_proj[l]
        y_conv = short_conv_mixer(conv_h, conv_b, conv_c, conv_w[l]) @ w_conv_proj[l]
        mg = jax.nn.sigmoid(merge_g).reshape(B, T, N_BRANCHES, D)
        merged = mg[:, :, 0] * y_nsa + mg[:, :, 1] * y_pool + mg[:, :, 2] * y_conv
        h = h + merged @ w_o[l]
        h = h + hier_moe(rms_norm(h, norm2_g[l]), router_group_w[l], router_group_b[l],
                         router_expert_w[l], router_expert_b[l], expert_w1[l], expert_w3[l], expert_w2[l])
    return rms_norm(h, final_norm_g)


_drawn_inputs = setup_inputs


def setup_inputs(seed=0):
    import zlib

    import numpy as np

    out = dict(_drawn_inputs(seed))
    spreads = {}
    factors = {'pool_scale': 4.603,
     'router_group_b': 48.552,
     'router_expert_b': 28.335,
     'final_norm_g': 7.575,
     'cmp_pe': 5.253,
     'norm2_g': 3.387}
    for name, (base, spread) in spreads.items():
        noise = np.random.default_rng([zlib.crc32(name.encode()), seed]).standard_normal(out[name].shape)
        drawn = base * np.exp(spread * noise) if base else spread * noise
        out[name] = __import__('jax').numpy.asarray(drawn.astype(out[name].dtype))
    for name, factor in factors.items():
        out[name] = (out[name] * factor).astype(out[name].dtype)
    return out
```

```python
from contextlib import ExitStack

import concourse.bass as bass
from concourse import mybir

ALU = mybir.AluOpType
ACT = mybir.ActivationFunctionType
AX = mybir.AxisListType
F32 = mybir.dt.float32
I32 = mybir.dt.int32

P = 128
D = 1024
T = 256
NT = T // P
KT = D // P
HD = 64
HEADS = 8
KVG = 2
REP = HEADS // KVG
CMP_LEN, CMP_STRIDE = 32, 16
NCMP = T // CMP_STRIDE - CMP_LEN // CMP_STRIDE + 1
POOL_WINDOWS = (2, 4, 8, 16)
PW = 256
PAD = 16
CONV_K = 3
GROUPS, PER_GROUP = 4, 8
NE = GROUPS * PER_GROUP
HID = D // 4
HT = HID // P
CAP = 32
EB = P // CAP
NB = NE // EB
EPS = 1e-6
NEG = -1e30
WCOLS = 512
CHUNK = KT * WCOLS
PROJ = 2 * 2 * 2 * P
EW = KT * HID
GATES = HEADS * 3
C2W = 2 * P + GATES
GELU_C = 0.7978845608028654

CH_Q, CH_KV, CH_KVG, CH_UH, CH_BC, CH_CK, CH_CV, CH_MG = 0, 1, 2, 3, 4, 5, 6, 7
N_MG = 4
CH_M0A = CH_MG + N_MG
CH_NSA = CH_M0A + 1
CH_M0B = CH_NSA + 1
CH_WO = CH_M0B + 1
N_CHUNKS = CH_WO + 2
WSLOTS = 2

NQ1 = KT
NQ2 = 2 * HT
NQ = NQ1 + NQ2
ECHUNK = EB * 2 * HID
MAXPASS = T // CAP

PR_G1 = 0
PR_PS = PR_G1 + KT
PR_CW = PR_PS + 2
PR_PE = PR_CW + 2 * CONV_K
PR_N = PR_PE + CMP_LEN

K_ID = 0
K_DIST = K_ID + P
K_TRI = K_DIST + 3 * P
K_ONE = K_TRI + P
K_IOTA = K_ONE + P
K_CB = K_IOTA + CAP
K_CM = K_CB + NT * HEADS * 16
K_IC = K_CM + NT * 16
K_SL = K_IC + 2 * T
K_RK = K_SL + HEADS
K_N = K_RK + PER_GROUP


def build(nc, x, params, consts, front, small, wgrp, vecs, routerw, routerb, experts, out):
    with ExitStack() as ctx:
        def sb(name, shape, dt=F32):
            return ctx.enter_context(nc.sbuf_tensor(name, shape, dt))

        def sem(name):
            return ctx.enter_context(nc.semaphore(name))

        bank = [ctx.enter_context(nc.psum_tensor(f"bank{i}", [P, 512], F32)) for i in range(8)]

        h = sb("h", [P, NT, D])
        con = sb("con", [P, K_N])
        prm = sb("prm", [P, PR_N])
        wexp = sb("wexp", [P, NQ, ECHUNK])
        stat = sb("stat", [P, 64])
        wch = sb("wch", [P, WSLOTS, CHUNK + PROJ])
        xnT = sb("xnT", [P, KT, T])
        merged = sb("merged", [P, KT, T])
        qT = sb("qT", [P, REP, T])
        kT = sb("kT", [P, 2, T])
        vN = sb("vN", [P, 2, NT, P])
        gts = sb("gts", [P, NT, GATES])
        hidg = sb("hidg", [P, 4, 2 * NCMP])
        hidu = sb("hidu", [P, 4, 2 * NCMP])
        hidT = sb("hidT", [P, 4, KVG, 32])
        cw2 = sb("cw2", [P, 4, HD])
        kcT = sb("kcT", [P, 16])
        vbd = sb("vbd", [P, KVG, REP * HD])
        pcx = sb("pcx", [P, NT * HEADS, 16])
        pcs = sb("pcs", [P, 4, NT * HEADS])
        att = sb("att", [P, 6 * 3 * P])
        qcur = sb("qcur", [P, T])
        npass = sb("npass", [P, 1], I32)
        smx = sb("smx", [P, 2, NT])
        ssum = sb("ssum", [P, 4, NT])
        coef = sb("coef", [P, 4, NT])
        otmp = sb("otmp", [P, KVG * NT * HD])
        oacc = sb("oacc", [P, NT, HEADS * HD])
        ga = sb("ga", [P, 512])
        gb = sb("gb", [P, 512])
        wg = sb("wg", [P, 2, P])
        poolT = sb("poolT", [P, 2, T])
        convT = sb("convT", [P, 2, T])
        rw = sb("rw", [P, KT, GROUPS + NE])
        rb = sb("rb", [P, GROUPS + NE])

        sS = att[:, 0:6 * P].rearrange("p (b k) -> p b k", b=2)
        sP = att[:, 6 * P:12 * P].rearrange("p (b k) -> p b k", b=2)
        sPT = att[:, 12 * P:18 * P].rearrange("p (b k) -> p b k", b=2)
        PL = PAD + T
        upad = att[:, 0:2 * PL].rearrange("p (a t) -> p a t", a=2)
        s2 = att[:, 2 * PL:4 * PL].rearrange("p (a t) -> p a t", a=2)
        s4 = att[:, 4 * PL:6 * PL].rearrange("p (a t) -> p a t", a=2)
        oT = att[:, 0:4 * T].rearrange("p (k t) -> p k t", k=4)
        gfb = att[:, 1024:2048]
        oflat = oacc[:].rearrange("p t c -> p (t c)")
        zpad = oflat[:, 0:2 * (2 + T)].rearrange("p (a t) -> p a t", a=2)
        g2b = oflat
        mflat = merged[:].rearrange("p k t -> p (k t)")
        shf = mflat[:, 0:1024].rearrange("p (a g t) -> p a g t", a=2, g=KVG)
        fpe = mflat[:, 1024:1984].rearrange("p (a j c) -> p a j c", a=2, j=16)
        pooled = ga[:].rearrange("p (a t) -> p a t", a=2)
        convh = gb[:].rearrange("p (a t) -> p a t", a=2)
        pc = poolT[:].rearrange("p a t -> p (a t)").rearrange("p (a c) -> p a c", c=32)
        pcT = convT[:].rearrange("p a t -> p (a t)").rearrange("p (a q) -> p a q", q=P)
        qflat = qT[:].rearrange("p r t -> p (r t)")
        rt = qflat[:, 0:256].rearrange("p (a t e) -> p a t e", t=NT, e=PER_GROUP)
        etmp = qflat[:, 256:320].rearrange("p (t e) -> p t e", t=NT)
        comb = qflat[:, 320:384].rearrange("p (t e) -> p t e", t=NT)
        mask = qflat[:, 384:448].rearrange("p (t e) -> p t e", t=NT)
        rank = qflat[:, 448:512].rearrange("p (t e) -> p t e", t=NT)
        lg = qflat[:, 512:512 + NT * (GROUPS + NE)].rearrange("p (t e) -> p t e", t=NT)
        wflat = wch[:].rearrange("p s c -> p (s c)")
        xn2 = wflat[:, 0:NT * D].rearrange("p (t d) -> p t d", t=NT)
        xgT = wflat[:, 2048:3072].rearrange("p (k s) -> p k s", k=KT)
        yN = wflat[:, 3072:4096]
        fin = wflat[:, 6144:8192].rearrange("p (t d) -> p t d", t=NT)
        xn2T = xnT
        sel = mflat[:, 0:256].rearrange("p (t e j) -> p t e j", t=NT, e=EB)
        selw = mflat[:, 256:512].rearrange("p (t e j) -> p t e j", t=NT, e=EB)
        cmbT = mflat[:, 512:768]
        sl1 = mflat[:, 768:1024]
        hN = mflat[:, 1024:1280]
        hT = mflat[:, 1280:1536].rearrange("p (k s) -> p k s", k=HT)

        ident = con[:, K_ID:K_ID + P]
        dist = con[:, K_DIST:K_DIST + 3 * P]
        tri = con[:, K_TRI:K_TRI + P]
        ones = con[:, K_ONE:K_ONE + P]
        iota = con[:, K_IOTA:K_IOTA + CAP]
        cbias = con[:, K_CB:K_CB + NT * HEADS * 16].rearrange("p (a c) -> p a c", c=16)
        cmask = con[:, K_CM:K_CM + NT * 16].rearrange("p (t c) -> p t c", c=16)
        icnt = con[:, K_IC:K_IC + 2 * T].rearrange("p (a t) -> p a t", a=2)
        rk8 = con[:, K_RK:K_RK + PER_GROUP]

        x_in = sem("x_in")
        con_in = sem("con_in")
        small_in = sem("small_in")
        wgrp_in = sem("wgrp_in")
        route_in = sem("route_in")
        vec_in = sem("vec_in")
        chunk_in = [sem(f"chunk_in{i}") for i in range(WSLOTS)]
        expert_in = [sem(f"expert_in{i}") for i in range(NQ)]
        expert_used = sem("expert_used")
        passes_done = sem("passes_done")
        out_done = sem("out_done")

        dve_step = sem("dve_step")
        loop_step = sem("loop_step")
        moe_step = sem("moe_step")
        zeros_set = sem("zeros_set")
        ssq_done = sem("ssq_done")
        rstd_done = sem("rstd_done")
        pool_step = sem("pool_step")
        xs_done = sem("xs_done")
        xT_full = sem("xT_full")
        xnT_done = sem("xnT_done")
        q_full = sem("q_full")
        kvc_full = sem("kvc_full")
        kvs_full = sem("kvs_full")
        kvw_full = sem("kvw_full")
        gl_full = sem("gl_full")
        u_full = sem("u_full")
        h_full = sem("h_full")
        b_full = sem("b_full")
        c_full = sem("c_full")
        hid_full = sem("hid_full")
        mix_full = sem("mix_full")
        kc_full = sem("kc_full")
        sc_full = sem("sc_full")
        q_done = sem("q_done")
        kvc_done = sem("kvc_done")
        kvs_done = sem("kvs_done")
        kvw_done = sem("kvw_done")
        gl_done = sem("gl_done")
        u_done = sem("u_done")
        ch_done = sem("ch_done")
        conv_done = sem("conv_done")
        pooled_done = sem("pooled_done")
        poolT_done = sem("poolT_done")
        flat_done = sem("flat_done")
        gelu_in = sem("gelu_in")
        tanh_done = sem("tanh_done")
        hidT_done = sem("hidT_done")
        kc_done = sem("kc_done")
        csub_done = sem("csub_done")
        cexp_done = sem("cexp_done")
        pc_done = sem("pc_done")
        pcT_full = sem("pcT_full")
        pcT_done = sem("pcT_done")
        oc_full = sem("oc_full")
        s_full = sem("s_full")
        qcur_done = sem("qcur_done")
        s_max = sem("s_max")
        p_done = sem("p_done")
        pT_full = sem("pT_full")
        pT_done = sem("pT_done")
        pv_full = sem("pv_full")
        o_read = sem("o_read")
        ga_full = sem("ga_full")
        gb_full = sem("gb_full")
        yp_full = sem("yp_full")
        yc_full = sem("yc_full")
        ga_done = sem("ga_done")
        gb_done = sem("gb_done")
        merge_done = sem("merge_done")
        o_done = sem("o_done")
        oT_full = sem("oT_full")
        oT_done = sem("oT_done")
        m0_full = sem("m0_full")
        yn_full = sem("yn_full")
        m0_done = sem("m0_done")
        m0_read = sem("m0_read")
        wo_full = sem("wo_full")
        h_done = sem("h_done")
        acc_full = sem("acc_full")
        ssq2_done = sem("ssq2_done")
        rstd2_done = sem("rstd2_done")
        xn2_done = sem("xn2_done")
        xn2T_full = sem("xn2T_full")
        xn2T_done = sem("xn2T_done")
        logit_full = sem("logit_full")
        gsub_done = sem("gsub_done")
        gexp_done = sem("gexp_done")
        tsub_done = sem("tsub_done")
        texp_done = sem("texp_done")
        mask_done = sem("mask_done")
        rank_full = sem("rank_full")
        sel_done = sem("sel_done")
        cmb_full = sem("cmb_full")
        cmb_done = sem("cmb_done")
        xg_full = sem("xg_full")
        xg_done = sem("xg_done")
        hid1_full = sem("hid1_full")
        silu_done = sem("silu_done")
        y_full = sem("y_full")
        yn_done = sem("yn_done")
        ssq3_done = sem("ssq3_done")
        rstd3_done = sem("rstd3_done")
        fin_done = sem("fin_done")

        comb_done = sem("comb_done")

        add_done = sem("add_done")
        hT_full = sem("hT_full")
        hT_done = sem("hT_done")
        hn_done = sem("hn_done")
        rank_done = sem("rank_done")
        sel_step = sem("sel_step")

        def flat(ap):
            n = len(ap.shape) - 1
            names = ["a", "b", "c", "d"][:n]
            return ap.rearrange(f"p {' '.join(names)} -> p ({' '.join(names)})") if n > 1 else ap

        def chunk_tiles(n, w=WCOLS):
            return wch[:, n % WSLOTS, 0:CHUNK if w == WCOLS else KT * w].rearrange("p (k c) -> p k c", c=w)

        def have_chunk(eng, n):
            eng.wait_ge(chunk_in[n % WSLOTS], 16 * (n // WSLOTS + 1))

        block = ctx.enter_context(nc.Block())

        @block.sync
        def _(sp):
            for t in range(NT):
                sp.dma_start(h[:, t], x[t * P:(t + 1) * P]).then_inc(x_in, 16)
            sp.dma_start(con[:], consts).then_inc(con_in, 16)
            last_product = {CH_Q: (q_full, 2), CH_KV: (kvs_full, 1), CH_KVG: (gl_full, 1), CH_UH: (h_full, 1),
                            CH_BC: (c_full, 1), CH_CK: (hid_full, 1), CH_CV: (hid_full, 2), CH_M0A: (m0_full, 2),
                            CH_NSA: (yn_full, 4), CH_M0B: (m0_full, 4)}
            for i in range(N_MG):
                last_product[CH_MG + i] = (yc_full, i + 1)
            piece = 0
            for n in range(N_CHUNKS):
                if n >= WSLOTS:
                    sp.wait_ge(*last_product[n - WSLOTS])
                w = KT * C2W if n == CH_KVG else CHUNK + PROJ if CH_MG <= n < CH_MG + N_MG else CHUNK
                sp.dma_start(wch[:, n % WSLOTS, 0:w], front[n, :, 0:w]).then_inc(chunk_in[n % WSLOTS], 16)
                while piece < NQ and (piece < n - 1 or n == N_CHUNKS - 1):
                    sp.dma_start(wexp[:, piece], experts[0, piece]).then_inc(expert_in[piece], 16)
                    piece += 1
            sp.wait_ge(passes_done, 1)
            passes = sp.value_load(npass[0:1, 0:1], min_val=1, max_val=MAXPASS)
            with sp.Fori(1, passes * NB) as b:
                for q in range(NQ):
                    sp.wait_ge(expert_used, b * NQ + (q + 1 - NQ))
                    sp.dma_start(wexp[:, q], experts[bass.ds(b % NB, 1), q].rearrange("o p c -> (o p) c")).then_inc(expert_in[q], 16)
            for t in range(NT):
                sp.wait_ge(fin_done, t + 1)
                sp.dma_start(out[t * P:(t + 1) * P], fin[:, t]).then_inc(out_done, 16)
            sp.wait_ge(out_done, 16 * NT)

        @block.gpsimd
        def _(pool):
            nc.gpsimd.memset(upad[:, :, 0:PAD], 0.0).then_inc(zeros_set, 1)
            nc.gpsimd.memset(s2[:, :, 0:PAD], 0.0).then_inc(zeros_set, 1)
            nc.gpsimd.memset(s4[:, :, 0:PAD], 0.0).then_inc(zeros_set, 1)
            nc.gpsimd.memset(zpad[:, :, 0:2], 0.0).then_inc(zeros_set, 1)
            nc.gpsimd.memset(hidT[:], 0.0).then_inc(zeros_set, 1)
            nc.gpsimd.memset(vbd[:], 0.0).then_inc(zeros_set, 1)
            nc.gpsimd.memset(stat[:, 32:34], -0.5).then_inc(zeros_set, 1)
            pool.wait_ge(zeros_set, 7)

            def rstd(col, n):
                nc.gpsimd.tensor_scalar(stat[:, col:col + 2], stat[:, col:col + 2], 1.0 / D, EPS,
                                        ALU.mult, ALU.add).then_inc(pool_step, 1)
                pool.wait_ge(pool_step, n)
                return nc.gpsimd.tensor_tensor(stat[:, col + 2:col + 4], stat[:, col:col + 2], stat[:, 32:34], ALU.pow)

            pool.wait_ge(ssq_done, NT)
            rstd(0, 1).then_inc(rstd_done, 1)
            pool.wait_ge(ssq2_done, NT)
            rstd(4, 2).then_inc(rstd2_done, 1)
            pool.wait_ge(ssq3_done, NT)
            rstd(8, 3).then_inc(rstd3_done, 1)

        @block.scalar
        def _(act):
            for s1 in (p_done, ga_done, gb_done, hT_done, yn_done):
                act.sem_inc(s1, 1)
            act.dma_start(prm[:], params).then_inc(small_in, 16)
            act.dma_start(flat(cw2[:]), small).then_inc(small_in, 16)
            act.dma_start(flat(wg[:]), wgrp).then_inc(small_in, 16)
            act.dma_start(flat(rw[:]), routerw).then_inc(route_in, 16)
            act.dma_start(rb[:], routerb.to_broadcast([P, GROUPS + NE])).then_inc(route_in, 16)
            for t in range(NT):
                act.wait_ge(x_in, 16 * NT)
                nc.scalar.activation(flat(xnT[:, 4 * t:4 * t + 4]), h[:, t], ACT.Square,
                                     accum_out=stat[:, t:t + 1]).then_inc(ssq_done, 1)
            act.wait_ge(small_in, 48)
            for k in (0, 1, 4, 5):
                act.wait_ge(xT_full, k // 2 + 1)
                nc.scalar.activation(xnT[:, k], bank[k // 2][:, (k % 2) * T:(k % 2 + 1) * T], ACT.Copy,
                                     scale=prm[:, PR_G1 + k:PR_G1 + k + 1]).then_inc(xnT_done, 1)
            for n in range(2):
                act.wait_ge(q_full, n + 1)
                nc.scalar.mul(flat(qT[:, 2 * n:2 * n + 2]), bank[4 + n][:], HD ** -0.5).then_inc(q_done, 1)
            act.wait_ge(kvs_full, 1)
            nc.scalar.copy(kT[:, 0], bank[1][:, 0:T])
            nc.scalar.copy(flat(vN[:, 0]), bank[1][:, T:2 * T]).then_inc(kvs_done, 1)
            act.wait_ge(kvw_full, 1)
            nc.scalar.copy(kT[:, 1], bank[2][:, 0:T])
            nc.scalar.copy(flat(vN[:, 1]), bank[2][:, T:2 * T]).then_inc(kvw_done, 1)
            act.wait_ge(gl_full, 1)
            nc.scalar.activation(flat(gts[:]), bank[3][:, 0:NT * GATES], ACT.Tanh, scale=0.5).then_inc(gl_done, 1)
            act.wait_ge(h_full, 1)
            nc.scalar.copy(flat(convh), bank[1][:]).then_inc(ch_done, 1)
            act.wait_ge(gelu_in, 1)
            nc.scalar.activation(hidg[:], hidu[:], ACT.Tanh, scale=GELU_C).then_inc(tanh_done, 1)

            with act.Fori(0, N_MG // 2) as i2:
                for s in range(2):
                    i = i2 * 2 + s
                    act.wait_ge(s_full, i * 4 + 1)
                    act.wait_ge(q_done, 2)
                    nc.scalar.copy(qcur[:], qT[:, bass.ds(i, 1)].rearrange("p r t -> p (r t)")).then_inc(qcur_done, 1)
                    for u in range(4):
                        if u == 2:
                            act.wait_ge(ga_full, i + 1)
                            act.wait_ge(merge_done, i + 1)
                            nc.scalar.activation(ga[:], bank[0][:], ACT.Tanh, scale=0.5).then_inc(ga_done, 1)
                        act.wait_ge(s_max, i * 4 + (u + 1) + 1)
                        act.wait_ge(pT_full, i * 4 + max(u - 1, 0) + 1)
                        act.wait_ge(o_read, i + 1)
                        nc.scalar.activation(sP[:, u % 2, 0:P], sS[:, u % 2, 0:P], ACT.Exp,
                                             bias=smx[:, u % 2, 0:1], accum_out=ssum[:, u, 0:1])
                        nc.scalar.activation(sP[:, u % 2, P:3 * P], sS[:, u % 2, P:3 * P], ACT.Exp,
                                             bias=smx[:, u % 2, 1:2], accum_out=ssum[:, u, 1:2]).then_inc(p_done, 1)
                    act.wait_ge(gb_full, i + 1)
                    nc.scalar.activation(gb[:], bank[1][:], ACT.Tanh, scale=0.5).then_inc(gb_done, 1)

            act.wait_ge(csub_done, 1)
            nc.scalar.activation(pcx[:], pcx[:], ACT.Exp).then_inc(cexp_done, 1)
            for n in range(2):
                act.wait_ge(m0_full, n + 1)
                act.wait_ge(merge_done, N_MG + 1)
                nc.scalar.activation((ga, gb)[n][:], bank[2 + n][:], ACT.Tanh, scale=0.5).then_inc(m0_done, 1)
            act.wait_ge(pcT_full, 1)
            nc.scalar.copy(flat(pcT), bank[6][:]).then_inc(pcT_done, 1)
            for n in range(2):
                act.wait_ge(oT_full, n + 1)
                nc.scalar.mul(flat(oT[:, 2 * n:2 * n + 2]), bank[n][:], 0.5).then_inc(oT_done, 1)
            act.dma_start(g2b, vecs[0:1].to_broadcast([P, D])).then_inc(vec_in, 16)
            act.dma_start(gfb, vecs[1:2].to_broadcast([P, D])).then_inc(vec_in, 16)
            for n in range(2, 4):
                act.wait_ge(m0_full, n + 1)
                act.wait_ge(m0_read, n - 1)
                nc.scalar.activation((ga, gb)[n % 2][:], bank[2 + n % 2][:], ACT.Tanh, scale=0.5).then_inc(m0_done, 1)

            for t in range(NT):
                act.wait_ge(h_done, 4)
                nc.scalar.activation(flat(xnT[:, 4 * t:4 * t + 4]), h[:, t], ACT.Square,
                                     accum_out=stat[:, 4 + t:5 + t]).then_inc(ssq2_done, 1)
            for n in (0, 2):
                act.wait_ge(xn2T_full, n + 1)
                nc.scalar.copy(flat(xn2T[:, 2 * n:2 * n + 2]), bank[4 + n][:]).then_inc(xn2T_done, 1)
            act.wait_ge(gsub_done, 1)
            nc.scalar.activation(rt[:, 1, :, 0:GROUPS], rt[:, 0, :, 0:GROUPS], ACT.Exp).then_inc(gexp_done, 1)
            act.wait_ge(tsub_done, 1)
            nc.scalar.activation(rt[:, 9, :, 0:1], rt[:, 8, :, 0:1], ACT.Exp).then_inc(texp_done, 1)

            act.wait_ge(passes_done, 1)
            passes = act.value_load(npass[0:1, 0:1], min_val=1, max_val=MAXPASS)
            with act.Fori(0, passes * NB) as b:
                act.wait_ge(xg_full, b * 2 + 2)
                nc.scalar.copy(flat(xgT[:, 0:4]), bank[2][:]).then_inc(xg_done, 1)
                act.wait_ge(hid1_full, b + 1)
                nc.scalar.activation(sl1, bank[0][:, 0:HID], ACT.Silu).then_inc(silu_done, 1)
                act.wait_ge(hT_full, b + 1)
                nc.scalar.copy(flat(hT), bank[1][:, 0:HT * P]).then_inc(hT_done, 1)
                for half in range(2):
                    act.wait_ge(y_full, b * 2 + (half + 1))
                    nc.scalar.copy(yN[:, half * 512:(half + 1) * 512], bank[4 + half][:]).then_inc(yn_done, 1)
            for t in range(NT):
                act.wait_ge(add_done, passes * (4 * NB) + t)
                nc.scalar.activation(flat(xnT[:, 4 * t:4 * t + 4]), h[:, t], ACT.Square,
                                     accum_out=stat[:, 8 + t:9 + t]).then_inc(ssq3_done, 1)

        @block.vector
        def _(dve):
            for s1 in (s_max, o_read, merge_done, pT_done, hn_done, add_done):
                dve.sem_inc(s1, 1)
            counted = [0]

            def step(ins):
                counted[0] += 1
                ins.then_inc(dve_step, 1)
                dve.wait_ge(dve_step, counted[0])

            dve.wait_ge(rstd_done, 1)
            for t in range(NT):
                dve.wait_ge(x_in, 16 * NT)
                nc.vector.tensor_scalar(flat(merged[:, 4 * t:4 * t + 4]), h[:, t], stat[:, 2 + t:3 + t], None,
                                        ALU.mult).then_inc(xs_done, 1)
            dve.wait_ge(small_in, 48)
            for k in (2, 3, 6, 7):
                dve.wait_ge(xT_full, k // 2 + 1)
                nc.vector.tensor_scalar(xnT[:, k], bank[k // 2][:, (k % 2) * T:(k % 2 + 1) * T], prm[:, PR_G1 + k:PR_G1 + k + 1], None,
                                        ALU.mult).then_inc(xnT_done, 1)
            dve.wait_ge(kvc_full, 1)
            raw = bank[0][:].rearrange("p (a t) -> p a t", a=2)
            for g in range(KVG):
                nc.vector.tensor_copy(shf[0:HD, :, g, :], raw[g * HD:(g + 1) * HD])
                ins = nc.vector.tensor_copy(shf[HD:P, :, g, 0:T - 1], raw[g * HD:(g + 1) * HD, :, 1:T])
            ins.then_inc(kvc_done, 1)
            dve.wait_ge(kvc_done, 1)
            for a in range(2):
                for g in range(KVG):
                    src = shf[:, a, g, 0:CMP_STRIDE * (NCMP + 1)].rearrange("p (c j z) -> p j c z", j=CMP_STRIDE // 2, z=2)
                    for hi in range(2):
                        ins = nc.vector.tensor_tensor(
                            fpe[:, a, 8 * hi:8 * hi + 8, g * NCMP:(g + 1) * NCMP],
                            src[:, :, hi:hi + NCMP, 0],
                            prm[:, PR_PE + 16 * a + 8 * hi:PR_PE + 16 * a + 8 * hi + 8].unsqueeze(2).to_broadcast([P, 8, NCMP]),
                            ALU.add)
            ins.then_inc(flat_done, 1)
            dve.wait_ge(gl_done, 1)
            step(nc.vector.tensor_scalar(gts[:], gts[:], 1.0, 0.5, ALU.add, ALU.mult))
            dve.wait_ge(u_full, 1)
            dve.wait_ge(zeros_set, 7)
            nc.vector.tensor_copy(upad[:, :, PAD:], bank[0][:].rearrange("p (a t) -> p a t", a=2)).then_inc(u_done, 1)
            dve.wait_ge(u_done, 1)
            step(nc.vector.tensor_tensor(s2[:, :, PAD:], upad[:, :, PAD:], upad[:, :, PAD - 1:-1], ALU.add))
            step(nc.vector.tensor_tensor(s4[:, :, PAD:], s2[:, :, PAD:], s2[:, :, PAD - 2:-2], ALU.add))
            nc.vector.tensor_tensor(pooled[0:HD, 0], s2[0:HD, 0, PAD:], icnt[0:HD, 0], ALU.mult)
            step(nc.vector.tensor_tensor(pooled[HD:P, 0], s4[HD:P, 0, PAD:], icnt[HD:P, 0], ALU.mult))
            step(nc.vector.tensor_tensor(s2[:, 1, PAD:], s4[:, 1, PAD:], s4[:, 1, PAD - 4:-4], ALU.add))
            nc.vector.tensor_tensor(pooled[0:HD, 1], s2[0:HD, 1, PAD:], icnt[0:HD, 1], ALU.mult)
            step(nc.vector.tensor_tensor(s4[HD:P, 1, PAD:], s2[HD:P, 1, PAD:], s2[HD:P, 1, PAD - 8:-8], ALU.add))
            step(nc.vector.tensor_tensor(pooled[HD:P, 1], s4[HD:P, 1, PAD:], icnt[HD:P, 1], ALU.mult))
            nc.vector.tensor_tensor(pooled, pooled, upad[:, :, PAD:], ALU.subtract).then_inc(pooled_done, 1)
            dve.wait_ge(ch_done, 1)
            dve.wait_ge(c_full, 1)
            step(nc.vector.tensor_tensor(zpad[:, :, 2:], bank[3][:].rearrange("p (a t) -> p a t", a=2), convh, ALU.mult))
            for tap in range(CONV_K):
                for a in range(2):
                    w = prm[:, PR_CW + 2 * tap + a:PR_CW + 2 * tap + a + 1]
                    z = zpad[:, a, tap:tap + T]
                    if tap == 0:
                        ins = nc.vector.tensor_scalar(convT[:, a], z, w, None, ALU.mult)
                    else:
                        ins = nc.vector.scalar_tensor_tensor(convT[:, a], z, w, convT[:, a], ALU.mult, ALU.add)
                step(ins)
            nc.vector.scalar_tensor_tensor(flat(convT[:]), flat(convT[:]), 0.5, bank[2][:], ALU.mult, ALU.mult).then_inc(conv_done, 1)
            dve.wait_ge(mix_full, 1)
            for a in range(2):
                ins = nc.vector.tensor_scalar(poolT[:, a], bank[5][:, a * T:(a + 1) * T],
                                              prm[:, PR_PS + a:PR_PS + a + 1], 0.5, ALU.mult, ALU.mult)
            ins.then_inc(poolT_done, 1)
            hx = bank[4][:, 0:4 * 32].rearrange("p (a c) -> p a c", c=32)[:, :, 0:2 * NCMP]
            dve.wait_ge(hid_full, 2)
            step(nc.vector.tensor_copy(hidg[:], hx))
            step(nc.vector.tensor_tensor(hidu[:], hidg[:], hidg[:], ALU.mult))
            step(nc.vector.tensor_scalar(hidu[:], hidu[:], 0.044715, 1.0, ALU.mult, ALU.add))
            nc.vector.tensor_tensor(hidu[:], hidu[:], hidg[:], ALU.mult).then_inc(gelu_in, 1)
            dve.wait_ge(tanh_done, 1)
            for g in range(KVG):
                c = slice(g * NCMP, (g + 1) * NCMP)
                ins = nc.vector.scalar_tensor_tensor(hidT[:, :, g, 0:NCMP], hidg[:, :, c], 1.0, hx[:, :, c], ALU.add, ALU.mult)
            ins.then_inc(hidT_done, 1)

            LS = 9
            with dve.Fori(0, N_MG // 2) as i2:
                k = [0]

                def lstep(ins):
                    k[0] += 1
                    ins.then_inc(loop_step, 1)
                    dve.wait_ge(loop_step, i2 * (2 * LS) + k[0])

                for s in range(2):
                    i = i2 * 2 + s

                    def scores(u):
                        g = u % 2
                        dve.wait_ge(s_full, i * 4 + (u + 1) + 1)
                        dve.wait_ge(p_done, i * 4 + max(u - 1, 0) + 1)
                        lstep(nc.vector.scalar_tensor_tensor(sS[:, u % 2], dist, con[:, bass.ds(i + (K_SL + g * REP), 1)],
                                                             bank[4 + u % 2][:, 0:3 * P], ALU.mult, ALU.add))
                        nc.vector.tensor_reduce(smx[:, u % 2, 0:1], sS[:, u % 2, 0:P], AX.X, ALU.max, negate=True)
                        nc.vector.tensor_reduce(smx[:, u % 2, 1:2], sS[:, u % 2, P:3 * P], AX.X, ALU.max,
                                                negate=True).then_inc(s_max, 1)

                    def take_pT(u):
                        dve.wait_ge(pT_full, i * 4 + (u + 1) + 1)
                        dve.wait_ge(pv_full, i * 4 + max(u - 1, 0) + 1)
                        nc.vector.tensor_copy(sPT[:, u % 2], bank[6][:, 0:3 * P]).then_inc(pT_done, 1)

                    scores(0)
                    scores(1)
                    take_pT(0)
                    scores(2)
                    take_pT(1)
                    scores(3)
                    take_pT(2)
                    take_pT(3)
                    dve.wait_ge(ga_done, i + 2)
                    dve.wait_ge(yp_full, i + 1)
                    nc.vector.scalar_tensor_tensor(ga[:], ga[:], 1.0, bank[2][:], ALU.add, ALU.mult)
                    dve.wait_ge(gb_done, i + 2)
                    dve.wait_ge(yc_full, i + 1)
                    lstep(nc.vector.scalar_tensor_tensor(gb[:], gb[:], 1.0, bank[3][:], ALU.add, ALU.mult))
                    nc.vector.tensor_tensor(merged[:, bass.ds(i * 2, 2)].rearrange("p k t -> p (k t)"), ga[:], gb[:],
                                            ALU.add).then_inc(merge_done, 1)
                    dve.wait_ge(pv_full, i * 4 + 4 + 1)
                    dve.wait_ge(p_done, i * 4 + 4 + 1)
                    lstep(nc.vector.reciprocal(coef[:], ssum[:]))
                    gv = gts[:].rearrange("p t (g r c) -> p g r c t", g=KVG, r=REP)
                    for b in range(2):
                        ins = nc.vector.tensor_tensor(coef[:, 2 * b:2 * b + 2], coef[:, 2 * b:2 * b + 2],
                                                      gv[:, :, bass.ds(i, 1), 1 + b, :].rearrange("p g r t -> p g (r t)"), ALU.mult)
                    lstep(ins)
                    ov = oacc[:].rearrange("p t (g r d) -> p g t r d", g=KVG, r=REP)[:, :, :, bass.ds(i, 1), :].rearrange("p g t r d -> p g t (r d)")
                    pv = bank[7][:].rearrange("p (u t d) -> p u t d", u=4, t=NT)
                    tv = otmp[:].rearrange("p (g t d) -> p g t d", g=KVG, t=NT)
                    lstep(nc.vector.tensor_tensor(ov, pv[:, 0:2], coef[:, 0:2].unsqueeze(3).to_broadcast([P, KVG, NT, HD]), ALU.mult))
                    lstep(nc.vector.tensor_tensor(tv, pv[:, 2:4], coef[:, 2:4].unsqueeze(3).to_broadcast([P, KVG, NT, HD]), ALU.mult))
                    nc.vector.tensor_tensor(ov, ov, tv, ALU.add).then_inc(o_read, 1)
                    assert k[0] == LS * (s + 1)

            dve.wait_ge(kc_full, 1)
            nc.vector.tensor_scalar(kcT[:], bank[4][:, 0:16], 0.5, None, ALU.mult)
            for r in range(REP):
                ins = nc.vector.tensor_scalar(vbd[32 * r:32 * r + 32, :, r * HD:(r + 1) * HD],
                                              bank[4][32 * r:32 * r + 32, 64:64 + KVG * HD].rearrange("p (g d) -> p g d", g=KVG),
                                              0.5, None, ALU.mult)
            ins.then_inc(kc_done, 1)
            dve.wait_ge(merge_done, N_MG + 1)
            dve.wait_ge(yp_full, N_MG)
            step(nc.vector.memset(pc, 0.0))
            dve.wait_ge(sc_full, 1)
            for g in range(KVG):
                def heads(ap):
                    return ap.rearrange("p (t g r) c -> p t g (r c)", t=NT, g=KVG)[:, :, g]
                ins = nc.vector.tensor_tensor(heads(pcx[:]), bank[(5, 7)[g]][:, 0:NT * REP * 16].rearrange("p (t a) -> p t a", t=NT),
                                              heads(cbias), ALU.add)
            step(ins)
            step(nc.vector.tensor_reduce(pcs[:, 0], pcx[:], AX.X, ALU.max))
            nc.vector.tensor_tensor(pcx[:], pcx[:], pcs[:, 0].unsqueeze(2).to_broadcast([P, NT * HEADS, 16]),
                                    ALU.subtract).then_inc(csub_done, 1)
            dve.wait_ge(cexp_done, 1)
            step(nc.vector.tensor_reduce(pcs[:, 1], pcx[:], AX.X, ALU.add))
            step(nc.vector.reciprocal(pcs[:, 2], pcs[:, 1]))
            step(nc.vector.tensor_tensor(pcs[:, 3].rearrange("p (t a) -> p t a", t=NT), pcs[:, 2].rearrange("p (t a) -> p t a", t=NT),
                                         gts[:].rearrange("p t (a c) -> p t a c", c=3)[:, :, :, 0], ALU.mult))
            step(nc.vector.tensor_tensor(pcx[:], pcx[:], pcs[:, 3].unsqueeze(2).to_broadcast([P, NT * HEADS, 16]), ALU.mult))
            for t in range(NT):
                a = slice(t * HEADS, (t + 1) * HEADS)
                ins = nc.vector.tensor_tensor(pc[:, a, 0:16], pcx[:, a], cmask[:, t].unsqueeze(1).to_broadcast([P, HEADS, 16]), ALU.mult)
            ins.then_inc(pc_done, 1)
            dve.wait_ge(oc_full, 1)
            dve.wait_ge(o_read, N_MG + 1)
            nc.vector.tensor_tensor(oacc[:, 0], oacc[:, 0], bank[7][:], ALU.add).then_inc(o_done, 1)
            nc.vector.tensor_tensor(oacc[:, 1], oacc[:, 1], bank[4][:], ALU.add).then_inc(o_done, 1)
            for n in range(4):
                g_ = (ga, gb)[n % 2]
                dve.wait_ge(m0_done, n + 1)
                dve.wait_ge(yn_full, n + 1)
                step(nc.vector.scalar_tensor_tensor(g_[:], g_[:], 1.0, bank[5 + n % 2][:], ALU.add, ALU.mult))
                m = flat(merged[:, 2 * n:2 * n + 2])
                nc.vector.tensor_tensor(m, m, g_[:], ALU.add).then_inc(m0_read, 1)
            for n in range(4):
                t, half = n % 2, n // 2
                dve.wait_ge(wo_full, n + 1)
                hv = h[:, t, half * 512:(half + 1) * 512]
                nc.vector.tensor_tensor(hv, hv, bank[(7, 4, 0, 1)[n]][:], ALU.add).then_inc(h_done, 1)

            dve.wait_ge(rstd2_done, 1)
            dve.wait_ge(vec_in, 32)
            for t in range(NT):
                dve.wait_ge(h_done, 4)
                nc.vector.scalar_tensor_tensor(xn2[:, t], h[:, t], stat[:, 6 + t:7 + t], g2b, ALU.mult, ALU.mult).then_inc(xn2_done, 1)
            for n in (1, 3):
                dve.wait_ge(xn2T_full, n + 1)
                nc.vector.tensor_copy(flat(xn2T[:, 2 * n:2 * n + 2]), bank[4 + n][:]).then_inc(xn2T_done, 1)
            dve.wait_ge(logit_full, 1)
            dve.wait_ge(route_in, 32)
            step(nc.vector.tensor_tensor(lg, bank[4][:, 0:NT * (GROUPS + NE)].rearrange("p (t e) -> p t e", t=NT),
                                         rb[:].unsqueeze(1).to_broadcast([P, NT, GROUPS + NE]), ALU.add))
            G = lg[:, :, 0:GROUPS]
            E4 = lg[:, :, GROUPS:].rearrange("p t (g e) -> p t g e", g=GROUPS)

            def one(row, c=0):
                return rt[:, row, :, c:c + 1]

            def wide(ap, n):
                return ap.to_broadcast([P, NT, n])

            step(nc.vector.tensor_reduce(one(2), G, AX.X, ALU.max))
            nc.vector.tensor_tensor(rt[:, 0, :, 0:GROUPS], G, wide(one(2), GROUPS), ALU.subtract).then_inc(gsub_done, 1)

            def first_largest(out_row, vals, top, n, scratch):
                v = rt[:, scratch, :, 0:n]
                step(nc.vector.tensor_tensor(v, vals, wide(top, n), ALU.is_equal))
                step(nc.vector.tensor_tensor(v, v, rk8[:, 0:n].unsqueeze(1).to_broadcast([P, NT, n]), ALU.mult))
                step(nc.vector.tensor_reduce(one(scratch + 1), v, AX.X, ALU.max))
                step(nc.vector.tensor_tensor(rt[:, out_row, :, 0:n], v, wide(one(scratch + 1), n), ALU.is_equal))

            first_largest(3, G, one(2), GROUPS, 4)
            et = etmp.rearrange("p t (g e) -> p t g e", g=GROUPS)
            for t in range(NT):
                ins = nc.vector.tensor_tensor(et[:, t], E4[:, t], rt[:, 3, t, 0:GROUPS].unsqueeze(2).to_broadcast([P, GROUPS, PER_GROUP]), ALU.mult)
            step(ins)
            step(nc.vector.tensor_reduce(rt[:, 6], etmp.rearrange("p t (g e) -> p t e g", g=GROUPS), AX.X, ALU.add))
            step(nc.vector.tensor_reduce(one(7), rt[:, 6], AX.X, ALU.max))
            first_largest(10, rt[:, 6], one(7), PER_GROUP, 4)
            step(nc.vector.scalar_tensor_tensor(rt[:, 11], rt[:, 10], NEG, rt[:, 6], ALU.mult, ALU.add))
            step(nc.vector.tensor_reduce(one(12), rt[:, 11], AX.X, ALU.max))
            first_largest(13, rt[:, 11], one(12), PER_GROUP, 4)
            nc.vector.tensor_tensor(one(8), one(12), one(7), ALU.subtract).then_inc(tsub_done, 1)
            step(nc.vector.tensor_tensor(rt[:, 14], rt[:, 10], rt[:, 13], ALU.add))
            for t in range(NT):
                ins = nc.vector.tensor_tensor(mask[:, t].rearrange("p (g e) -> p g e", g=GROUPS),
                                              rt[:, 3, t, 0:GROUPS].unsqueeze(2).to_broadcast([P, GROUPS, PER_GROUP]),
                                              rt[:, 14, t].unsqueeze(1).to_broadcast([P, GROUPS, PER_GROUP]), ALU.mult)
            ins.then_inc(mask_done, 1)
            dve.wait_ge(gexp_done, 1)
            step(nc.vector.tensor_reduce(one(4), rt[:, 1, :, 0:GROUPS], AX.X, ALU.add))
            dve.wait_ge(texp_done, 1)
            step(nc.vector.tensor_scalar(one(5), one(9), 1.0, None, ALU.add))
            step(nc.vector.tensor_tensor(one(4), one(4), one(5), ALU.mult))
            step(nc.vector.reciprocal(one(5), one(4)))
            step(nc.vector.tensor_tensor(one(9), one(9), one(5), ALU.mult))
            nc.vector.tensor_tensor(rt[:, 10], rt[:, 10], wide(one(5), PER_GROUP), ALU.mult)
            step(nc.vector.tensor_tensor(rt[:, 13], rt[:, 13], wide(one(9), PER_GROUP), ALU.mult))
            step(nc.vector.tensor_tensor(rt[:, 10], rt[:, 10], rt[:, 13], ALU.add))
            for t in range(NT):
                ins = nc.vector.tensor_tensor(comb[:, t].rearrange("p (g e) -> p g e", g=GROUPS),
                                              rt[:, 3, t, 0:GROUPS].unsqueeze(2).to_broadcast([P, GROUPS, PER_GROUP]),
                                              rt[:, 10, t].unsqueeze(1).to_broadcast([P, GROUPS, PER_GROUP]), ALU.mult)
            step(ins)
            dve.wait_ge(rank_full, 1)
            step(nc.vector.scalar_tensor_tensor(rank, bank[5][:, 0:NT * NE].rearrange("p (t e) -> p t e", t=NT), 1.0, mask, ALU.add, ALU.mult))

            step(nc.vector.tensor_reduce(rt[:, 4, 0, 0:1], bank[5][:, 2 * NE:3 * NE], AX.X, ALU.max))
            step(nc.vector.tensor_scalar(rt[:, 5, 0], rk8, 1.0, float(CAP), ALU.subtract, ALU.mult))
            step(nc.vector.tensor_scalar(rt[:, 5, 1], rt[:, 5, 0], rt[:, 4, 0, 0:1], None, ALU.is_lt))
            step(nc.vector.tensor_reduce(rt[:, 4, 0, 1:2], rt[:, 5, 1], AX.X, ALU.add))
            nc.vector.tensor_copy(npass[:], rt[:, 4, 0, 1:2]).then_inc(passes_done, 1)
            dve.wait_ge(passes_done, 1)
            passes = dve.value_load(npass[0:1, 0:1], min_val=1, max_val=MAXPASS)
            with dve.Fori(0, passes) as rnd:
                with dve.Fori(0, NB) as bb:
                    b = rnd * NB + bb
                    dve.wait_ge(xg_full, b * 2 + 1)
                    for t in range(NT):
                        ins = nc.vector.tensor_tensor(sel[:, t], iota.unsqueeze(1).to_broadcast([P, EB, CAP]),
                                                      rank[:, t, bass.ds(bb * EB, EB)].unsqueeze(2).to_broadcast([P, EB, CAP]),
                                                      ALU.is_equal)
                    ins.then_inc(sel_step, 1)
                    dve.wait_ge(sel_step, b + 1)
                    for t in range(NT):
                        ins = nc.vector.tensor_tensor(selw[:, t], sel[:, t],
                                                      comb[:, t, bass.ds(bb * EB, EB)].unsqueeze(2).to_broadcast([P, EB, CAP]),
                                                      ALU.mult)
                    ins.then_inc(sel_done, 1)
                    dve.wait_ge(cmb_full, b + 1)
                    nc.vector.tensor_copy(cmbT, bank[1][:, 0:T]).then_inc(cmb_done, 1)
                    dve.wait_ge(xg_full, b * 2 + 2 + 1)
                    nc.vector.tensor_copy(flat(xgT[:, 4:8]), bank[3][:]).then_inc(xg_done, 1)
                    dve.wait_ge(silu_done, b + 1)
                    nc.vector.tensor_tensor(hN, sl1, bank[0][:, HID:2 * HID], ALU.mult).then_inc(hn_done, 1)
                    for half in range(2):
                        for t in range(NT):
                            dve.wait_ge(comb_done, b * 4 + (2 * half + t + 1))
                            hv = h[:, t, half * 512:(half + 1) * 512]
                            nc.vector.tensor_tensor(hv, hv, bank[6 + t][:], ALU.add).then_inc(add_done, 1)
                nc.vector.tensor_scalar(rank, rank, float(CAP), None, ALU.subtract).then_inc(rank_done, 1)
                dve.wait_ge(rank_done, rnd + 1)
            dve.wait_ge(rstd3_done, 1)
            for t in range(NT):
                nc.vector.scalar_tensor_tensor(fin[:, t], h[:, t], stat[:, 10 + t:11 + t], gfb,
                                               ALU.mult, ALU.mult).then_inc(fin_done, 1)

        @block.tensor
        def _(pe):
            mm = nc.tensor.matmul
            for s1 in (s_full, pT_full, pv_full, xg_full):
                pe.sem_inc(s1, 1)

            pe.wait_ge(con_in, 16)
            pe.wait_ge(xs_done, NT)
            for k in range(KT):
                for t in range(NT):
                    src = flat(merged[:, 4 * t:4 * t + 4])[:, k * P:(k + 1) * P]
                    ins = nc.tensor.transpose(bank[k // 2][:, (k % 2) * T + t * P:(k % 2) * T + (t + 1) * P], src, ident)
                if k % 2:
                    ins.then_inc(xT_full, 1)
            pe.wait_ge(xnT_done, KT)

            def channels(dst, w, c0, rhs=xnT, kt=KT):
                for k in range(kt):
                    ins = mm(dst, w[:, k, c0:c0 + P], rhs[:, k], start=(k == 0), stop=(k == kt - 1))
                return ins

            def tokens(dst, w, c0, n, t):
                for k in range(KT):
                    ins = mm(dst, xnT[:, k, t * P:(t + 1) * P], w[:, k, c0:c0 + n], start=(k == 0), stop=(k == KT - 1))
                return ins

            have_chunk(pe, CH_Q)
            w = chunk_tiles(CH_Q)
            for n in range(4):
                ins = channels(bank[4 + n // 2][:, (n % 2) * T:(n % 2 + 1) * T], w, n * P)
                if n % 2:
                    ins.then_inc(q_full, 1)
            pe.wait_ge(q_full, 2)
            have_chunk(pe, CH_KV)
            w = chunk_tiles(CH_KV)
            for a in range(2):
                ins = channels(bank[0][:, a * T:(a + 1) * T], w, a * P)
            ins.then_inc(kvc_full, 1)
            channels(bank[1][:, 0:T], w, 2 * P)
            for t in range(NT):
                ins = tokens(bank[1][:, T + t * P:T + (t + 1) * P], w, 3 * P, P, t)
            ins.then_inc(kvs_full, 1)
            have_chunk(pe, CH_KVG)
            w = chunk_tiles(CH_KVG, C2W)
            channels(bank[2][:, 0:T], w, 0)
            for t in range(NT):
                ins = tokens(bank[2][:, T + t * P:T + (t + 1) * P], w, P, P, t)
            ins.then_inc(kvw_full, 1)
            for t in range(NT):
                ins = tokens(bank[3][:, t * GATES:(t + 1) * GATES], w, 2 * P, GATES, t)
            ins.then_inc(gl_full, 1)

            def pair(dst, w, c0, full):
                for a in range(2):
                    ins = channels(dst[:, a * T:(a + 1) * T], w, c0 + a * P)
                ins.then_inc(full, 1)

            have_chunk(pe, CH_UH)
            w = chunk_tiles(CH_UH)
            pe.wait_ge(kvc_done, 1)
            pair(bank[0], w, 0, u_full)
            pe.wait_ge(kvs_done, 1)
            pair(bank[1], w, 2 * P, h_full)
            have_chunk(pe, CH_BC)
            w = chunk_tiles(CH_BC)
            pe.wait_ge(kvw_done, 1)
            pair(bank[2], w, 0, b_full)
            pe.wait_ge(gl_done, 1)
            pair(bank[3], w, 2 * P, c_full)
            pe.wait_ge(flat_done, 1)
            pe.wait_ge(q_done, 2)
            for a in range(2):
                have_chunk(pe, CH_CK + a)
                w = wch[:, (CH_CK + a) % WSLOTS, 0:CHUNK].rearrange("p (j c) -> p j c", j=16)
                for ht in range(2):
                    c = 32 * (2 * a + ht)
                    for j in range(16):
                        ins = mm(bank[4][:, c:c + 2 * NCMP], w[:, j, ht * P:(ht + 1) * P], fpe[:, a, j],
                                 start=(j == 0), stop=(j == 15))
                ins.then_inc(hid_full, 1)
            pe.wait_ge(pooled_done, 1)
            pe.wait_ge(small_in, 48)
            for a in range(2):
                ins = mm(bank[5][:, a * T:(a + 1) * T], wg[:, a], pooled[:, a], start=True, stop=True)
            ins.then_inc(mix_full, 1)
            pe.wait_ge(conv_done, 1)
            pe.wait_ge(u_done, 1)
            pe.wait_ge(ch_done, 1)
            pe.wait_ge(poolT_done, 1)
            pe.wait_ge(hidT_done, 1)

            with pe.Fori(0, N_MG // 2) as i2:
                for s in range(2):
                    i = i2 * 2 + s
                    slot = (CH_MG + s) % WSLOTS
                    w = wch[:, slot, 0:CHUNK].rearrange("p (k c) -> p k c", c=WCOLS)
                    wp = wch[:, slot, CHUNK:].rearrange("p (a k c) -> p a k c", a=2, k=2)

                    def s_unit(u):
                        g, b = u % 2, u // 2
                        rows = slice(g * HD, (g + 1) * HD)
                        if u == 0:
                            pe.wait_ge(qcur_done, i + 1)
                        pe.wait_ge(s_max, i * 4 + max(u - 1, 0) + 1)
                        for t in range(NT):
                            ins = mm(bank[4 + u % 2][:, t * P:(t + 1) * P + t * P],
                                     qcur[rows, t * P:(t + 1) * P],
                                     kT[rows, b, 0:(t + 1) * P], start=True, stop=True)
                        ins.then_inc(s_full, 1)

                    def t_unit(u):
                        pe.wait_ge(p_done, i * 4 + (u + 1) + 1)
                        pe.wait_ge(pT_done, i * 4 + u + 1)
                        for c in range(3):
                            ins = nc.tensor.transpose(bank[6][:, c * P:(c + 1) * P], sP[:, u % 2, c * P:(c + 1) * P], ident)
                        ins.then_inc(pT_full, 1)

                    def pv_unit(u):
                        g, b = u % 2, u // 2
                        cols = slice(g * HD, (g + 1) * HD)
                        pe.wait_ge(pT_done, i * 4 + (u + 1) + 1)
                        if u == 0:
                            pe.wait_ge(o_read, i + 1)
                        c = 2 * HD * u
                        mm(bank[7][:, c:c + HD], sPT[:, u % 2, 0:P], vN[:, b, 0, cols], start=True, stop=True)
                        mm(bank[7][:, c + HD:c + 2 * HD], sPT[:, u % 2, P:2 * P], vN[:, b, 0, cols], start=True, stop=False)
                        mm(bank[7][:, c + HD:c + 2 * HD], sPT[:, u % 2, 2 * P:3 * P], vN[:, b, 1, cols],
                           start=False, stop=True).then_inc(pv_full, 1)

                    s_unit(0)
                    s_unit(1)
                    pe.wait_ge(chunk_in[slot], i2 * 16 + 16 * ((CH_MG + s) // WSLOTS + 1))
                    pe.wait_ge(ga_done, i + 1)
                    pair(bank[0], w, 0, ga_full)
                    t_unit(0)
                    s_unit(2)
                    pe.wait_ge(gb_done, i + 1)
                    channels(bank[1][:, 0:T], w, 2 * P)
                    pv_unit(0)
                    t_unit(1)
                    s_unit(3)
                    channels(bank[1][:, T:2 * T], w, 3 * P).then_inc(gb_full, 1)
                    pv_unit(1)
                    t_unit(2)
                    pe.wait_ge(merge_done, i + 1)
                    for a in range(2):
                        ins = channels(bank[2][:, a * T:(a + 1) * T], wp[:, 0], a * P, poolT, 2)
                    ins.then_inc(yp_full, 1)
                    pv_unit(2)
                    t_unit(3)
                    for a in range(2):
                        ins = channels(bank[3][:, a * T:(a + 1) * T], wp[:, 1], a * P, convT, 2)
                    ins.then_inc(yc_full, 1)
                    pv_unit(3)

            for g in range(KVG):
                for ht in range(2):
                    mm(bank[4][g * HD:(g + 1) * HD, 0:16], cw2[:, ht], hidT[:, ht, g, 0:16], start=(ht == 0), stop=(ht == 1))
            for g in range(KVG):
                for r in range(REP):
                    for ht in range(2):
                        ins = mm(bank[4][32 * r:32 * r + 32, 64 + g * HD:64 + (g + 1) * HD], hidT[:, 2 + ht, g], cw2[:, 2 + ht],
                                 start=(ht == 0), stop=(ht == 1))
            ins.then_inc(kc_full, 1)
            have_chunk(pe, CH_M0A)
            w = chunk_tiles(CH_M0A)
            pe.wait_ge(merge_done, N_MG + 1)
            pair(bank[2], w, 0, m0_full)
            pe.wait_ge(kc_done, 1)
            pe.wait_ge(o_read, N_MG + 1)
            for g in range(KVG):
                rows = slice(g * HD, (g + 1) * HD)
                for a in range(NT * REP):
                    t, r = a // REP, a % REP
                    ins = mm(bank[(5, 7)[g]][:, 16 * a:16 * a + 16], qT[rows, r, t * P:(t + 1) * P], kcT[rows], start=True, stop=True)
            ins.then_inc(sc_full, 1)
            pair(bank[3], w, 2 * P, m0_full)
            pe.wait_ge(pc_done, 1)
            for t in range(NT):
                for g in range(KVG):
                    src = pc[:, t * HEADS + g * REP:t * HEADS + (g + 1) * REP].rearrange("p a c -> p (a c)")
                    ins = nc.tensor.transpose(bank[6][:, (2 * t + g) * P:(2 * t + g + 1) * P], src, ident)
            ins.then_inc(pcT_full, 1)
            pe.wait_ge(pcT_done, 1)
            pe.wait_ge(o_read, N_MG + 1)
            for t in range(NT):
                for g in range(KVG):
                    ins = mm(bank[(7, 4)[t]][:, g * 256:(g + 1) * 256], pcT[:, 2 * t + g], vbd[:, g], start=True, stop=True)
            ins.then_inc(oc_full, 1)
            pe.wait_ge(o_done, 2)
            for k in range(4):
                for t in range(NT):
                    ins = nc.tensor.transpose(bank[k // 2][:, (k % 2) * T + t * P:(k % 2) * T + (t + 1) * P],
                                              oacc[:, t, k * P:(k + 1) * P], ident)
                if k % 2:
                    ins.then_inc(oT_full, 1)
            pe.wait_ge(oT_done, 2)
            have_chunk(pe, CH_NSA)
            wn = wch[:, CH_NSA % WSLOTS, 0:CHUNK].rearrange("p (k c) -> p k c", k=4)

            def nsa(n):
                for a in range(2):
                    ins = channels(bank[5 + n % 2][:, a * T:(a + 1) * T], wn, (2 * n + a) * P, oT, 4)
                ins.then_inc(yn_full, 1)

            nsa(0)
            nsa(1)
            have_chunk(pe, CH_M0B)
            w = chunk_tiles(CH_M0B)
            for n in range(2, 4):
                pe.wait_ge(m0_done, n - 1)
                pair(bank[n], w, (n - 2) * 2 * P, m0_full)
            for n in range(2, 4):
                pe.wait_ge(m0_read, n - 1)
                nsa(n)
            pe.wait_ge(m0_read, 4)
            for n in range(4):
                t, half = n % 2, n // 2
                have_chunk(pe, CH_WO + half)
                w = chunk_tiles(CH_WO + half)
                for k in range(KT):
                    ins = mm(bank[(7, 4, 0, 1)[n]][:], merged[:, k, t * P:(t + 1) * P], w[:, k], start=(k == 0), stop=(k == KT - 1))
                ins.then_inc(wo_full, 1)
            pe.wait_ge(h_done, 4)
            pe.wait_ge(xn2_done, NT)
            for k in range(KT):
                for t in range(NT):
                    ins = nc.tensor.transpose(bank[4 + k // 2][:, (k % 2) * T + t * P:(k % 2) * T + (t + 1) * P],
                                              xn2[:, t, k * P:(k + 1) * P], ident)
                if k % 2:
                    ins.then_inc(xn2T_full, 1)
            pe.wait_ge(xn2T_done, 4)
            pe.wait_ge(route_in, 32)
            for t in range(NT):
                c = t * (GROUPS + NE)
                for k in range(KT):
                    ins = mm(bank[4][:, c:c + GROUPS + NE], xn2T[:, k, t * P:(t + 1) * P], rw[:, k], start=(k == 0), stop=(k == KT - 1))
            ins.then_inc(logit_full, 1)
            pe.wait_ge(mask_done, 1)
            mm(bank[5][:, 0:NE], tri, mask[:, 0], start=True, stop=True)
            mm(bank[5][:, NE:2 * NE], tri, mask[:, 1], start=True, stop=False)
            mm(bank[5][:, NE:2 * NE], ones, mask[:, 0], start=False, stop=True)
            for t in range(NT):
                ins = mm(bank[5][:, 2 * NE:3 * NE], ones, mask[:, t], start=(t == 0), stop=(t == NT - 1))
            ins.then_inc(rank_full, 1)

            pe.wait_ge(passes_done, 1)
            passes = pe.value_load(npass[0:1, 0:1], min_val=1, max_val=MAXPASS)
            with pe.Fori(0, passes * NB) as b:
                pe.wait_ge(sel_done, b + 1)
                pe.wait_ge(hT_done, b + 1)
                for t in range(NT):
                    ins = nc.tensor.transpose(bank[1][:, t * P:(t + 1) * P], flat(selw[:, t]), ident)
                ins.then_inc(cmb_full, 1)
                for half in range(2):
                    for k in range(4):
                        for t in range(NT):
                            ins = mm(bank[2 + half][:, k * P:(k + 1) * P], xn2[:, t, (4 * half + k) * P:(4 * half + k + 1) * P],
                                     flat(sel[:, t]), start=(t == 0), stop=(t == NT - 1))
                    ins.then_inc(xg_full, 1)
                pe.wait_ge(xg_done, b * 2 + 2)
                pe.wait_ge(hn_done, b + 1)
                for q in range(NQ1):
                    pe.wait_ge(expert_in[q], b * 16 + 16)
                    for e in range(EB):
                        ins = mm(bank[0][CAP * e:CAP * (e + 1)], xgT[:, q, CAP * e:CAP * (e + 1)],
                                 wexp[:, q, e * 2 * HID:(e + 1) * 2 * HID], start=(q == 0), stop=(q == NQ1 - 1))
                    if q == NQ1 - 1:
                        ins.then_inc(hid1_full, 1)
                    else:
                        ins.then_inc(expert_used, 1)
                pe.wait_ge(hn_done, b + 2)
                pe.wait_ge(cmb_done, b + 1)
                pe.sem_inc(expert_used, 1)
                for k in range(HT):
                    ins = nc.tensor.transpose(bank[1][:, k * P:(k + 1) * P], hN[:, k * P:(k + 1) * P], ident)
                ins.then_inc(hT_full, 1)
                pe.wait_ge(hT_done, b + 2)
                for half in range(2):
                    pe.wait_ge(yn_done, b * 2 + half + 1)
                    for ht in range(HT):
                        q = NQ1 + HT * half + ht
                        pe.wait_ge(expert_in[q], b * 16 + 16)
                        for e in range(EB):
                            ins = mm(bank[4 + half][CAP * e:CAP * (e + 1)], hT[:, ht, CAP * e:CAP * (e + 1)],
                                     wexp[:, q, e * 512:(e + 1) * 512], start=(ht == 0), stop=(ht == HT - 1))
                        if ht < HT - 1:
                            ins.then_inc(expert_used, 1)
                    ins.then_inc(y_full, 1)
                    pe.wait_ge(yn_done, b * 2 + (half + 1) + 1)
                    pe.sem_inc(expert_used, 1)
                    for t in range(NT):
                        pe.wait_ge(add_done, b * 4 + max(2 * half + t - 1, 0) + 1)
                        mm(bank[6 + t][:], cmbT[:, t * P:(t + 1) * P], yN[:, half * 512:(half + 1) * 512],
                           start=True, stop=True).then_inc(comb_done, 1)


def constants():
    import numpy as np
    c = np.zeros((P, K_N), np.float32)
    q = np.arange(P)[:, None]
    far = np.float32(-1e34)
    c[:, K_ID:K_ID + P] = np.eye(P)
    key = np.arange(P)[None, :]
    c[:, K_DIST:K_DIST + P] = np.where(key <= q, key - q, far)
    key = np.arange(2 * P)[None, :]
    c[:, K_DIST + P:K_DIST + 3 * P] = np.where(key <= q + P, key - (q + P), far)
    c[:, K_TRI:K_TRI + P] = q < np.arange(P)[None, :]
    c[:, K_ONE:K_ONE + P] = 1.0
    c[:, K_IOTA:K_IOTA + CAP] = np.arange(1, CAP + 1)
    slopes = 2.0 ** (-8.0 * np.arange(1, HEADS + 1) / HEADS)
    for t in range(NT):
        d = t * P + q - (np.arange(16)[None, :] * CMP_STRIDE + CMP_LEN - 1)
        ok = (d >= 0) & (np.arange(16)[None, :] < NCMP)
        c[:, K_CM + t * 16:K_CM + (t + 1) * 16] = ok
        for hd in range(HEADS):
            o = K_CB + (t * HEADS + hd) * 16
            c[:, o:o + 16] = np.where(ok, -slopes[hd] * d, far)
    tt = np.arange(T)
    for a in range(2):
        for g in range(2):
            c[g * HD:(g + 1) * HD, K_IC + a * T:K_IC + (a + 1) * T] = 1.0 / np.minimum(tt + 1, POOL_WINDOWS[2 * a + g])
    c[:, K_SL:K_SL + HEADS] = slopes
    c[:, K_RK:K_RK + PER_GROUP] = PER_GROUP - np.arange(PER_GROUP)
    return c


def kernel(**inputs):
    import numpy as np
    import concourse.bacc as bacc
    from concourse.bass_utils import run_bass_kernel_spmd as run

    a = {k: np.asarray(v) for k, v in inputs.items()}

    def tiles(w):
        return w.reshape(-1, P, w.shape[1]).transpose(1, 0, 2).reshape(P, -1)

    w_in = a["w_in"][0]
    o_kv, o_gate = HEADS * HD, HEADS * HD + 6 * KVG * HD
    o_u = o_gate + GATES
    o_m = o_u + 4 * 256
    wq = w_in[:, 0:o_kv].reshape(D, KVG, REP, HD).transpose(0, 2, 1, 3).reshape(D, HEADS * HD)
    front = np.zeros((N_CHUNKS, P, CHUNK + PROJ), np.float32)

    def put(n, *parts):
        at = 0
        for part in parts:
            front[n, :, at:at + part.shape[1]] = part
            at += part.shape[1]

    put(CH_Q, tiles(wq))
    put(CH_KV, tiles(w_in[:, o_kv:o_kv + 512]))
    put(CH_KVG, tiles(w_in[:, o_kv + 512:o_u]))
    put(CH_UH, tiles(w_in[:, o_u:o_u + 512]))
    put(CH_BC, tiles(w_in[:, o_u + 512:o_m]))
    put(CH_CK, tiles(a["cmp_w1"][0, 0]))
    put(CH_CV, tiles(a["cmp_w1"][0, 1]))
    for i in range(N_MG):
        c = slice(256 * i, 256 * i + 256)
        gates = np.concatenate([w_in[:, o_m + D:o_m + 2 * D][:, c], w_in[:, o_m + 2 * D:o_m + 3 * D][:, c]], axis=1)
        put(CH_MG + i, tiles(gates), tiles(a["w_pool_proj"][0][:, c]), tiles(a["w_conv_proj"][0][:, c]))
    put(CH_M0A, tiles(w_in[:, o_m:o_m + 512]))
    put(CH_M0B, tiles(w_in[:, o_m + 512:o_m + 1024]))
    put(CH_NSA, tiles(a["w_nsa_proj"][0]))
    for i in range(2):
        put(CH_WO + i, tiles(a["w_o"][0][:, 512 * i:512 * i + 512]))

    params = np.concatenate([
        a["norm1_g"][0].reshape(KT, P), a["pool_scale"][0].reshape(2, P), a["conv_w"][0].reshape(2 * CONV_K, P),
        a["cmp_pe"][0].reshape(CMP_LEN, P)]).T
    wgrp = np.zeros((P, 2, P), np.float32)
    for g in range(4):
        o = (g % 2) * HD
        wgrp[o:o + HD, g // 2, o:o + HD] = a["pool_w"][0, g]

    w1 = a["expert_w1"][0].reshape(NB, EB, NQ1, P, HID)
    w3 = a["expert_w3"][0].reshape(NB, EB, NQ1, P, HID)
    w2 = a["expert_w2"][0].reshape(NB, EB, HT, P, 2, 512)
    experts = np.concatenate([
        np.concatenate([w1, w3], axis=4).transpose(0, 2, 3, 1, 4).reshape(NB, NQ1, P, ECHUNK),
        w2.transpose(0, 4, 2, 3, 1, 5).reshape(NB, NQ2, P, ECHUNK)], axis=1)

    arrays = {
        "x": a["x"][0],
        "params": params,
        "consts": constants(),
        "front": front,
        "small": tiles(a["cmp_w2"][0].reshape(2 * HID, HD)),
        "wgrp": wgrp.reshape(P, 2 * P),
        "vecs": np.stack([a["norm2_g"][0], a["final_norm_g"]]),
        "routerw": tiles(np.concatenate([a["router_group_w"][0], a["router_expert_w"][0]], axis=1)),
        "routerb": np.concatenate([a["router_group_b"][0], a["router_expert_b"][0]])[None],
        "experts": experts,
    }
    nc = bacc.Bacc("TRN2", target_bir_lowering=False, num_devices=1)
    args, feed = [], {}
    for name, v in arrays.items():
        feed[f"in_{name}"] = np.ascontiguousarray(v)
        args.append(nc.dram_tensor(f"in_{name}", v.shape, F32, kind="ExternalInput").ap())
    args.append(nc.dram_tensor("out_y", (T, D), F32, kind="ExternalOutput").ap())
    build(nc, *args)
    r = run(nc, [feed], core_ids=[0])
    return r.results[0]["out_y"].reshape(1, T, D)
```

```python
from contextlib import ExitStack

import concourse.bass as bass
from concourse import mybir

ALU = mybir.AluOpType
ACT = mybir.ActivationFunctionType
AX = mybir.AxisListType
F32 = mybir.dt.float32
F32R = mybir.dt.float32r
I32 = mybir.dt.int32

P = 128
D = 1024
T = 256
NT = T // P
KT = D // P
HD = 64
HEADS = 8
KVG = 2
REP = HEADS // KVG
CMP_LEN, CMP_STRIDE = 32, 16
NCMP = T // CMP_STRIDE - CMP_LEN // CMP_STRIDE + 1
POOL_WINDOWS = (2, 4, 8, 16)
PW = 256
PAD = 16
CONV_K = 3
GROUPS, PER_GROUP = 4, 8
NE = GROUPS * PER_GROUP
HID = D // 4
HT = HID // P
CAP = 32
EB = P // CAP
NB = NE // EB
EPS = 1e-6
NEG = -1e30
SLOT = 2048
SLOTS = 16
GATES = HEADS * 3
GELU_C = 0.7978845608028654

(CH_Q, CH_KV, CH_VG, CH_CK, CH_UH, CH_CV, CH_BC, CH_MG) = range(8)
N_MG = 4
CH_M0A = CH_MG + N_MG
CH_M0B = CH_M0A + 1
CH_NSA = CH_M0B + 1
CH_WO = CH_NSA + 1
N_CHUNKS = CH_WO + 2
VGC = 2 * P + GATES
PROJ = 2 * 2 * 2 * P
SPLITS = [n for n in range(N_CHUNKS) if n not in (CH_CK, CH_CV)]

SLOT_PROJ = 3
SET_C, SET_B, SET_A = 4, 8, 12
CHUNK_SET = {CH_Q: SET_A, CH_KV: SET_B, CH_VG: SET_C, CH_UH: SET_A, CH_BC: SET_C,
             CH_M0A: SET_B, CH_M0B: SET_C, CH_NSA: SET_A, CH_WO: SET_B, CH_WO + 1: SET_A}
for _i in range(N_MG):
    CHUNK_SET[CH_MG + _i] = (SET_B, SET_A)[_i % 2]

NQ1 = KT
NQ2 = 2 * HT
NQ = NQ1 + NQ2
ROUND = 4
ECHUNK = EB * 2 * HID
MAXPASS = T // CAP

PR_G1 = 0
PR_PS = PR_G1 + KT
PR_CW = PR_PS + 2
PR_PE = PR_CW + 2 * CONV_K
PR_G2 = PR_PE + CMP_LEN
PR_N = PR_G2 + KT

K_ID = 0
K_DIST = K_ID + P
K_TRI = K_DIST + 3 * P
K_ONE = K_TRI + P
K_IOTA = K_ONE + P
K_CB = K_IOTA + CAP
K_CM = K_CB + NT * HEADS * 16
K_IC = K_CM + NT * 16
K_SL = K_IC + 2 * T
K_RK = K_SL + HEADS
K_FOLD = K_RK + PER_GROUP
K_CAP = K_FOLD + 32
K_N = K_CAP + MAXPASS


def build(nc, x, params, consts, front, projs, small, wgrp, vecs, routerw, routerb, experts, out):
    with ExitStack() as ctx:
        start = {}

        def sb(name, shape, dt=F32):
            start[name] = (nc.sbuf_base + 31) // 32 * 32
            return ctx.enter_context(nc.sbuf_tensor(name, shape, dt))

        def over(name, shape, base, at=0):
            return nc.alloc_sbuf_tensor_at(name, shape, F32, offset=start[base] + 4 * at)

        def sem(name):
            return ctx.enter_context(nc.semaphore(name))

        bank = [ctx.enter_context(nc.psum_tensor(f"bank{i}", [P, 512], F32)) for i in range(8)]

        h = sb("h", [P, NT, D])
        con = sb("con", [P, K_N])
        prm = sb("prm", [P, PR_N])
        ring = sb("ring", [P, SLOTS, SLOT])
        stat = sb("stat", [P, 64])
        part = {s: over(f"part{s}", [P, SLOT], "ring", s * SLOT) for s in range(SET_C, SLOTS)}
        xhi = sb("xhi", [P, KT, T])
        xlo = sb("xlo", [P, KT, T])
        merged = sb("merged", [P, KT, T])
        qT = sb("qT", [P, REP, T])
        kv = sb("kv", [P, 4 * T])
        gts = sb("gts", [P, NT, GATES])
        hidg = sb("hidg", [P, 4, 2 * NCMP])
        hidu = sb("hidu", [P, 4, 2 * NCMP])
        hidT = sb("hidT", [P, 4, KVG, 32])
        cw2 = sb("cw2", [P, 4, HD])
        kcT = sb("kcT", [P, 32])
        vbd = sb("vbd", [P, KVG, REP * HD])
        pcx = sb("pcx", [P, NT * HEADS, 16])
        pcs = sb("pcs", [P, 4, NT * HEADS])
        att = sb("att", [P, 6 * 3 * P])
        qcur = sb("qcur", [P, T])
        npass = sb("npass", [P, 1], I32)
        pcnt = sb("pcnt", [P, 8 + MAXPASS])
        smx = sb("smx", [P, 2, NT])
        ssum = sb("ssum", [P, 4, NT])
        coef = sb("coef", [P, 4, NT])
        otmp = sb("otmp", [P, KVG * NT * HD])
        oacc = sb("oacc", [P, NT, HEADS * HD])
        gab = sb("gab", [P, 2, 512])
        wg = sb("wg", [P, 2, P])
        mixed = sb("mixed", [P, 2, 2, T])
        rw = sb("rw", [P, KT, GROUPS + NE])
        rb = sb("rb", [P, GROUPS + NE])

        kT = kv[:, 0:2 * T].rearrange("p (b t) -> p b t", b=2)
        vN = kv[:, 2 * T:4 * T].rearrange("p (b t c) -> p b t c", b=2, t=NT)
        ga, gb = gab[:, 0], gab[:, 1]
        poolT, convT = mixed[:, 0], mixed[:, 1]
        gates = (ga, gb, kv[:, 0:512], kv[:, 512:1024])
        sS = att[:, 0:6 * P].rearrange("p (b k) -> p b k", b=2)
        sP = att[:, 6 * P:12 * P].rearrange("p (b k) -> p b k", b=2)
        sPT = att[:, 12 * P:18 * P].rearrange("p (b k) -> p b k", b=2)
        PL = PAD + T
        upad = att[:, 0:2 * PL].rearrange("p (a t) -> p a t", a=2)
        s2 = att[:, 2 * PL:4 * PL].rearrange("p (a t) -> p a t", a=2)
        s4 = att[:, 4 * PL:6 * PL].rearrange("p (a t) -> p a t", a=2)
        scT = att[:, 0:512]
        osplit = over("osplit", [P, 2, 4, T], "att")
        ohi, olo = osplit[:, 0], osplit[:, 1]
        oflat = oacc[:].rearrange("p t c -> p (t c)")
        zpad = oflat[:, 0:2 * (2 + T)].rearrange("p (a t) -> p a t", a=2)
        g2b = oflat[:, 0:D]
        mflat = merged[:].rearrange("p k t -> p (k t)")
        shf = mflat[:, 0:1024].rearrange("p (a g t) -> p a g t", a=2, g=KVG)
        fpe = mflat[:, 1024:2048].rearrange("p (a j c) -> p a j c", a=2, j=16)
        hidp = mflat[:, 0:512].rearrange("p (a c) -> p a c", a=2)
        diag = gab[:, 0, 0:NT * P].rearrange("p (t q) -> p t q", t=NT)
        pooled = ga.rearrange("p (a t) -> p a t", a=2)
        convh = gb.rearrange("p (a t) -> p a t", a=2)
        pc = poolT.rearrange("p a t -> p (a t)").rearrange("p (a c) -> p a c", c=32)
        pcT = convT.rearrange("p a t -> p (a t)").rearrange("p (a q) -> p a q", q=P)
        mhi0 = over("mhi0", [P, 4, T], "mixed")
        mhi = (mhi0[:], xhi[:, 0:4])
        mlo = over("mlo", [P, KT, T], "merged")
        qflat = qT[:].rearrange("p r t -> p (r t)")
        rt = qflat[:, 0:256].rearrange("p (a t e) -> p a t e", t=NT, e=PER_GROUP)
        etmp = qflat[:, 256:320].rearrange("p (t e) -> p t e", t=NT)
        comb = qflat[:, 320:384].rearrange("p (t e) -> p t e", t=NT)
        mask = qflat[:, 384:448].rearrange("p (t e) -> p t e", t=NT)
        rank = qflat[:, 448:512].rearrange("p (t e) -> p t e", t=NT)
        lg = qflat[:, 512:512 + NT * (GROUPS + NE)].rearrange("p (t e) -> p t e", t=NT)
        xn2 = att[:, 0:NT * D].rearrange("p (t d) -> p t d", t=NT)
        fin = xn2
        xgT = kv[:].rearrange("p (k s) -> p k s", k=KT)
        yN = gab[:].rearrange("p a c -> p (a c)")
        xn2T = over("xn2T", [P, KT, T], "xhi")
        squares = over("squares", [P, KT * T], "xlo")
        sel = mflat[:, 0:256].rearrange("p (t e j) -> p t e j", t=NT, e=EB)
        selw = mflat[:, 256:512].rearrange("p (t e j) -> p t e j", t=NT, e=EB)
        cmbT = mflat[:, 512:768]
        sl1 = mflat[:, 768:1024]
        hN = mflat[:, 1024:1280]
        hT = mflat[:, 1280:1536].rearrange("p (k s) -> p k s", k=HT)

        ident = con[:, K_ID:K_ID + P]
        dist = con[:, K_DIST:K_DIST + 3 * P]
        tri = con[:, K_TRI:K_TRI + P]
        ones = con[:, K_ONE:K_ONE + P]
        iota = con[:, K_IOTA:K_IOTA + CAP]
        cbias = con[:, K_CB:K_CB + NT * HEADS * 16].rearrange("p (a c) -> p a c", c=16)
        cmask = con[:, K_CM:K_CM + NT * 16].rearrange("p (t c) -> p t c", c=16)
        icnt = con[:, K_IC:K_IC + 2 * T].rearrange("p (a t) -> p a t", a=2)
        rk8 = con[:, K_RK:K_RK + PER_GROUP]
        fold = con[:, K_FOLD:K_FOLD + 32]
        steps_of_cap = con[:, K_CAP:K_CAP + MAXPASS]

        x_in = [sem(f"x_in{t}") for t in range(NT)]
        ident_in = sem("ident_in")
        con_in = sem("con_in")
        prm_in = sem("prm_in")
        small_in = sem("small_in")
        route_in = sem("route_in")
        vec_in = sem("vec_in")
        chunk_in = {s: sem(f"chunk_in{s}") for s in (0, 1, 2, 3, *range(SET_C, SLOTS, 2))}
        proj_in = [sem(f"proj_in{i}") for i in range(2)]
        expert_in = [sem(f"expert_in{i}") for i in range(SLOTS)]
        expert_used = sem("expert_used")
        passes_done = sem("passes_done")
        out_done = sem("out_done")

        dve_step = sem("dve_step")
        loop_step = sem("loop_step")
        moe_step = sem("moe_step")
        zeros_set = sem("zeros_set")
        ssq_done = sem("ssq_done")
        rstd_done = sem("rstd_done")
        pool_step = sem("pool_step")
        warm_done = sem("warm_done")
        hi_done = sem("hi_done")
        split_done = sem("split_done")
        diag_done = sem("diag_done")
        xhi_done = sem("xhi_done")
        xT_full = sem("xT_full")
        xnT_done = sem("xnT_done")
        q_full = sem("q_full")
        kvc_full = sem("kvc_full")
        kk_full = sem("kk_full")
        vg_full = sem("vg_full")
        u_full = sem("u_full")
        h_full = sem("h_full")
        b_full = sem("b_full")
        c_full = sem("c_full")
        hidp_full = sem("hidp_full")
        hidp_done = sem("hidp_done")
        hid_full = sem("hid_full")
        hid_done = sem("hid_done")
        mix_full = sem("mix_full")
        kc_full = sem("kc_full")
        scT_full = sem("scT_full")
        scT_done = sem("scT_done")
        sc_full = sem("sc_full")
        q_done = sem("q_done")
        kvc_done = sem("kvc_done")
        kk_done = sem("kk_done")
        vg_done = sem("vg_done")
        u_done = sem("u_done")
        ch_done = sem("ch_done")
        conv_done = sem("conv_done")
        pooled_done = sem("pooled_done")
        poolT_done = sem("poolT_done")
        flat_done = sem("flat_done")
        gelu_in = sem("gelu_in")
        tanh_done = sem("tanh_done")
        hidT_done = sem("hidT_done")
        kc_done = sem("kc_done")
        csub_done = sem("csub_done")
        cexp_done = sem("cexp_done")
        pc_done = sem("pc_done")
        pcT_full = sem("pcT_full")
        pcT_done = sem("pcT_done")
        oc_full = sem("oc_full")
        s_full = sem("s_full")
        qcur_done = sem("qcur_done")
        s_max = sem("s_max")
        p_done = sem("p_done")
        pT_full = sem("pT_full")
        pT_done = sem("pT_done")
        pv_full = sem("pv_full")
        o_read = sem("o_read")
        ga_full = sem("ga_full")
        gb_full = sem("gb_full")
        yp_full = sem("yp_full")
        yc_full = sem("yc_full")
        ga_done = sem("ga_done")
        gb_done = sem("gb_done")
        merge_done = sem("merge_done")
        o_done = sem("o_done")
        oT_full = sem("oT_full")
        ohi_done = sem("ohi_done")
        oT_done = sem("oT_done")
        m0_full = sem("m0_full")
        yn_full = sem("yn_full")
        m0_done = sem("m0_done")
        m0_read = sem("m0_read")
        merged_done = sem("merged_done")
        mhi_done = sem("mhi_done")
        mlo_done = sem("mlo_done")
        wo_used = sem("wo_used")
        wo_full = sem("wo_full")
        h_done = sem("h_done")
        ssq2_done = sem("ssq2_done")
        rstd2_done = sem("rstd2_done")
        xn2_done = sem("xn2_done")
        xn2T_full = sem("xn2T_full")
        xn2T_done = sem("xn2T_done")
        logit_full = sem("logit_full")
        gsub_done = sem("gsub_done")
        gexp_done = sem("gexp_done")
        tsub_done = sem("tsub_done")
        texp_done = sem("texp_done")
        mask_done = sem("mask_done")
        rank_full = sem("rank_full")
        count_full = sem("count_full")
        sel_done = sem("sel_done")
        cmb_full = sem("cmb_full")
        cmb_done = sem("cmb_done")
        xg_full = sem("xg_full")
        xg_done = sem("xg_done")
        hid1_full = sem("hid1_full")
        silu_done = sem("silu_done")
        y_full = sem("y_full")
        yn_done = sem("yn_done")
        ssq3_done = sem("ssq3_done")
        rstd3_done = sem("rstd3_done")
        gained = sem("gained")
        dve_fin = sem("dve_fin")
        act_fin = sem("act_fin")

        comb_done = sem("comb_done")

        add_done = sem("add_done")
        hT_full = sem("hT_full")
        hT_done = sem("hT_done")
        hn_done = sem("hn_done")
        rank_done = sem("rank_done")
        sel_step = sem("sel_step")

        def flat(ap):
            n = len(ap.shape) - 1
            names = ["a", "b", "c", "d"][:n]
            return ap.rearrange(f"p {' '.join(names)} -> p ({' '.join(names)})") if n > 1 else ap

        def slot(n, half):
            return (CH_CK, CH_CV).index(n) * 2 + half if n in (CH_CK, CH_CV) else CHUNK_SET[n] + 2 * half

        def raw(n, half):
            return ring[:, slot(n, half)]

        def low(n, half):
            return part[slot(n, half)]

        def high(n, half):
            return part[slot(n, half) + 1]

        def before(n):
            return [m for m in range(n) if slot(m, 0) == slot(n, 0)]

        def floats(n):
            return KT // 2 * VGC if n == CH_VG else SLOT

        def proj(i):
            return ring[:, SLOT_PROJ, (i % 2) * PROJ:(i % 2 + 1) * PROJ]

        def landed(eng, n, half, more=0):
            eng.wait_ge(chunk_in[slot(n, half)], more * 16 + 16 * (len(before(n)) + 1))

        def have_high(act, n, half, more=0):
            landed(act, n, half, more)
            c = floats(n)
            nc.scalar.copy(high(n, half)[:, 0:c].bitcast(F32R), raw(n, half)[:, 0:c]).then_inc(hi_done, 1)

        def have_low(dve, n, half, more=0):
            c = floats(n)
            dve.wait_ge(hi_done, more * 4 + 2 * SPLITS.index(n) + half + 1)
            nc.vector.tensor_tensor(low(n, half)[:, 0:c].bitcast(F32R), raw(n, half)[:, 0:c], high(n, half)[:, 0:c], ALU.subtract).then_inc(split_done, 1)

        block = ctx.enter_context(nc.Block())

        @block.sync
        def _(sp):
            for t in range(NT):
                sp.dma_start(h[:, t], x[t * P:(t + 1) * P]).then_inc(x_in[t], 16)
            last_product = {CH_Q: ((q_full, 1), (q_full, 2)), CH_KV: ((kvc_full, 1), (kk_full, 1)),
                            CH_VG: ((vg_full, 1), (vg_full, 1)), CH_CK: ((hidp_full, 1), (hidp_full, 2)),
                            CH_UH: ((u_full, 1), (h_full, 1)), CH_CV: ((hidp_full, 3), (hidp_full, 4)),
                            CH_BC: ((b_full, 1), (c_full, 1)), CH_M0A: ((m0_full, 1), (m0_full, 2)),
                            CH_NSA: ((yn_full, 2), (yn_full, 4)), CH_M0B: ((m0_full, 3), (m0_full, 4))}
            for i in range(N_MG):
                last_product[CH_MG + i] = ((ga_full, i + 1), (gb_full, i + 1))
            for n in range(N_CHUNKS):
                if n == CH_Q:
                    sp.dma_start(ident, consts[:, K_ID:K_ID + P]).then_inc(ident_in, 16)
                if n == CH_KV:
                    sp.dma_start(con[:, P:], consts[:, P:]).then_inc(con_in, 16)
                for half in range(2):
                    if before(n):
                        sp.wait_ge(*last_product[before(n)[-1]][half])
                    c = floats(n)
                    sp.dma_start(raw(n, half)[:, 0:c], front[n, half, :, 0:c]).then_inc(chunk_in[slot(n, half)], 16)
                i = n - CH_MG
                if 0 <= i < N_MG:
                    sp.wait_ge(*((yc_full, i - 1) if i >= 2 else (hidp_full, 4)))
                    sp.dma_start(proj(i), projs[i]).then_inc(proj_in[i % 2], 16)
                if 0 <= i < SLOT_PROJ:
                    sp.wait_ge(hidp_full, i + 1)
                    sp.dma_start(ring[:, i], experts[0, i]).then_inc(expert_in[i], 16)
            for c in range(SLOT_PROJ, SLOTS):
                if c == SLOT_PROJ:
                    sp.wait_ge(yc_full, N_MG)
                elif c < SET_B:
                    sp.wait_ge(m0_full, 3 + (c - SET_C) // 2)
                elif c < SET_A:
                    sp.wait_ge(wo_used, 1 + (c - SET_B) // 2)
                else:
                    sp.wait_ge(wo_full, 4)
                b, q = c // NQ, c % NQ
                sp.dma_start(ring[:, c], experts[b, q]).then_inc(expert_in[c], 16)

            for c in range(SLOTS, ROUND * NQ):
                b, q = c // NQ, c % NQ
                sp.wait_ge(expert_used, c - SLOTS + 1)
                sp.dma_start(ring[:, c % SLOTS], experts[b, q]).then_inc(expert_in[c % SLOTS], 16)
            sp.wait_ge(passes_done, 1)
            passes = sp.value_load(npass[0:1, 0:1], min_val=1, max_val=MAXPASS)
            rounds = experts.rearrange("(r b) q p c -> r b q p c", b=ROUND)
            with sp.Fori(1, passes * (NB // ROUND)) as r:
                for c in range(ROUND * NQ):
                    b, q = c // NQ, c % NQ
                    sp.wait_ge(expert_used, r * (ROUND * NQ) + (c - SLOTS + 1))
                    sp.dma_start(ring[:, c % SLOTS],
                                 rounds[bass.ds(r % (NB // ROUND), 1), b, q].rearrange("o p c -> (o p) c")).then_inc(expert_in[c % SLOTS], 16)
            for t in range(NT):
                sp.wait_ge((dve_fin, act_fin)[t], 1)
                sp.dma_start(out[t * P:(t + 1) * P], fin[:, t]).then_inc(out_done, 16)
            sp.wait_ge(out_done, 16 * NT)

        @block.gpsimd
        def _(pool):
            nc.gpsimd.memset(upad[:, :, 0:PAD], 0.0).then_inc(zeros_set, 1)
            nc.gpsimd.memset(s2[:, :, 0:PAD], 0.0).then_inc(zeros_set, 1)
            nc.gpsimd.memset(s4[:, :, 0:PAD], 0.0).then_inc(zeros_set, 1)
            nc.gpsimd.memset(zpad[:, :, 0:2], 0.0).then_inc(zeros_set, 1)
            nc.gpsimd.memset(hidT[:], 0.0).then_inc(zeros_set, 1)
            nc.gpsimd.memset(vbd[:], 0.0).then_inc(zeros_set, 1)
            nc.gpsimd.memset(stat[:, 32:34], -0.5).then_inc(zeros_set, 1)
            nc.gpsimd.memset(kcT[:], 0.0).then_inc(zeros_set, 1)
            pool.wait_ge(zeros_set, 8)
            steps = [0]

            def step(ins):
                steps[0] += 1
                ins.then_inc(pool_step, 1)
                pool.wait_ge(pool_step, steps[0])

            def rstd(total, col):
                step(nc.gpsimd.tensor_scalar(total, total, 1.0 / D, EPS, ALU.mult, ALU.add))
                return nc.gpsimd.tensor_tensor(stat[:, col:col + 2], total, stat[:, 32:34], ALU.pow)

            pool.wait_ge(ssq_done, NT)
            rstd(stat[:, 0:2], 2).then_inc(rstd_done, 1)
            pool.wait_ge(ssq2_done, 4)
            step(nc.gpsimd.tensor_tensor(stat[:, 4:6], stat[:, 4:6], stat[:, 6:8], ALU.add))
            rstd(stat[:, 4:6], 8).then_inc(rstd2_done, 1)
            pool.wait_ge(ssq3_done, 4)
            step(nc.gpsimd.tensor_tensor(stat[:, 12:14], stat[:, 12:14], stat[:, 14:16], ALU.add))
            rstd(stat[:, 12:14], 16).then_inc(rstd3_done, 1)

        @block.scalar
        def _(act):
            for s1 in (p_done, ga_done, gb_done, hT_done, yn_done):
                act.sem_inc(s1, 1)
            act.dma_start(prm[:], params).then_inc(prm_in, 16)
            act.wait_ge(zeros_set, 8)
            nc.scalar.activation(squares[:, 0:2], stat[:, 32:34], ACT.Square).then_inc(warm_done, 1)
            act.wait_ge(warm_done, 1)
            for t in range(NT):
                act.wait_ge(x_in[t], 16)
                nc.scalar.activation(squares[:, t * D:(t + 1) * D], h[:, t], ACT.Square,
                                     accum_out=stat[:, t:t + 1]).then_inc(ssq_done, 1)
            act.dma_start(flat(cw2[:]), small).then_inc(small_in, 16)
            act.dma_start(flat(wg[:]), wgrp).then_inc(small_in, 16)
            act.dma_start(flat(rw[:]), routerw).then_inc(route_in, 16)
            act.dma_start(rb[:], routerb.to_broadcast([P, GROUPS + NE])).then_inc(route_in, 16)
            have_high(act, CH_Q, 0)
            act.wait_ge(prm_in, 16)
            for k in range(KT):
                act.wait_ge(xT_full, k // 2 + 1)
                nc.scalar.activation(xhi[:, k].bitcast(F32R), bank[k // 2][:, (k % 2) * T:(k % 2 + 1) * T], ACT.Copy,
                                     scale=prm[:, PR_G1 + k:PR_G1 + k + 1]).then_inc(xhi_done, 1)
            have_high(act, CH_Q, 1)
            have_high(act, CH_KV, 0)
            have_high(act, CH_KV, 1)
            for half in range(2):
                have_high(act, CH_VG, half)
                act.wait_ge(q_full, half + 1)
                nc.scalar.mul(flat(qT[:, 2 * half:2 * half + 2]), bank[4 + half][:], HD ** -0.5).then_inc(q_done, 1)
            have_high(act, CH_UH, 0)
            act.wait_ge(kk_full, 1)
            nc.scalar.copy(flat(kT), bank[1][:]).then_inc(kk_done, 1)
            have_high(act, CH_UH, 1)
            act.wait_ge(vg_full, 1)
            for t in range(NT):
                nc.scalar.copy(vN[:, :, t], bank[2 + t][:, 0:2 * P].rearrange("p (b c) -> p b c", b=2))
                ins = nc.scalar.activation(gts[:, t], bank[2 + t][:, 2 * P:VGC], ACT.Tanh, scale=0.5)
            ins.then_inc(vg_done, 1)
            have_high(act, CH_BC, 0)
            for a in range(2):
                if a:
                    have_high(act, CH_BC, 1)
                    act.wait_ge(h_full, 1)
                    nc.scalar.copy(flat(convh), bank[1][:]).then_inc(ch_done, 1)
                act.wait_ge(hidp_full, 2 * a + 2)
                nc.scalar.copy(hidp[:, a], bank[6 + a][:, 0:2 * P]).then_inc(hidp_done, 1)
            have_high(act, CH_MG, 0)
            have_high(act, CH_MG, 1)
            with act.Fori(0, N_MG // 2) as i2:
                for s in range(2):
                    i = i2 * 2 + s
                    act.wait_ge(s_full, i * 4 + 1)
                    act.wait_ge(q_done, 2)
                    nc.scalar.copy(qcur[:], qT[:, bass.ds(i, 1)].rearrange("p r t -> p (r t)")).then_inc(qcur_done, 1)
                    have_high(act, CH_MG + 1 + s, 0, i2)
                    for u in range(4):
                        if u == 2:
                            act.wait_ge(ga_full, i + 1)
                            act.wait_ge(merge_done, i + 1)
                            nc.scalar.activation(ga, bank[0][:], ACT.Tanh, scale=0.5).then_inc(ga_done, 1)
                        if u == 3:
                            have_high(act, CH_MG + 1 + s, 1, i2)
                        act.wait_ge(s_max, i * 4 + (u + 1) + 1)
                        act.wait_ge(pT_full, i * 4 + max(u - 1, 0) + 1)
                        act.wait_ge(o_read, i + 1)
                        nc.scalar.activation(sP[:, u % 2, 0:P], sS[:, u % 2, 0:P], ACT.Exp,
                                             bias=smx[:, u % 2, 0:1], accum_out=ssum[:, u, 0:1])
                        nc.scalar.activation(sP[:, u % 2, P:3 * P], sS[:, u % 2, P:3 * P], ACT.Exp,
                                             bias=smx[:, u % 2, 1:2], accum_out=ssum[:, u, 1:2]).then_inc(p_done, 1)
                    act.wait_ge(gb_full, i + 1)
                    nc.scalar.activation(gb, bank[1][:], ACT.Tanh, scale=0.5).then_inc(gb_done, 1)

            act.wait_ge(gelu_in, 1)
            nc.scalar.activation(hidu[:], hidu[:], ACT.Tanh, scale=GELU_C).then_inc(tanh_done, 1)

            def gate_tanh(n):
                act.wait_ge(m0_full, n + 1)
                nc.scalar.activation(gates[n], bank[n][:], ACT.Tanh, scale=0.5).then_inc(m0_done, 1)

            have_high(act, CH_M0B, 0)
            have_high(act, CH_M0B, 1)
            act.wait_ge(merge_done, N_MG + 1)
            gate_tanh(0)
            have_high(act, CH_NSA, 0)
            gate_tanh(1)
            act.wait_ge(scT_full, 1)
            nc.scalar.copy(scT[:, 0:T], bank[5][:, 0:T])
            nc.scalar.copy(scT[:, T:2 * T], bank[7][:, 0:T]).then_inc(scT_done, 1)
            have_high(act, CH_NSA, 1)
            gate_tanh(2)
            act.wait_ge(csub_done, 1)
            nc.scalar.activation(pcx[:], pcx[:], ACT.Exp).then_inc(cexp_done, 1)
            have_high(act, CH_WO, 0)
            act.wait_ge(pcT_full, 1)
            nc.scalar.copy(flat(pcT), bank[7][:]).then_inc(pcT_done, 1)
            have_high(act, CH_WO, 1)
            gate_tanh(3)
            for n in range(2):
                act.wait_ge(oT_full, n + 1)
                nc.scalar.activation(flat(ohi[:, 2 * n:2 * n + 2]).bitcast(F32R), bank[6 + n][:], ACT.Copy, scale=0.5).then_inc(ohi_done, 1)
            act.dma_start(g2b, vecs[0:1].to_broadcast([P, D])).then_inc(vec_in, 16)

            def merged_high(n):
                act.wait_ge(merged_done, n + 1)
                act.wait_ge(oc_full, 1)
                nc.scalar.copy(flat(mhi[n // 2][:, 2 * (n % 2):2 * (n % 2) + 2]).bitcast(F32R),
                               flat(merged[:, 2 * n:2 * n + 2])).then_inc(mhi_done, 1)

            for n in range(4):
                merged_high(n)
            have_high(act, CH_WO + 1, 0)
            have_high(act, CH_WO + 1, 1)

            for n in range(4):
                t, half = n % 2, n // 2
                act.wait_ge(h_done, n + 1)
                nc.scalar.activation(squares[:, n * 512:(n + 1) * 512], h[:, t, half * 512:(half + 1) * 512], ACT.Square,
                                     accum_out=stat[:, 4 + n:5 + n]).then_inc(ssq2_done, 1)
            for k in (0, 1, 4, 5):
                act.wait_ge(xn2T_full, k // 2 + 1)
                nc.scalar.activation(xn2T[:, k], bank[4 + k // 2][:, (k % 2) * T:(k % 2 + 1) * T], ACT.Copy,
                                     scale=prm[:, PR_G2 + k:PR_G2 + k + 1]).then_inc(xn2T_done, 1)
            act.wait_ge(xn2_done, NT)
            act.dma_start(g2b, vecs[1:2].to_broadcast([P, D])).then_inc(vec_in, 16)
            act.wait_ge(gsub_done, 1)
            nc.scalar.activation(rt[:, 1, :, 0:GROUPS], rt[:, 0, :, 0:GROUPS], ACT.Exp).then_inc(gexp_done, 1)
            act.wait_ge(tsub_done, 1)
            nc.scalar.activation(rt[:, 9, :, 0:1], rt[:, 8, :, 0:1], ACT.Exp).then_inc(texp_done, 1)

            act.wait_ge(passes_done, 1)
            passes = act.value_load(npass[0:1, 0:1], min_val=1, max_val=MAXPASS)
            with act.Fori(0, passes * NB) as b:
                act.wait_ge(xg_full, b * 2 + 2)
                nc.scalar.copy(flat(xgT[:, 0:4]), bank[2][:]).then_inc(xg_done, 1)
                act.wait_ge(hid1_full, b + 1)
                nc.scalar.activation(sl1, bank[0][:, 0:HID], ACT.Silu).then_inc(silu_done, 1)
                act.wait_ge(hT_full, b + 1)
                nc.scalar.copy(flat(hT), bank[1][:, 0:HT * P]).then_inc(hT_done, 1)
                for half in range(2):
                    act.wait_ge(y_full, b * 2 + (half + 1))
                    nc.scalar.copy(yN[:, half * 512:(half + 1) * 512], bank[4 + half][:]).then_inc(yn_done, 1)
            for n in range(4):
                t, half = n % 2, n // 2
                act.wait_ge(add_done, passes * (4 * NB) + n)
                nc.scalar.activation(squares[:, n * 512:(n + 1) * 512], h[:, t, half * 512:(half + 1) * 512], ACT.Square,
                                     accum_out=stat[:, 12 + n:13 + n]).then_inc(ssq3_done, 1)
            act.wait_ge(rstd3_done, 1)
            act.wait_ge(gained, 1)
            nc.scalar.activation(fin[:, 1], fin[:, 1], ACT.Copy, scale=stat[:, 17:18]).then_inc(act_fin, 1)

        @block.vector
        def _(dve):
            for s1 in (s_max, o_read, merge_done, pT_done, hn_done):
                dve.sem_inc(s1, 1)
            dve.sem_inc(add_done, 3)
            counted = [0]

            def step(ins):
                counted[0] += 1
                ins.then_inc(dve_step, 1)
                dve.wait_ge(dve_step, counted[0])

            dve.wait_ge(rstd_done, 1)
            dve.wait_ge(ident_in, 16)
            for t in range(NT):
                nc.vector.tensor_scalar(diag[:, t], ident, stat[:, 2 + t:3 + t], None, ALU.mult).then_inc(diag_done, 1)
            nc.vector.memset(fpe[:, :, :, 2 * NCMP:32], 0.0)
            have_low(dve, CH_Q, 0)
            dve.wait_ge(prm_in, 16)
            for k in range(KT):
                dve.wait_ge(xhi_done, k // 2 * 2 + 2)
                nc.vector.scalar_tensor_tensor(xlo[:, k].bitcast(F32R), bank[k // 2][:, (k % 2) * T:(k % 2 + 1) * T],
                                               prm[:, PR_G1 + k:PR_G1 + k + 1], xhi[:, k],
                                               ALU.mult, ALU.subtract).then_inc(xnT_done, 1)
            have_low(dve, CH_Q, 1)
            have_low(dve, CH_KV, 0)
            have_low(dve, CH_KV, 1)
            have_low(dve, CH_VG, 0)
            have_low(dve, CH_VG, 1)
            dve.wait_ge(kvc_full, 1)
            kvc = bank[0][:].rearrange("p (a t) -> p a t", a=2)
            for g in range(KVG):
                nc.vector.tensor_copy(shf[0:HD, :, g, :], kvc[g * HD:(g + 1) * HD])
                ins = nc.vector.tensor_copy(shf[HD:P, :, g, 0:T - 1], kvc[g * HD:(g + 1) * HD, :, 1:T])
            ins.then_inc(kvc_done, 1)
            dve.wait_ge(kvc_done, 1)
            for a in range(2):
                for g in range(KVG):
                    src = shf[:, a, g, 0:CMP_STRIDE * (NCMP + 1)].rearrange("p (c j z) -> p j c z", j=CMP_STRIDE // 2, z=2)
                    for hi in range(2):
                        ins = nc.vector.tensor_tensor(
                            fpe[:, a, 8 * hi:8 * hi + 8, g * NCMP:(g + 1) * NCMP],
                            src[:, :, hi:hi + NCMP, 0],
                            prm[:, PR_PE + 16 * a + 8 * hi:PR_PE + 16 * a + 8 * hi + 8].unsqueeze(2).to_broadcast([P, 8, NCMP]),
                            ALU.add)
            ins.then_inc(flat_done, 1)
            have_low(dve, CH_UH, 0)
            have_low(dve, CH_UH, 1)
            dve.wait_ge(vg_done, 1)
            step(nc.vector.tensor_scalar(gts[:], gts[:], 1.0, 0.5, ALU.add, ALU.mult))
            dve.wait_ge(u_full, 1)
            dve.wait_ge(zeros_set, 8)
            nc.vector.tensor_copy(upad[:, :, PAD:], bank[0][:].rearrange("p (a t) -> p a t", a=2)).then_inc(u_done, 1)
            dve.wait_ge(u_done, 1)
            have_low(dve, CH_BC, 0)
            have_low(dve, CH_BC, 1)
            step(nc.vector.tensor_tensor(s2[:, :, PAD:], upad[:, :, PAD:], upad[:, :, PAD - 1:-1], ALU.add))
            dve.wait_ge(con_in, 16)
            step(nc.vector.tensor_tensor(s4[:, :, PAD:], s2[:, :, PAD:], s2[:, :, PAD - 2:-2], ALU.add))
            nc.vector.tensor_tensor(pooled[0:HD, 0], s2[0:HD, 0, PAD:], icnt[0:HD, 0], ALU.mult)
            step(nc.vector.tensor_tensor(pooled[HD:P, 0], s4[HD:P, 0, PAD:], icnt[HD:P, 0], ALU.mult))
            step(nc.vector.tensor_tensor(s2[:, 1, PAD:], s4[:, 1, PAD:], s4[:, 1, PAD - 4:-4], ALU.add))
            nc.vector.tensor_tensor(pooled[0:HD, 1], s2[0:HD, 1, PAD:], icnt[0:HD, 1], ALU.mult)
            step(nc.vector.tensor_tensor(s4[HD:P, 1, PAD:], s2[HD:P, 1, PAD:], s2[HD:P, 1, PAD - 8:-8], ALU.add))
            step(nc.vector.tensor_tensor(pooled[HD:P, 1], s4[HD:P, 1, PAD:], icnt[HD:P, 1], ALU.mult))
            nc.vector.tensor_tensor(pooled, pooled, upad[:, :, PAD:], ALU.subtract).then_inc(pooled_done, 1)
            have_low(dve, CH_MG, 0)
            have_low(dve, CH_MG, 1)
            dve.wait_ge(ch_done, 1)
            dve.wait_ge(c_full, 1)
            step(nc.vector.tensor_tensor(zpad[:, :, 2:], bank[3][:].rearrange("p (a t) -> p a t", a=2), convh, ALU.mult))
            for tap in range(CONV_K):
                for a in range(2):
                    w = prm[:, PR_CW + 2 * tap + a:PR_CW + 2 * tap + a + 1]
                    z = zpad[:, a, tap:tap + T]
                    if tap == 0:
                        ins = nc.vector.tensor_scalar(convT[:, a], z, w, None, ALU.mult)
                    else:
                        ins = nc.vector.scalar_tensor_tensor(convT[:, a], z, w, convT[:, a], ALU.mult, ALU.add)
                step(ins)
            nc.vector.scalar_tensor_tensor(flat(convT), flat(convT), 0.5, bank[2][:], ALU.mult, ALU.mult).then_inc(conv_done, 1)
            dve.wait_ge(mix_full, 1)
            for a in range(2):
                ins = nc.vector.tensor_scalar(poolT[:, a], bank[6][:, a * T:(a + 1) * T],
                                              prm[:, PR_PS + a:PR_PS + a + 1], 0.5, ALU.mult, ALU.mult)
            ins.then_inc(poolT_done, 1)
            dve.wait_ge(hid_full, 1)
            nc.vector.tensor_copy(hidg[:], bank[7][:, 0:4 * 32].rearrange("p (a c) -> p a c", c=32)[:, :, 0:2 * NCMP]).then_inc(hid_done, 1)
            dve.wait_ge(hid_done, 1)

            LS = 9
            with dve.Fori(0, N_MG // 2) as i2:
                k = [0]

                def lstep(ins):
                    k[0] += 1
                    ins.then_inc(loop_step, 1)
                    dve.wait_ge(loop_step, i2 * (2 * LS) + k[0])

                for s in range(2):
                    i = i2 * 2 + s

                    def scores(u):
                        g = u % 2
                        dve.wait_ge(s_full, i * 4 + (u + 1) + 1)
                        dve.wait_ge(p_done, i * 4 + max(u - 1, 0) + 1)
                        lstep(nc.vector.scalar_tensor_tensor(sS[:, u % 2], dist, con[:, bass.ds(i + (K_SL + g * REP), 1)],
                                                             bank[4 + u % 2][:, 0:3 * P], ALU.mult, ALU.add))
                        nc.vector.tensor_reduce(smx[:, u % 2, 0:1], sS[:, u % 2, 0:P], AX.X, ALU.max, negate=True)
                        nc.vector.tensor_reduce(smx[:, u % 2, 1:2], sS[:, u % 2, P:3 * P], AX.X, ALU.max,
                                                negate=True).then_inc(s_max, 1)

                    def take_pT(u):
                        dve.wait_ge(pT_full, i * 4 + (u + 1) + 1)
                        dve.wait_ge(pv_full, i * 4 + max(u - 1, 0) + 1)
                        nc.vector.tensor_copy(sPT[:, u % 2], bank[6][:, 0:3 * P]).then_inc(pT_done, 1)

                    scores(0)
                    scores(1)
                    have_low(dve, CH_MG + 1 + s, 0, i2)
                    take_pT(0)
                    scores(2)
                    take_pT(1)
                    scores(3)
                    take_pT(2)
                    have_low(dve, CH_MG + 1 + s, 1, i2)
                    take_pT(3)
                    dve.wait_ge(ga_done, i + 2)
                    dve.wait_ge(yp_full, i + 1)
                    nc.vector.scalar_tensor_tensor(ga, ga, 1.0, bank[2][:], ALU.add, ALU.mult)
                    dve.wait_ge(gb_done, i + 2)
                    dve.wait_ge(yc_full, i + 1)
                    lstep(nc.vector.scalar_tensor_tensor(gb, gb, 1.0, bank[3][:], ALU.add, ALU.mult))
                    nc.vector.tensor_tensor(merged[:, bass.ds(i * 2, 2)].rearrange("p k t -> p (k t)"), ga, gb,
                                            ALU.add).then_inc(merge_done, 1)
                    dve.wait_ge(pv_full, i * 4 + 4 + 1)
                    dve.wait_ge(p_done, i * 4 + 4 + 1)
                    lstep(nc.vector.reciprocal(coef[:], ssum[:]))
                    gv = gts[:].rearrange("p t (g r c) -> p g r c t", g=KVG, r=REP)
                    for b in range(2):
                        ins = nc.vector.tensor_tensor(coef[:, 2 * b:2 * b + 2], coef[:, 2 * b:2 * b + 2],
                                                      gv[:, :, bass.ds(i, 1), 1 + b, :].rearrange("p g r t -> p g (r t)"), ALU.mult)
                    lstep(ins)
                    ov = oacc[:].rearrange("p t (g r d) -> p g t r d", g=KVG, r=REP)[:, :, :, bass.ds(i, 1), :].rearrange("p g t r d -> p g t (r d)")
                    pv = bank[7][:].rearrange("p (u t d) -> p u t d", u=4, t=NT)
                    tv = otmp[:].rearrange("p (g t d) -> p g t d", g=KVG, t=NT)
                    lstep(nc.vector.tensor_tensor(ov, pv[:, 0:2], coef[:, 0:2].unsqueeze(3).to_broadcast([P, KVG, NT, HD]), ALU.mult))
                    lstep(nc.vector.tensor_tensor(tv, pv[:, 2:4], coef[:, 2:4].unsqueeze(3).to_broadcast([P, KVG, NT, HD]), ALU.mult))
                    nc.vector.tensor_tensor(ov, ov, tv, ALU.add).then_inc(o_read, 1)
                    assert k[0] == LS * (s + 1)

            step(nc.vector.tensor_tensor(hidu[:], hidg[:], hidg[:], ALU.mult))
            step(nc.vector.tensor_scalar(hidu[:], hidu[:], 0.044715, 1.0, ALU.mult, ALU.add))
            nc.vector.tensor_tensor(hidu[:], hidu[:], hidg[:], ALU.mult).then_inc(gelu_in, 1)
            dve.wait_ge(tanh_done, 1)
            for g in range(KVG):
                c = slice(g * NCMP, (g + 1) * NCMP)
                ins = nc.vector.scalar_tensor_tensor(hidT[:, :, g, 0:NCMP], hidu[:, :, c], 1.0, hidg[:, :, c], ALU.add, ALU.mult)
            ins.then_inc(hidT_done, 1)
            have_low(dve, CH_M0B, 0)
            dve.wait_ge(kc_full, 1)
            nc.vector.tensor_scalar(kcT[:, 0:16], bank[4][:, 0:16], 0.5, None, ALU.mult)
            for r in range(REP):
                ins = nc.vector.tensor_scalar(vbd[32 * r:32 * r + 32, :, r * HD:(r + 1) * HD],
                                              bank[4][32 * r:32 * r + 32, 64:64 + KVG * HD].rearrange("p (g d) -> p g d", g=KVG),
                                              0.5, None, ALU.mult)
            ins.then_inc(kc_done, 1)
            dve.wait_ge(merge_done, N_MG + 1)
            dve.wait_ge(yp_full, N_MG)
            step(nc.vector.memset(pc, 0.0))
            have_low(dve, CH_M0B, 1)
            have_low(dve, CH_NSA, 0)
            dve.wait_ge(sc_full, 1)
            step(nc.vector.tensor_tensor(pcx[:], bank[6][:].rearrange("p (a c) -> p a c", c=32)[:, :, 0:16], cbias, ALU.add))
            step(nc.vector.tensor_reduce(pcs[:, 0], pcx[:], AX.X, ALU.max))
            nc.vector.tensor_tensor(pcx[:], pcx[:], pcs[:, 0].unsqueeze(2).to_broadcast([P, NT * HEADS, 16]),
                                    ALU.subtract).then_inc(csub_done, 1)
            dve.wait_ge(cexp_done, 1)
            step(nc.vector.tensor_reduce(pcs[:, 1], pcx[:], AX.X, ALU.add))
            step(nc.vector.reciprocal(pcs[:, 2], pcs[:, 1]))
            step(nc.vector.tensor_tensor(pcs[:, 3].rearrange("p (t a) -> p t a", t=NT), pcs[:, 2].rearrange("p (t a) -> p t a", t=NT),
                                         gts[:].rearrange("p t (a c) -> p t a c", c=3)[:, :, :, 0], ALU.mult))
            step(nc.vector.tensor_tensor(pcx[:], pcx[:], pcs[:, 3].unsqueeze(2).to_broadcast([P, NT * HEADS, 16]), ALU.mult))
            for t in range(NT):
                a = slice(t * HEADS, (t + 1) * HEADS)
                ins = nc.vector.tensor_tensor(pc[:, a, 0:16], pcx[:, a], cmask[:, t].unsqueeze(1).to_broadcast([P, HEADS, 16]), ALU.mult)
            ins.then_inc(pc_done, 1)
            have_low(dve, CH_NSA, 1)
            have_low(dve, CH_WO, 0)
            dve.wait_ge(oc_full, 1)
            dve.wait_ge(o_read, N_MG + 1)
            for t in range(NT):
                nc.vector.tensor_tensor(oacc[:, t], oacc[:, t], bank[4 + t][:], ALU.add).then_inc(o_done, 1)
            for n in range(2):
                dve.wait_ge(ohi_done, n + 1)
                nc.vector.scalar_tensor_tensor(flat(olo[:, 2 * n:2 * n + 2]).bitcast(F32R), bank[6 + n][:], 0.5,
                                               flat(ohi[:, 2 * n:2 * n + 2]), ALU.mult, ALU.subtract).then_inc(oT_done, 1)
            have_low(dve, CH_WO, 1)

            def merge(n):
                dve.wait_ge(m0_done, n + 1)
                dve.wait_ge(yn_full, n + 1)
                step(nc.vector.scalar_tensor_tensor(gates[n], gates[n], 1.0, bank[(4, 5, 0, 1)[n]][:], ALU.add, ALU.mult))
                m = flat(merged[:, 2 * n:2 * n + 2])
                nc.vector.tensor_tensor(m, m, gates[n], ALU.add).then_inc(merged_done, 1)

            def merged_low(n):
                m = flat(merged[:, 2 * n:2 * n + 2])
                dve.wait_ge(mhi_done, n + 1)
                nc.vector.tensor_tensor(flat(mlo[:, 2 * n:2 * n + 2]).bitcast(F32R), m, flat(mhi[n // 2][:, 2 * (n % 2):2 * (n % 2) + 2]),
                                        ALU.subtract).then_inc(mlo_done, 1)

            for n in range(4):
                merge(n)
                if n > 0:
                    merged_low(n - 1)
            merged_low(3)
            have_low(dve, CH_WO + 1, 0)
            have_low(dve, CH_WO + 1, 1)
            for n in range(4):
                t, half = n % 2, n // 2
                dve.wait_ge(wo_full, n + 1)
                hv = h[:, t, half * 512:(half + 1) * 512]
                nc.vector.tensor_tensor(hv, hv, bank[(2, 3, 6, 7)[n]][:], ALU.add).then_inc(h_done, 1)

            dve.wait_ge(rstd2_done, 1)
            for t in range(NT):
                nc.vector.tensor_scalar(diag[:, t], ident, stat[:, 8 + t:9 + t], None, ALU.mult).then_inc(diag_done, 1)
            for k in (2, 3, 6, 7):
                dve.wait_ge(xn2T_full, k // 2 + 1)
                nc.vector.tensor_scalar(xn2T[:, k], bank[4 + k // 2][:, (k % 2) * T:(k % 2 + 1) * T],
                                        prm[:, PR_G2 + k:PR_G2 + k + 1], None, ALU.mult).then_inc(xn2T_done, 1)
            dve.wait_ge(vec_in, 16)
            for t in range(NT):
                dve.wait_ge(h_done, 4)
                nc.vector.scalar_tensor_tensor(xn2[:, t], h[:, t], stat[:, 8 + t:9 + t], g2b, ALU.mult, ALU.mult).then_inc(xn2_done, 1)
            dve.wait_ge(logit_full, 1)
            dve.wait_ge(route_in, 32)
            step(nc.vector.tensor_tensor(lg, bank[0][:, 0:NT * (GROUPS + NE)].rearrange("p (t e) -> p t e", t=NT),
                                         rb[:].unsqueeze(1).to_broadcast([P, NT, GROUPS + NE]), ALU.add))
            G = lg[:, :, 0:GROUPS]
            E4 = lg[:, :, GROUPS:].rearrange("p t (g e) -> p t g e", g=GROUPS)

            def one(row, c=0):
                return rt[:, row, :, c:c + 1]

            def wide(ap, n):
                return ap.to_broadcast([P, NT, n])

            step(nc.vector.tensor_reduce(one(2), G, AX.X, ALU.max))
            nc.vector.tensor_tensor(rt[:, 0, :, 0:GROUPS], G, wide(one(2), GROUPS), ALU.subtract).then_inc(gsub_done, 1)

            def first_largest(out_row, vals, top, n, scratch):
                v = rt[:, scratch, :, 0:n]
                step(nc.vector.tensor_tensor(v, vals, wide(top, n), ALU.is_equal))
                step(nc.vector.tensor_tensor(v, v, rk8[:, 0:n].unsqueeze(1).to_broadcast([P, NT, n]), ALU.mult))
                step(nc.vector.tensor_reduce(one(scratch + 1), v, AX.X, ALU.max))
                step(nc.vector.tensor_tensor(rt[:, out_row, :, 0:n], v, wide(one(scratch + 1), n), ALU.is_equal))

            first_largest(3, G, one(2), GROUPS, 4)
            et = etmp.rearrange("p t (g e) -> p t g e", g=GROUPS)
            for t in range(NT):
                ins = nc.vector.tensor_tensor(et[:, t], E4[:, t], rt[:, 3, t, 0:GROUPS].unsqueeze(2).to_broadcast([P, GROUPS, PER_GROUP]), ALU.mult)
            step(ins)
            step(nc.vector.tensor_reduce(rt[:, 6], etmp.rearrange("p t (g e) -> p t e g", g=GROUPS), AX.X, ALU.add))
            step(nc.vector.tensor_reduce(one(7), rt[:, 6], AX.X, ALU.max))
            first_largest(10, rt[:, 6], one(7), PER_GROUP, 4)
            step(nc.vector.scalar_tensor_tensor(rt[:, 11], rt[:, 10], NEG, rt[:, 6], ALU.mult, ALU.add))
            step(nc.vector.tensor_reduce(one(12), rt[:, 11], AX.X, ALU.max))
            first_largest(13, rt[:, 11], one(12), PER_GROUP, 4)
            nc.vector.tensor_tensor(one(8), one(12), one(7), ALU.subtract).then_inc(tsub_done, 1)
            step(nc.vector.tensor_tensor(rt[:, 14], rt[:, 10], rt[:, 13], ALU.add))
            for t in range(NT):
                ins = nc.vector.tensor_tensor(mask[:, t].rearrange("p (g e) -> p g e", g=GROUPS),
                                              rt[:, 3, t, 0:GROUPS].unsqueeze(2).to_broadcast([P, GROUPS, PER_GROUP]),
                                              rt[:, 14, t].unsqueeze(1).to_broadcast([P, GROUPS, PER_GROUP]), ALU.mult)
            ins.then_inc(mask_done, 1)
            dve.wait_ge(gexp_done, 1)
            step(nc.vector.tensor_reduce(one(4), rt[:, 1, :, 0:GROUPS], AX.X, ALU.add))
            dve.wait_ge(texp_done, 1)
            step(nc.vector.tensor_scalar(one(5), one(9), 1.0, None, ALU.add))
            step(nc.vector.tensor_tensor(one(4), one(4), one(5), ALU.mult))
            step(nc.vector.reciprocal(one(5), one(4)))
            dve.wait_ge(count_full, 1)
            step(nc.vector.tensor_reduce(pcnt[:, 0:1], bank[2][:, 0:NE], AX.X, ALU.max))
            step(nc.vector.tensor_scalar(pcnt[:, 8:8 + MAXPASS], steps_of_cap, pcnt[:, 0:1], None, ALU.is_lt))
            step(nc.vector.tensor_reduce(pcnt[:, 1:2], pcnt[:, 8:8 + MAXPASS], AX.X, ALU.add))
            nc.vector.tensor_copy(npass[:], pcnt[:, 1:2]).then_inc(passes_done, 1)
            step(nc.vector.tensor_tensor(one(9), one(9), one(5), ALU.mult))
            nc.vector.tensor_tensor(rt[:, 10], rt[:, 10], wide(one(5), PER_GROUP), ALU.mult)
            step(nc.vector.tensor_tensor(rt[:, 13], rt[:, 13], wide(one(9), PER_GROUP), ALU.mult))
            step(nc.vector.tensor_tensor(rt[:, 10], rt[:, 10], rt[:, 13], ALU.add))
            for t in range(NT):
                ins = nc.vector.tensor_tensor(comb[:, t].rearrange("p (g e) -> p g e", g=GROUPS),
                                              rt[:, 3, t, 0:GROUPS].unsqueeze(2).to_broadcast([P, GROUPS, PER_GROUP]),
                                              rt[:, 10, t].unsqueeze(1).to_broadcast([P, GROUPS, PER_GROUP]), ALU.mult)
            step(ins)
            dve.wait_ge(rank_full, 1)
            step(nc.vector.scalar_tensor_tensor(rank, bank[1][:, 0:NT * NE].rearrange("p (t e) -> p t e", t=NT), 1.0, mask, ALU.add, ALU.mult))
            dve.wait_ge(passes_done, 1)
            passes = dve.value_load(npass[0:1, 0:1], min_val=1, max_val=MAXPASS)
            with dve.Fori(0, passes) as rnd:
                with dve.Fori(0, NB) as bb:
                    b = rnd * NB + bb
                    dve.wait_ge(xg_full, b * 2 + 1)
                    for t in range(NT):
                        ins = nc.vector.tensor_tensor(sel[:, t], iota.unsqueeze(1).to_broadcast([P, EB, CAP]),
                                                      rank[:, t, bass.ds(bb * EB, EB)].unsqueeze(2).to_broadcast([P, EB, CAP]),
                                                      ALU.is_equal)
                    ins.then_inc(sel_step, 1)
                    dve.wait_ge(sel_step, b + 1)
                    for t in range(NT):
                        ins = nc.vector.tensor_tensor(selw[:, t], sel[:, t],
                                                      comb[:, t, bass.ds(bb * EB, EB)].unsqueeze(2).to_broadcast([P, EB, CAP]),
                                                      ALU.mult)
                    ins.then_inc(sel_done, 1)
                    dve.wait_ge(xg_full, b * 2 + 2 + 1)
                    nc.vector.tensor_copy(flat(xgT[:, 4:8]), bank[3][:]).then_inc(xg_done, 1)
                    dve.wait_ge(cmb_full, b + 1)
                    nc.vector.tensor_copy(cmbT, bank[1][:, 0:T]).then_inc(cmb_done, 1)
                    dve.wait_ge(silu_done, b + 1)
                    nc.vector.tensor_tensor(hN, sl1, bank[0][:, HID:2 * HID], ALU.mult).then_inc(hn_done, 1)
                    for half in range(2):
                        for t in range(NT):
                            dve.wait_ge(comb_done, b * 4 + (2 * half + t + 1))
                            hv = h[:, t, half * 512:(half + 1) * 512]
                            nc.vector.tensor_tensor(hv, hv, bank[6 + t][:], ALU.add).then_inc(add_done, 1)
                nc.vector.tensor_scalar(rank, rank, float(CAP), None, ALU.subtract).then_inc(rank_done, 1)
                dve.wait_ge(rank_done, rnd + 1)
            dve.wait_ge(vec_in, 32)
            for n in range(4):
                t, half = n % 2, n // 2
                c = slice(half * 512, (half + 1) * 512)
                dve.wait_ge(add_done, passes * (4 * NB) + n)
                ins = nc.vector.tensor_tensor(fin[:, t, c], h[:, t, c], g2b[:, c], ALU.mult)
            ins.then_inc(gained, 1)
            dve.wait_ge(rstd3_done, 1)
            dve.wait_ge(gained, 1)
            nc.vector.tensor_scalar(fin[:, 0], fin[:, 0], stat[:, 16:17], None, ALU.mult).then_inc(dve_fin, 1)

        @block.tensor
        def _(pe):
            mm = nc.tensor.matmul
            for s1 in (s_full, pT_full, pv_full, xg_full):
                pe.sem_inc(s1, 1)

            def turned(banks, full):
                for k in range(KT):
                    for t in range(NT):
                        ins = mm(bank[banks + k // 2][:, (k % 2) * T + t * P:(k % 2) * T + (t + 1) * P], h[:, t, k * P:(k + 1) * P],
                                 diag[:, t], start=True, stop=True)
                    if k % 2:
                        ins.then_inc(full, 1)

            pe.wait_ge(diag_done, NT)
            turned(0, xT_full)

            def product(dst, whi, wlo, ahi, alo, start, stop):
                mm(dst, whi, ahi, start=start, stop=False)
                mm(dst, whi, alo, start=False, stop=False)
                return mm(dst, wlo, ahi, start=False, stop=stop)

            def parts(n, half, c):
                return [w[:, 0:floats(n)].bitcast(F32R).rearrange("p (k c) -> p k c", c=c) for w in (high(n, half), low(n, half))]

            def split(n, half, more=0):
                pe.wait_ge(split_done, more * 4 + 2 * SPLITS.index(n) + half + 1)

            XH, XL = xhi[:].bitcast(F32R), xlo[:].bitcast(F32R)

            def channels(dst, w, c0, k_tiles=KT, ahi=XH, alo=XL):
                for k in range(k_tiles):
                    ins = product(dst, w[0][:, k, c0:c0 + P], w[1][:, k, c0:c0 + P], ahi[:, k], alo[:, k], k == 0, k == k_tiles - 1)
                return ins

            def pair(dst, n, half, full, more=0):
                split(n, half, more)
                for a in range(2):
                    ins = channels(dst[:, a * T:(a + 1) * T], parts(n, half, 2 * P), a * P)
                ins.then_inc(full, 1)

            split(CH_Q, 0)
            w = parts(CH_Q, 0, 2 * P)
            for a in range(2):
                for k in range(KT):
                    if a == 0:
                        pe.wait_ge(xnT_done, k + 1)
                    ins = product(bank[4][:, a * T:(a + 1) * T], w[0][:, k, a * P:(a + 1) * P], w[1][:, k, a * P:(a + 1) * P],
                                  XH[:, k], XL[:, k], k == 0, k == KT - 1)
            ins.then_inc(q_full, 1)
            pair(bank[5], CH_Q, 1, q_full)
            pair(bank[0], CH_KV, 0, kvc_full)
            pair(bank[1], CH_KV, 1, kk_full)
            for half in range(2):
                split(CH_VG, half)
            for t in range(NT):
                for k in range(KT):
                    w = parts(CH_VG, k // 4, VGC)
                    cols = slice(t * P, (t + 1) * P)
                    mm(bank[2 + t][:, 0:VGC], XH[:, k, cols], w[0][:, k % 4], start=(k == 0), stop=False)
                    mm(bank[2 + t][:, 0:VGC], XH[:, k, cols], w[1][:, k % 4], start=False, stop=False)
                    ins = mm(bank[2 + t][:, 0:VGC], XL[:, k, cols], w[0][:, k % 4], start=False, stop=(k == KT - 1))
            ins.then_inc(vg_full, 1)

            def compress(a):
                for half in range(2):
                    landed(pe, (CH_CK, CH_CV)[a], half)
                    w = raw((CH_CK, CH_CV)[a], half).rearrange("p (j c) -> p j c", j=8)
                    for j in range(8):
                        r = slice(32 * (j % 4), 32 * (j % 4) + 32)
                        ins = mm(bank[6 + a][r, 0:2 * P], fpe[:, a, 8 * half + j], w[:, j],
                                 start=(half == 0 and j < 4), stop=(half == 1 and j >= 4))
                    ins.then_inc(hidp_full, 1)

            pe.wait_ge(flat_done, 1)
            compress(0)
            pe.wait_ge(kvc_done, 1)
            pair(bank[0], CH_UH, 0, u_full)
            pe.wait_ge(kk_done, 1)
            pair(bank[1], CH_UH, 1, h_full)
            compress(1)
            pe.wait_ge(vg_done, 1)
            pair(bank[2], CH_BC, 0, b_full)
            pair(bank[3], CH_BC, 1, c_full)
            pe.wait_ge(con_in, 16)
            pe.wait_ge(hidp_done, 2)
            for a in range(2):
                for ht in range(2):
                    c = 32 * (2 * a + ht)
                    ins = mm(bank[7][:, c:c + 32], hidp[:, a, ht * P:(ht + 1) * P], fold, start=True, stop=True)
            ins.then_inc(hid_full, 1)
            pe.wait_ge(pooled_done, 1)
            pe.wait_ge(small_in, 32)
            for a in range(2):
                ins = mm(bank[6][:, a * T:(a + 1) * T], wg[:, a], pooled[:, a], start=True, stop=True)
            ins.then_inc(mix_full, 1)
            pe.wait_ge(q_done, 2)
            pe.wait_ge(u_done, 1)
            pe.wait_ge(ch_done, 1)

            with pe.Fori(0, N_MG // 2) as i2:
                for s in range(2):
                    i = i2 * 2 + s
                    n = CH_MG + s
                    wp = proj(s).rearrange("p (a k c) -> p a k c", a=2, k=2)

                    def project(dst, w, src):
                        for a in range(2):
                            for k in range(2):
                                ins = mm(dst[:, a * T:(a + 1) * T], w[:, k, a * P:(a + 1) * P], src[:, k], start=(k == 0), stop=(k == 1))
                        return ins

                    def s_unit(u):
                        g, b = u % 2, u // 2
                        rows = slice(g * HD, (g + 1) * HD)
                        if u == 0:
                            pe.wait_ge(qcur_done, i + 1)
                        pe.wait_ge(s_max, i * 4 + max(u - 1, 0) + 1)
                        for t in range(NT):
                            ins = mm(bank[4 + u % 2][:, t * P:(t + 1) * P + t * P],
                                     qcur[rows, t * P:(t + 1) * P],
                                     kT[rows, b, 0:(t + 1) * P], start=True, stop=True)
                        ins.then_inc(s_full, 1)

                    def t_unit(u):
                        pe.wait_ge(p_done, i * 4 + (u + 1) + 1)
                        pe.wait_ge(pT_done, i * 4 + u + 1)
                        if u == 0:
                            pe.wait_ge(poolT_done, 1)
                        for c in range(3):
                            ins = nc.tensor.transpose(bank[6][:, c * P:(c + 1) * P], sP[:, u % 2, c * P:(c + 1) * P], ident)
                        ins.then_inc(pT_full, 1)

                    def pv_unit(u):
                        g, b = u % 2, u // 2
                        cols = slice(g * HD, (g + 1) * HD)
                        pe.wait_ge(pT_done, i * 4 + (u + 1) + 1)
                        if u == 0:
                            pe.wait_ge(hid_done, 1)
                            pe.wait_ge(o_read, i + 1)
                        c = 2 * HD * u
                        mm(bank[7][:, c:c + HD], sPT[:, u % 2, 0:P], vN[:, b, 0, cols], start=True, stop=True)
                        mm(bank[7][:, c + HD:c + 2 * HD], sPT[:, u % 2, P:2 * P], vN[:, b, 0, cols], start=True, stop=False)
                        mm(bank[7][:, c + HD:c + 2 * HD], sPT[:, u % 2, 2 * P:3 * P], vN[:, b, 1, cols],
                           start=False, stop=True).then_inc(pv_full, 1)

                    s_unit(0)
                    s_unit(1)
                    pe.wait_ge(ga_done, i + 1)
                    pair(bank[0], n, 0, ga_full, i2)
                    t_unit(0)
                    s_unit(2)
                    pe.wait_ge(gb_done, i + 1)
                    split(n, 1, i2)
                    w = parts(n, 1, 2 * P)
                    channels(bank[1][:, 0:T], w, 0)
                    pv_unit(0)
                    t_unit(1)
                    s_unit(3)
                    channels(bank[1][:, T:2 * T], w, P).then_inc(gb_full, 1)
                    pv_unit(1)
                    t_unit(2)
                    pe.wait_ge(merge_done, i + 1)
                    pe.wait_ge(proj_in[s], i2 * 16 + 16)
                    pe.wait_ge(conv_done, 1)
                    project(bank[2], wp[:, 0], poolT).then_inc(yp_full, 1)
                    pv_unit(2)
                    t_unit(3)
                    project(bank[3], wp[:, 1], convT).then_inc(yc_full, 1)
                    pv_unit(3)

            pe.wait_ge(ga_done, N_MG + 1)
            pair(bank[0], CH_M0A, 0, m0_full)
            pe.wait_ge(hidT_done, 1)
            for g in range(KVG):
                for ht in range(2):
                    mm(bank[4][g * HD:(g + 1) * HD, 0:16], cw2[:, ht], hidT[:, ht, g, 0:16], start=(ht == 0), stop=(ht == 1))
            for g in range(KVG):
                for r in range(REP):
                    for ht in range(2):
                        ins = mm(bank[4][32 * r:32 * r + 32, 64 + g * HD:64 + (g + 1) * HD], hidT[:, 2 + ht, g], cw2[:, 2 + ht],
                                 start=(ht == 0), stop=(ht == 1))
            ins.then_inc(kc_full, 1)
            pe.wait_ge(gb_done, N_MG + 1)
            pair(bank[1], CH_M0A, 1, m0_full)
            pe.wait_ge(kc_done, 1)
            pe.wait_ge(o_read, N_MG + 1)
            for g in range(KVG):
                rows = slice(g * HD, (g + 1) * HD)
                for r in range(REP):
                    ins = mm(bank[(5, 7)[g]][32 * r:32 * r + 32, 0:T], kcT[rows], qT[rows, r], start=True, stop=True)
            ins.then_inc(scT_full, 1)
            pe.wait_ge(merge_done, N_MG + 1)
            pair(bank[2], CH_M0B, 0, m0_full)
            pe.wait_ge(scT_done, 1)
            pe.wait_ge(pT_done, N_MG * 4 + 1)
            for t in range(NT):
                for g in range(KVG):
                    ins = nc.tensor.transpose(bank[6][:, (2 * t + g) * P:(2 * t + g + 1) * P], scT[:, g * T + t * P:g * T + (t + 1) * P], ident)
            ins.then_inc(sc_full, 1)
            split(CH_M0B, 1)
            w = parts(CH_M0B, 1, 2 * P)
            channels(bank[3][:, 0:T], w, 0)
            pe.wait_ge(pc_done, 1)
            for t in range(NT):
                for g in range(KVG):
                    src = pc[:, t * HEADS + g * REP:t * HEADS + (g + 1) * REP].rearrange("p a c -> p (a c)")
                    ins = nc.tensor.transpose(bank[7][:, (2 * t + g) * P:(2 * t + g + 1) * P], src, ident)
            ins.then_inc(pcT_full, 1)
            channels(bank[3][:, T:2 * T], w, P).then_inc(m0_full, 1)
            pe.wait_ge(pcT_done, 1)
            for t in range(NT):
                for g in range(KVG):
                    ins = mm(bank[4 + t][:, g * 256:(g + 1) * 256], pcT[:, 2 * t + g], vbd[:, g], start=True, stop=True)
            ins.then_inc(oc_full, 1)
            pe.wait_ge(o_done, 2)
            for k in range(4):
                for t in range(NT):
                    ins = nc.tensor.transpose(bank[6 + k // 2][:, (k % 2) * T + t * P:(k % 2) * T + (t + 1) * P],
                                              oacc[:, t, k * P:(k + 1) * P], ident)
                if k % 2:
                    ins.then_inc(oT_full, 1)
            pe.wait_ge(oT_done, 2)

            def nsa(n):
                split(CH_NSA, n // 2)
                for a in range(2):
                    ins = channels(bank[(4, 5, 0, 1)[n]][:, a * T:(a + 1) * T], parts(CH_NSA, n // 2, 4 * P), (2 * (n % 2) + a) * P, 4,
                                   ohi.bitcast(F32R), olo.bitcast(F32R))
                ins.then_inc(yn_full, 1)

            for n in range(4):
                if n > 1:
                    pe.wait_ge(m0_done, n - 1)
                nsa(n)

            def output(n, k):
                t, half = n % 2, n // 2
                whi, wlo = parts(CH_WO + k // 4, k // 2 % 2, D)
                cols, wc = slice(t * P, (t + 1) * P), slice(half * 512, (half + 1) * 512)
                mh, ml = mhi[k // 4][:, k % 4].bitcast(F32R), mlo[:, k].bitcast(F32R)
                dst = bank[(2, 3, 6, 7)[n]][:]
                mm(dst, mh[:, cols], whi[:, k % 2, wc], start=(k == 0), stop=False)
                mm(dst, mh[:, cols], wlo[:, k % 2, wc], start=False, stop=False)
                return mm(dst, ml[:, cols], whi[:, k % 2, wc], start=False, stop=(k == KT - 1))

            pe.wait_ge(m0_done, 4)
            for j in range(2):
                split(CH_WO, j)
                pe.wait_ge(mlo_done, 2)
                for n in range(4):
                    for k in (2 * j, 2 * j + 1):
                        ins = output(n, k)
                ins.then_inc(wo_used, 1)
            split(CH_WO + 1, 1)
            pe.wait_ge(mlo_done, 4)
            for n in range(4):
                for k in range(4, KT):
                    ins = output(n, k)
                ins.then_inc(wo_full, 1)
            pe.wait_ge(diag_done, 2 * NT)
            turned(4, xn2T_full)
            pe.wait_ge(xn2T_done, KT)
            pe.wait_ge(route_in, 32)
            for t in range(NT):
                c = t * (GROUPS + NE)
                for k in range(KT):
                    ins = mm(bank[0][:, c:c + GROUPS + NE], xn2T[:, k, t * P:(t + 1) * P], rw[:, k], start=(k == 0), stop=(k == KT - 1))
            ins.then_inc(logit_full, 1)
            pe.wait_ge(mask_done, 1)
            for t in range(NT):
                ins = mm(bank[2][:, 0:NE], ones, mask[:, t], start=(t == 0), stop=(t == NT - 1))
            ins.then_inc(count_full, 1)
            mm(bank[1][:, 0:NE], tri, mask[:, 0], start=True, stop=True)
            mm(bank[1][:, NE:2 * NE], tri, mask[:, 1], start=True, stop=False)
            mm(bank[1][:, NE:2 * NE], ones, mask[:, 0], start=False, stop=True).then_inc(rank_full, 1)

            pe.wait_ge(passes_done, 1)
            passes = pe.value_load(npass[0:1, 0:1], min_val=1, max_val=MAXPASS)

            def expert(j, q, e):
                return ring[:, (j * NQ + q) % SLOTS, e * 512:(e + 1) * 512]

            def have_expert(j, q):
                c = j * NQ + q
                pe.wait_ge(expert_in[c % SLOTS], bb * (16 * ROUND * NQ // SLOTS) + 16 * (c // SLOTS + 1))

            with pe.Fori(0, passes * (NB // ROUND)) as bb:
                for j in range(ROUND):
                    b = bb * ROUND + j
                    pe.wait_ge(sel_step, b + 1)
                    for half in range(2):
                        for k in range(4):
                            for t in range(NT):
                                ins = mm(bank[2 + half][:, k * P:(k + 1) * P], xn2[:, t, (4 * half + k) * P:(4 * half + k + 1) * P],
                                         flat(sel[:, t]), start=(t == 0), stop=(t == NT - 1))
                        ins.then_inc(xg_full, 1)
                    pe.wait_ge(sel_done, b + 1)
                    pe.wait_ge(hT_done, b + 1)
                    for t in range(NT):
                        ins = nc.tensor.transpose(bank[1][:, t * P:(t + 1) * P], flat(selw[:, t]), ident)
                    ins.then_inc(cmb_full, 1)
                    pe.wait_ge(xg_done, b * 2 + 2)
                    pe.wait_ge(hn_done, b + 1)
                    for q in range(NQ1):
                        have_expert(j, q)
                        for e in range(EB):
                            ins = mm(bank[0][CAP * e:CAP * (e + 1)], xgT[:, q, CAP * e:CAP * (e + 1)],
                                     expert(j, q, e), start=(q == 0), stop=(q == NQ1 - 1))
                        if q == NQ1 - 1:
                            ins.then_inc(hid1_full, 1)
                        else:
                            ins.then_inc(expert_used, 1)
                    pe.wait_ge(hn_done, b + 2)
                    pe.wait_ge(cmb_done, b + 1)
                    pe.sem_inc(expert_used, 1)
                    for k in range(HT):
                        ins = nc.tensor.transpose(bank[1][:, k * P:(k + 1) * P], hN[:, k * P:(k + 1) * P], ident)
                    ins.then_inc(hT_full, 1)
                    pe.wait_ge(hT_done, b + 2)
                    for half in range(2):
                        pe.wait_ge(yn_done, b * 2 + half + 1)
                        for ht in range(HT):
                            q = NQ1 + HT * half + ht
                            have_expert(j, q)
                            for e in range(EB):
                                ins = mm(bank[4 + half][CAP * e:CAP * (e + 1)], hT[:, ht, CAP * e:CAP * (e + 1)],
                                         expert(j, q, e), start=(ht == 0), stop=(ht == HT - 1))
                            if ht < HT - 1:
                                ins.then_inc(expert_used, 1)
                        ins.then_inc(y_full, 1)
                        pe.wait_ge(yn_done, b * 2 + (half + 1) + 1)
                        pe.sem_inc(expert_used, 1)
                        for t in range(NT):
                            pe.wait_ge(add_done, b * 4 + max(2 * half + t - 1, 0) + 3)
                            mm(bank[6 + t][:], cmbT[:, t * P:(t + 1) * P], yN[:, half * 512:(half + 1) * 512],
                               start=True, stop=True).then_inc(comb_done, 1)


def constants():
    import numpy as np
    c = np.zeros((P, K_N), np.float32)
    q = np.arange(P)[:, None]
    far = np.float32(-1e34)
    c[:, K_ID:K_ID + P] = np.eye(P)
    key = np.arange(P)[None, :]
    c[:, K_DIST:K_DIST + P] = np.where(key <= q, key - q, far)
    key = np.arange(2 * P)[None, :]
    c[:, K_DIST + P:K_DIST + 3 * P] = np.where(key <= q + P, key - (q + P), far)
    c[:, K_TRI:K_TRI + P] = q < np.arange(P)[None, :]
    c[:, K_ONE:K_ONE + P] = 1.0
    c[:, K_IOTA:K_IOTA + CAP] = np.arange(1, CAP + 1)
    slopes = 2.0 ** (-8.0 * np.arange(1, HEADS + 1) / HEADS)
    for t in range(NT):
        d = t * P + q - (np.arange(16)[None, :] * CMP_STRIDE + CMP_LEN - 1)
        ok = (d >= 0) & (np.arange(16)[None, :] < NCMP)
        c[:, K_CM + t * 16:K_CM + (t + 1) * 16] = ok
        for hd in range(HEADS):
            o = K_CB + (t * HEADS + hd) * 16
            c[:, o:o + 16] = np.where(ok, -slopes[hd] * d, far)
    tt = np.arange(T)
    for a in range(2):
        for g in range(2):
            c[g * HD:(g + 1) * HD, K_IC + a * T:K_IC + (a + 1) * T] = 1.0 / np.minimum(tt + 1, POOL_WINDOWS[2 * a + g])
    c[:, K_SL:K_SL + HEADS] = slopes
    c[:, K_FOLD:K_FOLD + 32] = q % 32 == np.arange(32)[None, :]
    c[:, K_CAP:K_CAP + MAXPASS] = CAP * np.arange(MAXPASS)
    c[:, K_RK:K_RK + PER_GROUP] = PER_GROUP - np.arange(PER_GROUP)
    return c


def kernel(**inputs):
    import numpy as np
    import concourse.bacc as bacc
    from concourse.bass_utils import run_bass_kernel_spmd as run

    a = {k: np.asarray(v) for k, v in inputs.items()}

    def tiles(w):
        return w.reshape(-1, P, w.shape[1]).transpose(1, 0, 2).reshape(P, -1)

    w_in = a["w_in"][0]
    o_kv, o_gate = HEADS * HD, HEADS * HD + 6 * KVG * HD
    o_u = o_gate + GATES
    o_m = o_u + 4 * 256
    wq = w_in[:, 0:o_kv].reshape(D, KVG, REP, HD).transpose(0, 2, 1, 3).reshape(D, HEADS * HD)
    front = np.zeros((N_CHUNKS, 2, P, SLOT), np.float32)

    def put(n, w, by_columns=True):
        for half, part in enumerate(np.split(w, 2, axis=1 if by_columns else 0)):
            part = tiles(part)
            front[n, half, :, 0:part.shape[1]] = part

    def gate(i, c0, n):
        return w_in[:, o_m + i * D + c0:o_m + i * D + c0 + n]

    k_cmp, v_cmp, k_slc, v_slc, k_win, v_win = (w_in[:, o_kv + P * i:o_kv + P * (i + 1)] for i in range(6))
    put(CH_Q, wq)
    put(CH_KV, np.concatenate([k_cmp, v_cmp, k_slc, k_win], axis=1))
    put(CH_VG, np.concatenate([v_slc, v_win, w_in[:, o_gate:o_u]], axis=1), False)
    put(CH_UH, w_in[:, o_u:o_u + 512])
    put(CH_BC, w_in[:, o_u + 512:o_m])
    put(CH_CK, a["cmp_w1"][0, 0], False)
    put(CH_CV, a["cmp_w1"][0, 1], False)
    for i in range(N_MG):
        put(CH_MG + i, np.concatenate([gate(1, 256 * i, 256), gate(2, 256 * i, 256)], axis=1))
    projs = np.stack([np.concatenate([tiles(a[w][0][:, 256 * i:256 * i + 256]) for w in ("w_pool_proj", "w_conv_proj")], axis=1)
                      for i in range(N_MG)])
    put(CH_M0A, gate(0, 0, 512))
    put(CH_M0B, gate(0, 512, 512))
    put(CH_NSA, a["w_nsa_proj"][0])
    for i in range(2):
        put(CH_WO + i, a["w_o"][0][512 * i:512 * i + 512], False)

    params = np.concatenate([
        a["norm1_g"][0].reshape(KT, P), a["pool_scale"][0].reshape(2, P), a["conv_w"][0].reshape(2 * CONV_K, P),
        a["cmp_pe"][0].reshape(CMP_LEN, P), a["norm2_g"][0].reshape(KT, P)]).T
    wgrp = np.zeros((P, 2, P), np.float32)
    for g in range(4):
        o = (g % 2) * HD
        wgrp[o:o + HD, g // 2, o:o + HD] = a["pool_w"][0, g]

    w1 = a["expert_w1"][0].reshape(NB, EB, NQ1, P, HID)
    w3 = a["expert_w3"][0].reshape(NB, EB, NQ1, P, HID)
    w2 = a["expert_w2"][0].reshape(NB, EB, HT, P, 2, 512)
    experts = np.concatenate([
        np.concatenate([w1, w3], axis=4).transpose(0, 2, 3, 1, 4).reshape(NB, NQ1, P, ECHUNK),
        w2.transpose(0, 4, 2, 3, 1, 5).reshape(NB, NQ2, P, ECHUNK)], axis=1)

    arrays = {
        "x": a["x"][0],
        "params": params,
        "consts": constants(),
        "front": front,
        "projs": projs,
        "small": tiles(a["cmp_w2"][0].reshape(2 * HID, HD)),
        "wgrp": wgrp.reshape(P, 2 * P),
        "vecs": np.stack([a["norm2_g"][0], a["final_norm_g"]]),
        "routerw": tiles(np.concatenate([a["router_group_w"][0], a["router_expert_w"][0]], axis=1)),
        "routerb": np.concatenate([a["router_group_b"][0], a["router_expert_b"][0]])[None],
        "experts": experts,
    }
    nc = bacc.Bacc("TRN2", target_bir_lowering=False, num_devices=1)
    args, feed = [], {}
    for name, v in arrays.items():
        feed[f"in_{name}"] = np.ascontiguousarray(v)
        args.append(nc.dram_tensor(f"in_{name}", v.shape, F32, kind="ExternalInput").ap())
    args.append(nc.dram_tensor("out_y", (T, D), F32, kind="ExternalOutput").ap())
    build(nc, *args)
    r = run(nc, [feed], core_ids=[0])
    return r.results[0]["out_y"].reshape(1, T, D)
```

```python
from contextlib import ExitStack

import concourse.bass as bass
from concourse import mybir

ALU = mybir.AluOpType
ACT = mybir.ActivationFunctionType
AX = mybir.AxisListType
F32 = mybir.dt.float32
F32R = mybir.dt.float32r
I32 = mybir.dt.int32

P = 128
D = 1024
T = 256
NT = T // P
KT = D // P
HD = 64
HEADS = 8
KVG = 2
REP = HEADS // KVG
CMP_LEN, CMP_STRIDE = 32, 16
NCMP = T // CMP_STRIDE - CMP_LEN // CMP_STRIDE + 1
POOL_WINDOWS = (2, 4, 8, 16)
PAD = 16
CONV_K = 3
GROUPS, PER_GROUP = 4, 8
NE = GROUPS * PER_GROUP
HID = D // 4
HT = HID // P
CAP = 32
EB = P // CAP
NB = NE // EB
EPS = 1e-6
NEG = -1e30
SLOT = 2048
SLOTS = 16
GATES = HEADS * 3
GELU_C = 0.7978845608028654

(CH_Q, CH_KV, CH_VG, CH_CK, CH_UH, CH_CV, CH_BC, CH_MG) = range(8)
N_MG = 4
CH_M0A = CH_MG + N_MG
CH_M0B = CH_M0A + 1
CH_NSA = CH_M0B + 1
CH_WO = CH_NSA + 1
N_CHUNKS = CH_WO + 2
VGC = 2 * P + GATES
PROJ = 2 * 2 * 2 * P
SPLITS = [n for n in range(N_CHUNKS) if n not in (CH_CK, CH_CV)]

SLOT_PROJ = 3
SET_C, SET_B, SET_A = 4, 8, 12
CHUNK_SET = {CH_Q: SET_A, CH_KV: SET_B, CH_VG: SET_C, CH_UH: SET_A, CH_BC: SET_C,
             CH_M0A: SET_B, CH_M0B: SET_C, CH_NSA: SET_A, CH_WO: SET_B, CH_WO + 1: SET_A}
for _i in range(N_MG):
    CHUNK_SET[CH_MG + _i] = (SET_B, SET_A)[_i % 2]

NQ1 = KT
NQ2 = 2 * HT
NQ = NQ1 + NQ2
ROUND = 4
ECHUNK = EB * 2 * HID
MAXPASS = T // CAP

PR_G1 = 0
PR_PS = PR_G1 + KT
PR_CW = PR_PS + 2
PR_PE = PR_CW + 2 * CONV_K
PR_G2 = PR_PE + CMP_LEN
PR_N = PR_G2 + KT

K_ID = 0
K_DIST = K_ID + P
K_CB = K_DIST + 3 * P
K_CM = K_CB + NT * HEADS * 16
K_IC = K_CM + NT * 16
K_TRI = K_IC + 2 * T
K_ONE = K_TRI + P
K_IOTA = K_ONE + P
K_SL = K_IOTA + CAP
K_RK = K_SL + HEADS
K_FOLD = K_RK + PER_GROUP
K_CAP = K_FOLD + 32
K_FOLD2 = K_CAP + MAXPASS
K_N = K_FOLD2 + GROUPS + NE


def build(nc, x, params, consts, front, projs, small, wgrp, vecs, routerw, routerb, experts, out):
    with ExitStack() as ctx:
        start = {}

        def sb(name, shape, dt=F32):
            start[name] = (nc.sbuf_base + 31) // 32 * 32
            return ctx.enter_context(nc.sbuf_tensor(name, shape, dt))

        def over(name, shape, base, at=0):
            return nc.alloc_sbuf_tensor_at(name, shape, F32, offset=start[base] + 4 * at)

        def sem(name):
            return ctx.enter_context(nc.semaphore(name))

        bank = [ctx.enter_context(nc.psum_tensor(f"bank{i}", [P, 512], F32)) for i in range(8)]

        h = sb("h", [P, NT, D])
        con = sb("con", [P, K_N])
        prm = sb("prm", [P, PR_N])
        ring = sb("ring", [P, SLOTS, SLOT])
        stat = sb("stat", [P, 64])
        part = {s: over(f"part{s}", [P, SLOT], "ring", s * SLOT) for s in range(SET_C, SLOTS)}
        xhi = sb("xhi", [P, KT, T])
        xlo = sb("xlo", [P, KT, T])
        merged = sb("merged", [P, KT, T])
        qT = sb("qT", [P, REP, T])
        kv = sb("kv", [P, 4 * T])
        gts = sb("gts", [P, NT, GATES])
        hidg = sb("hidg", [P, 4, 2 * NCMP])
        hidu = sb("hidu", [P, 4, 2 * NCMP])
        hidT = sb("hidT", [P, 4, KVG, 32])
        cw2 = sb("cw2", [P, 4, HD])
        kcT = sb("kcT", [P, 32])
        vbd = sb("vbd", [P, KVG, REP * HD])
        pcs = sb("pcs", [P, 4, NT * HEADS])
        att = sb("att", [P, 6 * 3 * P])
        qcur = sb("qcur", [P, T])
        npass = sb("npass", [P, 1], I32)
        pcnt = sb("pcnt", [P, 8 + MAXPASS])
        smx = sb("smx", [P, 2, NT])
        ssum = sb("ssum", [P, 4, NT])
        coef = sb("coef", [P, 4, NT])
        otmp = sb("otmp", [P, KVG * NT * HD])
        oT = sb("oT", [P, REP, T])
        gab = sb("gab", [P, 2, 512])
        wg = sb("wg", [P, 2, P])
        mixed = sb("mixed", [P, 2, 2, T])
        rw = sb("rw", [P, KT, HD])
        rb = sb("rb", [P, GROUPS + NE])

        kT = kv[:, 0:2 * T].rearrange("p (b t) -> p b t", b=2)
        vN = kv[:, 2 * T:4 * T].rearrange("p (b t c) -> p b t c", b=2, t=NT)
        ga, gb = gab[:, 0], gab[:, 1]
        poolT, convT = mixed[:, 0], mixed[:, 1]
        gates = (ga, gb, kv[:, 0:512], kv[:, 512:1024])
        sS = att[:, 0:6 * P].rearrange("p (b k) -> p b k", b=2)
        sP = att[:, 6 * P:12 * P].rearrange("p (b k) -> p b k", b=2)
        sPT = att[:, 12 * P:18 * P].rearrange("p (b k) -> p b k", b=2)
        PL = PAD + T
        upad = att[:, 0:2 * PL].rearrange("p (a t) -> p a t", a=2)
        s2 = att[:, 2 * PL:4 * PL].rearrange("p (a t) -> p a t", a=2)
        s4 = att[:, 4 * PL:6 * PL].rearrange("p (a t) -> p a t", a=2)
        pcx = otmp[:].rearrange("p (a c) -> p a c", c=16)
        scT = att[:, 0:512]
        mixhi = over("mixhi", [P, 1024], "ring", (SET_C + 3) * SLOT)
        mixlo = over("mixlo", [P, 1024], "mixed")
        projhi = over("projhi", [P, 2, PROJ], "ring", (SET_C + 1) * SLOT)
        projlo = over("projlo", [P, 2, PROJ], "ring", SLOT_PROJ * SLOT)
        osplit = over("osplit", [P, 2, 4, T], "att")
        ohi, olo = osplit[:, 0], osplit[:, 1]
        oflat = oT[:].rearrange("p r t -> p (r t)")
        zpad = oflat[:, 0:2 * (2 + T)].rearrange("p (a t) -> p a t", a=2)
        g2b = oflat[:, 0:D]
        mflat = merged[:].rearrange("p k t -> p (k t)")
        shf = mflat[:, 0:1024].rearrange("p (a g t) -> p a g t", a=2, g=KVG)
        fpe = mflat[:, 1024:2048].rearrange("p (a j c) -> p a j c", a=2, j=16)
        hidp = mflat[:, 0:512].rearrange("p (a c) -> p a c", a=2)
        diag = gab[:, 0, 0:NT * P].rearrange("p (t q) -> p t q", t=NT)
        pooled = ga.rearrange("p (a t) -> p a t", a=2)
        convh = gb.rearrange("p (a t) -> p a t", a=2)
        pc = poolT.rearrange("p a t -> p (a t)").rearrange("p (a c) -> p a c", c=32)
        pcT = convT.rearrange("p a t -> p (a t)").rearrange("p (a q) -> p a q", q=P)
        mhi0 = over("mhi0", [P, 4, T], "mixed")
        mhi = (mhi0[:], xhi[:, 0:4])
        mlo = over("mlo", [P, KT, T], "merged")
        qflat = qT[:].rearrange("p r t -> p (r t)")
        rt = qflat[:, 0:256].rearrange("p (a t e) -> p a t e", t=NT, e=PER_GROUP)
        etmp = qflat[:, 256:320].rearrange("p (t e) -> p t e", t=NT)
        comb = qflat[:, 320:384].rearrange("p (t e) -> p t e", t=NT)
        mask = qflat[:, 384:448].rearrange("p (t e) -> p t e", t=NT)
        rank = qflat[:, 448:512].rearrange("p (t e) -> p t e", t=NT)
        lgT = qcur[:]
        lg = qflat[:, 512:512 + NT * (GROUPS + NE)].rearrange("p (t e) -> p t e", t=NT)
        xn2 = att[:, 0:NT * D].rearrange("p (t d) -> p t d", t=NT)
        fin = xn2
        xgT = kv[:].rearrange("p (k s) -> p k s", k=KT)
        yN = gab[:].rearrange("p a c -> p (a c)")
        xn2T = over("xn2T", [P, KT, T], "xhi")
        squares = over("squares", [P, KT * T], "xlo")
        sel = qcur[:].rearrange("p (t e j) -> p t e j", t=NT, e=EB)
        selw = otmp[:].rearrange("p (t e j) -> p t e j", t=NT, e=EB)
        vflat = vbd[:].rearrange("p g c -> p (g c)")
        cmbT = vflat[:, 0:256]
        hN = vflat[:, 256:512]
        sl1 = cw2[:].rearrange("p a c -> p (a c)")
        hT = hidT[:].rearrange("p a g c -> p (a g c)").rearrange("p (k s) -> p k s", k=HT)
        spare = ([squares[:]], [mixed[:].rearrange("p b a t -> p (b a t)"), con[:, K_DIST:K_DIST + SLOT // 2]],
                 [mflat], [xn2T[:].rearrange("p k t -> p (k t)")])
        first_spare = 2 * SLOTS - len(spare)

        ident = con[:, K_ID:K_ID + P]
        dist = con[:, K_DIST:K_DIST + 3 * P]
        tri = con[:, K_TRI:K_TRI + P]
        ones = con[:, K_ONE:K_ONE + P]
        iota = con[:, K_IOTA:K_IOTA + CAP]
        cbias = con[:, K_CB:K_CB + NT * HEADS * 16].rearrange("p (a c) -> p a c", c=16)
        cmask = con[:, K_CM:K_CM + NT * 16].rearrange("p (t c) -> p t c", c=16)
        icnt = con[:, K_IC:K_IC + 2 * T].rearrange("p (a t) -> p a t", a=2)
        rk8 = con[:, K_RK:K_RK + PER_GROUP]
        fold = con[:, K_FOLD:K_FOLD + 32]
        fold2 = con[:, K_FOLD2:K_FOLD2 + GROUPS + NE]
        steps_of_cap = con[:, K_CAP:K_CAP + MAXPASS]

        x_in = [sem(f"x_in{t}") for t in range(NT)]
        ident_in = sem("ident_in")
        con_in = sem("con_in")
        prm_in = sem("prm_in")
        small_in = sem("small_in")
        vec_in = sem("vec_in")
        chunk_in = {s: sem(f"chunk_in{s}") for s in (0, 1, 2, 3, *range(SET_C, SLOTS, 2))}
        proj_in = [sem(f"proj_in{i}") for i in range(2)]
        expert_in = [sem(f"expert_in{i}") for i in range(SLOTS)]
        spare_in = sem("spare_in")
        expert_used = sem("expert_used")
        passes_done = sem("passes_done")
        out_done = sem("out_done")

        dve_step = sem("dve_step")
        loop_step = sem("loop_step")
        zeros_set = sem("zeros_set")
        ssq_done = sem("ssq_done")
        rstd_done = sem("rstd_done")
        pool_step = sem("pool_step")
        warm_done = sem("warm_done")
        hi_done = sem("hi_done")
        split_done = sem("split_done")
        diag_done = sem("diag_done")
        xhi_done = sem("xhi_done")
        xT_full = sem("xT_full")
        xnT_done = sem("xnT_done")
        q_full = sem("q_full")
        kvc_full = sem("kvc_full")
        kk_full = sem("kk_full")
        vg_full = sem("vg_full")
        u_full = sem("u_full")
        h_full = sem("h_full")
        b_full = sem("b_full")
        c_full = sem("c_full")
        hidp_full = sem("hidp_full")
        hidp_done = sem("hidp_done")
        hid_full = sem("hid_full")
        hid_done = sem("hid_done")
        mix_full = sem("mix_full")
        mix_split = sem("mix_split")
        projhi_done = sem("projhi_done")
        proj_split = sem("proj_split")
        kc_full = sem("kc_full")
        scT_full = sem("scT_full")
        scT_done = sem("scT_done")
        sc_full = sem("sc_full")
        q_done = sem("q_done")
        kvc_done = sem("kvc_done")
        kk_done = sem("kk_done")
        vg_done = sem("vg_done")
        u_done = sem("u_done")
        ch_done = sem("ch_done")
        conv_done = sem("conv_done")
        pooled_done = sem("pooled_done")
        poolT_done = sem("poolT_done")
        flat_done = sem("flat_done")
        gelu_in = sem("gelu_in")
        tanh_done = sem("tanh_done")
        hidT_done = sem("hidT_done")
        kc_done = sem("kc_done")
        csub_done = sem("csub_done")
        cexp_done = sem("cexp_done")
        pc_done = sem("pc_done")
        pcT_full = sem("pcT_full")
        pcT_done = sem("pcT_done")
        oc_full = sem("oc_full")
        s_full = sem("s_full")
        qcur_done = sem("qcur_done")
        s_max = sem("s_max")
        p_done = sem("p_done")
        weighed = sem("weighed")
        pT_full = sem("pT_full")
        pT_done = sem("pT_done")
        pv_full = sem("pv_full")
        o_read = sem("o_read")
        ga_full = sem("ga_full")
        gb_full = sem("gb_full")
        yp_full = sem("yp_full")
        yc_full = sem("yc_full")
        ga_done = sem("ga_done")
        gb_done = sem("gb_done")
        merge_done = sem("merge_done")
        o_done = sem("o_done")
        ohi_done = sem("ohi_done")
        oT_done = sem("oT_done")
        m0_full = sem("m0_full")
        yn_full = sem("yn_full")
        m0_done = sem("m0_done")
        merged_done = sem("merged_done")
        mhi_done = sem("mhi_done")
        mlo_done = sem("mlo_done")
        wo_used = sem("wo_used")
        wo_full = sem("wo_full")
        h_done = sem("h_done")
        xn2_done = sem("xn2_done")
        xn2T_full = sem("xn2T_full")
        xn2T_done = sem("xn2T_done")
        lgT_full = sem("lgT_full")
        lgT_done = sem("lgT_done")
        logit_full = sem("logit_full")
        sub_done = sem("sub_done")
        exp_done = sem("exp_done")
        mask_done = sem("mask_done")
        rank_full = sem("rank_full")
        count_full = sem("count_full")
        sel_done = sem("sel_done")
        cmb_full = sem("cmb_full")
        cmb_done = sem("cmb_done")
        xg_full = sem("xg_full")
        xg_done = sem("xg_done")
        hid1_full = sem("hid1_full")
        silu_done = sem("silu_done")
        y_full = sem("y_full")
        yn_done = sem("yn_done")
        gained = sem("gained")
        dve_fin = sem("dve_fin")
        act_fin = sem("act_fin")

        comb_done = sem("comb_done")
        comb_in = sem("comb_in")
        comb_ready = sem("comb_ready")

        add_done = sem("add_done")
        hT_full = sem("hT_full")
        hT_done = sem("hT_done")
        hn_done = sem("hn_done")
        rank_done = sem("rank_done")
        sel_step = sem("sel_step")

        def one(row):
            return rt[:, row, :, 0:1]

        def wide(ap, n):
            return ap.to_broadcast([P, NT, n])

        def flat(ap):
            n = len(ap.shape) - 1
            names = ["a", "b", "c", "d"][:n]
            return ap.rearrange(f"p {' '.join(names)} -> p ({' '.join(names)})") if n > 1 else ap

        def slot(n, half):
            return (CH_CK, CH_CV).index(n) * 2 + half if n in (CH_CK, CH_CV) else CHUNK_SET[n] + 2 * half

        def raw(n, half):
            return ring[:, slot(n, half)]

        def low(n, half):
            return part[slot(n, half)]

        def high(n, half):
            return part[slot(n, half) + 1]

        def before(n):
            return [m for m in range(n) if slot(m, 0) == slot(n, 0)]

        def floats(n):
            return KT // 2 * VGC if n == CH_VG else SLOT

        def proj(i):
            return ring[:, SLOT_PROJ, (i % 2) * PROJ:(i % 2 + 1) * PROJ]

        def landed(eng, n, half, more=0):
            eng.wait_ge(chunk_in[slot(n, half)], more * 16 + 16 * (len(before(n)) + 1))

        def have_high(act, n, half, more=0):
            landed(act, n, half, more)
            c = floats(n)
            nc.scalar.copy(high(n, half)[:, 0:c].bitcast(F32R), raw(n, half)[:, 0:c]).then_inc(hi_done, 1)

        def have_low(dve, n, half, more=0):
            c = floats(n)
            dve.wait_ge(hi_done, more * 4 + 2 * SPLITS.index(n) + half + 1)
            nc.vector.tensor_tensor(low(n, half)[:, 0:c].bitcast(F32R), raw(n, half)[:, 0:c], high(n, half)[:, 0:c], ALU.subtract).then_inc(split_done, 1)

        block = ctx.enter_context(nc.Block())

        @block.sync
        def _(sp):
            for t in range(NT):
                sp.dma_start(h[:, t], x[t * P:(t + 1) * P]).then_inc(x_in[t], 16)
            last_product = {CH_Q: ((q_full, 1), (q_full, 2)), CH_KV: ((kvc_full, 1), (kk_full, 1)),
                            CH_VG: ((vg_full, 1), (vg_full, 1)), CH_CK: ((hidp_full, 1), (hidp_full, 2)),
                            CH_UH: ((u_full, 1), (h_full, 1)), CH_CV: ((hidp_full, 3), (hidp_full, 4)),
                            CH_BC: ((b_full, 1), (c_full, 1)), CH_M0A: ((m0_full, 1), (m0_full, 2)),
                            CH_NSA: ((yn_full, 2), (yn_full, 4)), CH_M0B: ((m0_full, 3), (m0_full, 4))}
            for i in range(N_MG):
                last_product[CH_MG + i] = ((ga_full, i + 1), (gb_full, i + 1))

            def early_experts(first, end, free):
                sp.wait_ge(*free)
                for c in range(first, end):
                    sp.dma_start(ring[:, c], experts[c // NQ, c % NQ]).then_inc(expert_in[c], 16)

            def early_spare(n, free):
                sp.wait_ge(*free)
                b, q = divmod(first_spare + n, NQ)
                w = SLOT // len(spare[n])
                for i, piece in enumerate(spare[n]):
                    sp.dma_start(piece, experts[b, q, :, i * w:(i + 1) * w]).then_inc(spare_in, 16)

            for n in range(N_CHUNKS):
                if n == CH_WO:
                    early_experts(SLOT_PROJ, SET_C, (yc_full, N_MG))
                if n == CH_WO + 1:
                    early_experts(SET_C, SET_C + 2, (m0_full, 3))
                    early_experts(SET_C + 2, SET_B, (m0_full, 4))
                    early_spare(0, (m0_full, 4))
                if n == CH_Q:
                    sp.dma_start(ident, consts[:, K_ID:K_ID + P]).then_inc(ident_in, 16)
                if n == CH_KV:
                    sp.dma_start(con[:, P:], consts[:, P:]).then_inc(con_in, 16)
                for half in range(2):
                    if before(n):
                        sp.wait_ge(*last_product[before(n)[-1]][half])
                    c = floats(n)
                    sp.dma_start(raw(n, half)[:, 0:c], front[n, half, :, 0:c]).then_inc(chunk_in[slot(n, half)], 16)
                i = n - CH_MG
                if 0 <= i < N_MG:
                    sp.wait_ge(*((yc_full, i - 1) if i >= 2 else (hidp_full, 4)))
                    sp.dma_start(proj(i), projs[i]).then_inc(proj_in[i % 2], 16)
                if 0 <= i < SLOT_PROJ:
                    sp.wait_ge(hidp_full, i + 1)
                    sp.dma_start(ring[:, i], experts[0, i]).then_inc(expert_in[i], 16)
            early_experts(SET_B, SET_B + 2, (wo_used, 1))
            early_experts(SET_B + 2, SET_A, (wo_used, 2))
            early_spare(1, (wo_used, 2))
            early_experts(SET_A, SLOTS, (wo_full, 4))
            early_spare(2, (wo_full, 4))
            early_spare(3, (lgT_full, 1))

            for c in (*range(SLOTS, first_spare), *range(2 * SLOTS, ROUND * NQ)):
                b, q = c // NQ, c % NQ
                sp.wait_ge(expert_used, c - SLOTS + 1)
                sp.dma_start(ring[:, c % SLOTS], experts[b, q]).then_inc(expert_in[c % SLOTS], 16)
            sp.wait_ge(passes_done, 1)
            passes = sp.value_load(npass[0:1, 0:1], min_val=1, max_val=MAXPASS)
            rounds = experts.rearrange("(r b) q p c -> r b q p c", b=ROUND)
            with sp.Fori(1, passes * (NB // ROUND)) as r:
                for c in range(ROUND * NQ):
                    b, q = c // NQ, c % NQ
                    sp.wait_ge(expert_used, r * (ROUND * NQ) + (c - SLOTS + 1))
                    sp.dma_start(ring[:, c % SLOTS],
                                 rounds[bass.ds(r % (NB // ROUND), 1), b, q].rearrange("o p c -> (o p) c")).then_inc(expert_in[c % SLOTS], 16)
            for t in range(NT):
                sp.wait_ge((dve_fin, act_fin)[t], 1)
                sp.dma_start(out[t * P:(t + 1) * P], fin[:, t]).then_inc(out_done, 16)
            sp.wait_ge(out_done, 16 * NT)

        @block.gpsimd
        def _(pool):
            nc.gpsimd.memset(upad[:, :, 0:PAD], 0.0).then_inc(zeros_set, 1)
            nc.gpsimd.memset(s2[:, :, 0:PAD], 0.0).then_inc(zeros_set, 1)
            nc.gpsimd.memset(s4[:, :, 0:PAD], 0.0).then_inc(zeros_set, 1)
            nc.gpsimd.memset(zpad[:, :, 0:2], 0.0).then_inc(zeros_set, 1)
            nc.gpsimd.memset(hidT[:], 0.0).then_inc(zeros_set, 1)
            nc.gpsimd.memset(vbd[:], 0.0).then_inc(zeros_set, 1)
            nc.gpsimd.memset(stat[:, 32:34], -0.5).then_inc(zeros_set, 1)
            nc.gpsimd.memset(kcT[:], 0.0).then_inc(zeros_set, 1)
            pool.wait_ge(zeros_set, 8)
            steps = [0]

            def step(ins):
                steps[0] += 1
                ins.then_inc(pool_step, 1)
                pool.wait_ge(pool_step, steps[0])

            def rstd(col, done):
                nc.gpsimd.tensor_tensor(stat[:, col + 2:col + 4], stat[:, col:col + 2], stat[:, 32:34], ALU.pow).then_inc(done, 1)

            def half_means(first, col, before, done):
                pool.wait_ge(ssq_done, before + NT)
                step(nc.gpsimd.tensor_scalar(stat[:, col:col + 2], stat[:, first:first + 2], EPS, None, ALU.add))
                pool.wait_ge(ssq_done, before + 2 * NT)
                step(nc.gpsimd.tensor_tensor(stat[:, col:col + 2], stat[:, col:col + 2], stat[:, first + 2:first + 4], ALU.add))
                rstd(col, done)

            pool.wait_ge(ssq_done, NT)
            step(nc.gpsimd.tensor_scalar(stat[:, 20:22], stat[:, 0:2], EPS, None, ALU.add))
            rstd(20, rstd_done)

            for n in range(2):
                pool.wait_ge((poolT_done, conv_done)[n], 1)
                step(nc.gpsimd.tensor_copy(mixhi[:, 512 * n:512 * n + 512].bitcast(F32R), flat(mixed[:, n])))
                nc.gpsimd.tensor_tensor(mixlo[:, 512 * n:512 * n + 512].bitcast(F32R), flat(mixed[:, n]), mixhi[:, 512 * n:512 * n + 512],
                                        ALU.subtract).then_inc(mix_split, 1)

            half_means(4, 24, NT, rstd_done)
            pool.wait_ge(comb_in, 1)
            nc.gpsimd.tensor_tensor(one(9), one(9), one(5), ALU.mult)
            step(nc.gpsimd.tensor_tensor(rt[:, 10], rt[:, 10], wide(one(5), PER_GROUP), ALU.mult))
            step(nc.gpsimd.tensor_tensor(rt[:, 13], rt[:, 13], wide(one(9), PER_GROUP), ALU.mult))
            step(nc.gpsimd.tensor_tensor(rt[:, 10], rt[:, 10], rt[:, 13], ALU.add))
            for t in range(NT):
                nc.gpsimd.tensor_tensor(comb[:, t].rearrange("p (g e) -> p g e", g=GROUPS),
                                        rt[:, 3, t, 0:GROUPS].unsqueeze(2).to_broadcast([P, GROUPS, PER_GROUP]),
                                        rt[:, 10, t].unsqueeze(1).to_broadcast([P, GROUPS, PER_GROUP]), ALU.mult).then_inc(comb_ready, 1)
            pool.wait_ge(spare_in, 16 * sum(len(pieces) for pieces in spare))
            for n, pieces in enumerate(spare):
                c = first_spare + n
                pool.wait_ge(expert_used, c - SLOTS + 1)
                w = SLOT // 4
                for i in range(4):
                    piece = pieces[i * w // (SLOT // len(pieces))]
                    at = i * w % (SLOT // len(pieces))
                    nc.gpsimd.tensor_copy(ring[:, c % SLOTS, i * w:(i + 1) * w], piece[:, at:at + w]).then_inc(expert_in[c % SLOTS], 4)
            half_means(12, 28, 3 * NT, rstd_done)

        @block.scalar
        def _(act):
            for s1 in (p_done, pT_done, ga_done, gb_done, hT_done, yn_done):
                act.sem_inc(s1, 1)
            act.dma_start(prm[:], params).then_inc(prm_in, 16)
            act.wait_ge(zeros_set, 8)
            nc.scalar.activation(squares[:, 0:2], stat[:, 32:34], ACT.Square).then_inc(warm_done, 1)
            act.wait_ge(warm_done, 1)
            for t in range(NT):
                act.wait_ge(x_in[t], 16)
                nc.scalar.activation(squares[:, t * D:(t + 1) * D], h[:, t], ACT.Square,
                                     scale=D ** -0.5, accum_out=stat[:, t:t + 1]).then_inc(ssq_done, 1)
            act.dma_start(flat(cw2[:]), small).then_inc(small_in, 16)
            act.dma_start(flat(wg[:]), wgrp).then_inc(small_in, 16)
            act.dma_start(flat(rw[:]), routerw).then_inc(small_in, 16)
            act.dma_start(rb[:], routerb.to_broadcast([P, GROUPS + NE])).then_inc(small_in, 16)
            have_high(act, CH_Q, 0)
            act.wait_ge(prm_in, 16)
            for k in range(KT):
                act.wait_ge(xT_full, k // 2 + 1)
                nc.scalar.activation(xhi[:, k].bitcast(F32R), bank[k // 2][:, (k % 2) * T:(k % 2 + 1) * T], ACT.Copy,
                                     scale=prm[:, PR_G1 + k:PR_G1 + k + 1]).then_inc(xhi_done, 1)
            have_high(act, CH_Q, 1)
            have_high(act, CH_KV, 0)
            have_high(act, CH_KV, 1)
            for half in range(2):
                have_high(act, CH_VG, half)
                act.wait_ge(q_full, half + 1)
                nc.scalar.mul(flat(qT[:, 2 * half:2 * half + 2]), bank[4 + half][:], HD ** -0.5).then_inc(q_done, 1)
            have_high(act, CH_UH, 0)
            act.wait_ge(kk_full, 1)
            nc.scalar.copy(flat(kT), bank[1][:]).then_inc(kk_done, 1)
            have_high(act, CH_UH, 1)
            act.wait_ge(vg_full, 1)
            for t in range(NT):
                nc.scalar.copy(vN[:, :, t], bank[2 + t][:, 0:2 * P].rearrange("p (b c) -> p b c", b=2))
                ins = nc.scalar.activation(gts[:, t], bank[2 + t][:, 2 * P:VGC], ACT.Tanh, scale=0.5)
            ins.then_inc(vg_done, 1)
            have_high(act, CH_BC, 0)
            for a in range(2):
                if a:
                    have_high(act, CH_BC, 1)
                    act.wait_ge(h_full, 1)
                    nc.scalar.copy(flat(convh), bank[1][:]).then_inc(ch_done, 1)
                act.wait_ge(hidp_full, 2 * a + 2)
                nc.scalar.copy(hidp[:, a], bank[6 + a][:, 0:2 * P]).then_inc(hidp_done, 1)
            have_high(act, CH_MG, 0)
            have_high(act, CH_MG, 1)
            with act.Fori(0, N_MG // 2) as i2:
                for s in range(2):
                    i = i2 * 2 + s
                    act.wait_ge(s_full, i * 4 + 1)
                    act.wait_ge(q_done, 2)
                    nc.scalar.copy(qcur[:], qT[:, bass.ds(i, 1)].rearrange("p r t -> p (r t)")).then_inc(qcur_done, 1)
                    have_high(act, CH_MG + 1 + s, 0, i2)
                    act.wait_ge(proj_in[s], i2 * 16 + 16)
                    act.wait_ge(b_full, 1)
                    nc.scalar.copy(projhi[:, s].bitcast(F32R), proj(s)).then_inc(projhi_done, 1)

                    def exps(u):
                        act.wait_ge(s_max, i * 4 + (u + 1) + 1)
                        act.wait_ge(pT_full, i * 4 + max(u - 1, 0) + 1)
                        act.wait_ge(weighed, i * 4 + 1)
                        nc.scalar.activation(sP[:, u % 2, 0:P], sS[:, u % 2, 0:P], ACT.Exp,
                                             bias=smx[:, u % 2, 0:1], accum_out=ssum[:, u, 0:1])
                        nc.scalar.activation(sP[:, u % 2, P:3 * P], sS[:, u % 2, P:3 * P], ACT.Exp,
                                             bias=smx[:, u % 2, 1:2], accum_out=ssum[:, u, 1:2]).then_inc(p_done, 1)

                    def take_pT(u):
                        act.wait_ge(pT_full, i * 4 + (u + 1) + 1)
                        act.wait_ge(pv_full, i * 2 + u // 2 + 1)
                        nc.scalar.copy(sPT[:, u % 2], bank[6][:, 0:3 * P]).then_inc(pT_done, 1)

                    exps(0)
                    exps(1)
                    take_pT(0)
                    act.wait_ge(ga_full, i + 1)
                    act.wait_ge(merge_done, i + 1)
                    nc.scalar.activation(ga, bank[0][:], ACT.Tanh, scale=0.5).then_inc(ga_done, 1)
                    exps(2)
                    take_pT(1)
                    have_high(act, CH_MG + 1 + s, 1, i2)
                    exps(3)
                    take_pT(2)
                    take_pT(3)
                    act.wait_ge(gb_full, i + 1)
                    nc.scalar.activation(gb, bank[1][:], ACT.Tanh, scale=0.5).then_inc(gb_done, 1)

            act.wait_ge(gelu_in, 1)
            nc.scalar.activation(hidu[:], hidu[:], ACT.Tanh, scale=GELU_C).then_inc(tanh_done, 1)

            def gate_tanh(n):
                act.wait_ge(m0_full, n + 1)
                nc.scalar.activation(gates[n], bank[n][:], ACT.Tanh, scale=0.5).then_inc(m0_done, 1)

            act.wait_ge(yc_full, N_MG)
            have_high(act, CH_M0B, 0)
            have_high(act, CH_M0B, 1)
            act.wait_ge(merge_done, N_MG + 1)
            gate_tanh(0)
            have_high(act, CH_NSA, 0)
            gate_tanh(1)
            act.wait_ge(scT_full, 1)
            nc.scalar.copy(scT[:, 0:T], bank[5][:, 0:T])
            nc.scalar.copy(scT[:, T:2 * T], bank[7][:, 0:T]).then_inc(scT_done, 1)
            have_high(act, CH_NSA, 1)
            gate_tanh(2)
            act.wait_ge(csub_done, 1)
            nc.scalar.activation(pcx, pcx, ACT.Exp).then_inc(cexp_done, 1)
            have_high(act, CH_WO, 0)
            act.wait_ge(pcT_full, 1)
            nc.scalar.copy(flat(pcT), bank[7][:]).then_inc(pcT_done, 1)
            have_high(act, CH_WO, 1)
            gate_tanh(3)
            for n in range(2):
                act.wait_ge(o_done, n + 1)
                nc.scalar.activation(flat(ohi[:, 2 * n:2 * n + 2]).bitcast(F32R), flat(oT[:, 2 * n:2 * n + 2]), ACT.Copy,
                                     scale=0.5).then_inc(ohi_done, 1)
            act.wait_ge(oT_done, 2)
            act.dma_start(g2b, vecs[0:1].to_broadcast([P, D])).then_inc(vec_in, 16)

            def merged_high(n):
                act.wait_ge(merged_done, n + 1)
                act.wait_ge(oc_full, 2)
                nc.scalar.copy(flat(mhi[n // 2][:, 2 * (n % 2):2 * (n % 2) + 2]).bitcast(F32R),
                               flat(merged[:, 2 * n:2 * n + 2])).then_inc(mhi_done, 1)

            for n in range(4):
                merged_high(n)
            have_high(act, CH_WO + 1, 0)
            have_high(act, CH_WO + 1, 1)

            for n in range(4):
                t, half = n % 2, n // 2
                act.wait_ge(h_done, n + 1)
                nc.scalar.activation(gates[n], h[:, t, half * 512:(half + 1) * 512], ACT.Square,
                                     scale=D ** -0.5, accum_out=stat[:, 4 + n:5 + n]).then_inc(ssq_done, 1)
            for k in (0, 1, 4, 5):
                act.wait_ge(xn2T_full, k // 2 + 1)
                nc.scalar.activation(xn2T[:, k], bank[4 + k // 2][:, (k % 2) * T:(k % 2 + 1) * T], ACT.Copy,
                                     scale=prm[:, PR_G2 + k:PR_G2 + k + 1]).then_inc(xn2T_done, 1)
            act.wait_ge(lgT_full, 1)
            nc.scalar.copy(lgT, bank[0][:, 0:T]).then_inc(lgT_done, 1)
            act.wait_ge(xn2_done, NT)
            act.dma_start(g2b, vecs[1:2].to_broadcast([P, D])).then_inc(vec_in, 16)
            act.wait_ge(sub_done, 1)
            nc.scalar.activation(rt[:, 1, :, 0:GROUPS], rt[:, 0, :, 0:GROUPS], ACT.Exp).then_inc(exp_done, 1)
            act.wait_ge(sub_done, 2)
            nc.scalar.activation(rt[:, 9, :, 0:1], rt[:, 8, :, 0:1], ACT.Exp).then_inc(exp_done, 1)

            act.wait_ge(passes_done, 1)
            passes = act.value_load(npass[0:1, 0:1], min_val=1, max_val=MAXPASS)
            with act.Fori(0, passes * NB) as b:
                act.wait_ge(xg_full, b * 2 + 2)
                nc.scalar.copy(flat(xgT[:, 0:4]), bank[2][:]).then_inc(xg_done, 1)
                act.wait_ge(hid1_full, b + 1)
                nc.scalar.activation(sl1, bank[0][:, 0:HID], ACT.Silu).then_inc(silu_done, 1)
                act.wait_ge(hT_full, b + 1)
                nc.scalar.copy(flat(hT), bank[1][:, 0:HT * P]).then_inc(hT_done, 1)
                for half in range(2):
                    act.wait_ge(y_full, b * 2 + (half + 1))
                    nc.scalar.copy(yN[:, half * 512:(half + 1) * 512], bank[4 + half][:]).then_inc(yn_done, 1)
            for n in range(4):
                t, half = n % 2, n // 2
                act.wait_ge(add_done, passes * (4 * NB) + n)
                nc.scalar.activation(squares[:, n * 512:(n + 1) * 512], h[:, t, half * 512:(half + 1) * 512], ACT.Square,
                                     scale=D ** -0.5, accum_out=stat[:, 12 + n:13 + n]).then_inc(ssq_done, 1)
            act.wait_ge(rstd_done, 3)
            act.wait_ge(gained, 1)
            nc.scalar.activation(fin[:, 1], fin[:, 1], ACT.Copy, scale=stat[:, 31:32]).then_inc(act_fin, 1)

        @block.vector
        def _(dve):
            for s1 in (s_max, weighed, merge_done, o_read, hn_done):
                dve.sem_inc(s1, 1)
            dve.sem_inc(add_done, 3)
            counted = [0]

            def step(ins):
                counted[0] += 1
                ins.then_inc(dve_step, 1)
                dve.wait_ge(dve_step, counted[0])

            dve.wait_ge(rstd_done, 1)
            dve.wait_ge(ident_in, 16)
            for t in range(NT):
                nc.vector.tensor_scalar(diag[:, t], ident, stat[:, 22 + t:23 + t], None, ALU.mult).then_inc(diag_done, 1)
            nc.vector.memset(fpe[:, :, :, 2 * NCMP:32], 0.0)
            have_low(dve, CH_Q, 0)
            dve.wait_ge(prm_in, 16)
            for k in range(KT):
                dve.wait_ge(xhi_done, k // 2 * 2 + 2)
                nc.vector.scalar_tensor_tensor(xlo[:, k].bitcast(F32R), bank[k // 2][:, (k % 2) * T:(k % 2 + 1) * T],
                                               prm[:, PR_G1 + k:PR_G1 + k + 1], xhi[:, k],
                                               ALU.mult, ALU.subtract).then_inc(xnT_done, 1)
            have_low(dve, CH_Q, 1)
            have_low(dve, CH_KV, 0)
            have_low(dve, CH_KV, 1)
            have_low(dve, CH_VG, 0)
            have_low(dve, CH_VG, 1)
            dve.wait_ge(kvc_full, 1)
            kvc = bank[0][:].rearrange("p (a t) -> p a t", a=2)
            for g in range(KVG):
                nc.vector.tensor_copy(shf[0:HD, :, g, :], kvc[g * HD:(g + 1) * HD])
                ins = nc.vector.tensor_copy(shf[HD:P, :, g, 0:T - 1], kvc[g * HD:(g + 1) * HD, :, 1:T])
            ins.then_inc(kvc_done, 1)
            dve.wait_ge(kvc_done, 1)
            for a in range(2):
                for g in range(KVG):
                    src = shf[:, a, g, 0:CMP_STRIDE * (NCMP + 1)].rearrange("p (c j z) -> p j c z", j=CMP_STRIDE // 2, z=2)
                    for hi in range(2):
                        ins = nc.vector.tensor_tensor(
                            fpe[:, a, 8 * hi:8 * hi + 8, g * NCMP:(g + 1) * NCMP],
                            src[:, :, hi:hi + NCMP, 0],
                            prm[:, PR_PE + 16 * a + 8 * hi:PR_PE + 16 * a + 8 * hi + 8].unsqueeze(2).to_broadcast([P, 8, NCMP]),
                            ALU.add)
            ins.then_inc(flat_done, 1)
            have_low(dve, CH_UH, 0)
            have_low(dve, CH_UH, 1)
            dve.wait_ge(vg_done, 1)
            step(nc.vector.tensor_scalar(gts[:], gts[:], 1.0, 0.5, ALU.add, ALU.mult))
            dve.wait_ge(u_full, 1)
            dve.wait_ge(zeros_set, 8)
            nc.vector.tensor_copy(upad[:, :, PAD:], bank[0][:].rearrange("p (a t) -> p a t", a=2)).then_inc(u_done, 1)
            dve.wait_ge(u_done, 1)
            have_low(dve, CH_BC, 0)
            have_low(dve, CH_BC, 1)
            step(nc.vector.tensor_tensor(s2[:, :, PAD:], upad[:, :, PAD:], upad[:, :, PAD - 1:-1], ALU.add))
            dve.wait_ge(con_in, 16)
            step(nc.vector.tensor_tensor(s4[:, :, PAD:], s2[:, :, PAD:], s2[:, :, PAD - 2:-2], ALU.add))
            nc.vector.tensor_tensor(pooled[0:HD, 0], s2[0:HD, 0, PAD:], icnt[0:HD, 0], ALU.mult)
            step(nc.vector.tensor_tensor(pooled[HD:P, 0], s4[HD:P, 0, PAD:], icnt[HD:P, 0], ALU.mult))
            step(nc.vector.tensor_tensor(s2[:, 1, PAD:], s4[:, 1, PAD:], s4[:, 1, PAD - 4:-4], ALU.add))
            nc.vector.tensor_tensor(pooled[0:HD, 1], s2[0:HD, 1, PAD:], icnt[0:HD, 1], ALU.mult)
            step(nc.vector.tensor_tensor(s4[HD:P, 1, PAD:], s2[HD:P, 1, PAD:], s2[HD:P, 1, PAD - 8:-8], ALU.add))
            step(nc.vector.tensor_tensor(pooled[HD:P, 1], s4[HD:P, 1, PAD:], icnt[HD:P, 1], ALU.mult))
            nc.vector.tensor_tensor(pooled, pooled, upad[:, :, PAD:], ALU.subtract).then_inc(pooled_done, 1)
            have_low(dve, CH_MG, 0)
            have_low(dve, CH_MG, 1)
            dve.wait_ge(ch_done, 1)
            dve.wait_ge(c_full, 1)
            step(nc.vector.tensor_tensor(zpad[:, :, 2:], bank[3][:].rearrange("p (a t) -> p a t", a=2), convh, ALU.mult))
            for tap in range(CONV_K):
                for a in range(2):
                    w = prm[:, PR_CW + 2 * tap + a:PR_CW + 2 * tap + a + 1]
                    z = zpad[:, a, tap:tap + T]
                    if tap == 0:
                        ins = nc.vector.tensor_scalar(convT[:, a], z, w, None, ALU.mult)
                    else:
                        ins = nc.vector.scalar_tensor_tensor(convT[:, a], z, w, convT[:, a], ALU.mult, ALU.add)
                step(ins)
            nc.vector.scalar_tensor_tensor(flat(convT), flat(convT), 0.5, bank[2][:], ALU.mult, ALU.mult).then_inc(conv_done, 1)
            dve.wait_ge(mix_full, 1)
            for a in range(2):
                ins = nc.vector.tensor_scalar(poolT[:, a], bank[6][:, a * T:(a + 1) * T],
                                              prm[:, PR_PS + a:PR_PS + a + 1], 0.5, ALU.mult, ALU.mult)
            ins.then_inc(poolT_done, 1)
            dve.wait_ge(hid_full, 1)
            nc.vector.tensor_copy(hidg[:], bank[7][:, 0:4 * 32].rearrange("p (a c) -> p a c", c=32)[:, :, 0:2 * NCMP]).then_inc(hid_done, 1)
            dve.wait_ge(hid_done, 1)

            LS = 13
            with dve.Fori(0, N_MG // 2) as i2:
                k = [0]

                def lstep(ins):
                    k[0] += 1
                    ins.then_inc(loop_step, 1)
                    dve.wait_ge(loop_step, i2 * (2 * LS) + k[0])

                for s in range(2):
                    i = i2 * 2 + s

                    def scores(u):
                        g = u % 2
                        dve.wait_ge(s_full, i * 4 + (u + 1) + 1)
                        dve.wait_ge(p_done, i * 4 + max(u - 1, 0) + 1)
                        lstep(nc.vector.scalar_tensor_tensor(sS[:, u % 2], dist, con[:, bass.ds(i + (K_SL + g * REP), 1)],
                                                             bank[4 + u % 2][:, 0:3 * P], ALU.mult, ALU.add))
                        nc.vector.tensor_reduce(smx[:, u % 2, 0:1], sS[:, u % 2, 0:P], AX.X, ALU.max, negate=True)
                        nc.vector.tensor_reduce(smx[:, u % 2, 1:2], sS[:, u % 2, P:3 * P], AX.X, ALU.max,
                                                negate=True).then_inc(s_max, 1)

                    def weigh(u):
                        g, b = u % 2, u // 2
                        dve.wait_ge(p_done, i * 4 + (u + 1) + 1)
                        lstep(nc.vector.reciprocal(coef[:, u], ssum[:, u]))
                        gv = gts[:].rearrange("p t (a c) -> p a c t", c=3)[:, bass.ds(i + g * REP, 1), 1 + b]
                        lstep(nc.vector.tensor_tensor(coef[:, u], coef[:, u], gv.rearrange("p a t -> p (a t)"), ALU.mult))
                        nc.vector.tensor_scalar(sP[:, u % 2, 0:P], sP[:, u % 2, 0:P], coef[:, u, 0:1], None, ALU.mult)
                        nc.vector.tensor_scalar(sP[:, u % 2, P:3 * P], sP[:, u % 2, P:3 * P], coef[:, u, 1:2], None,
                                                ALU.mult).then_inc(weighed, 1)

                    scores(0)
                    scores(1)
                    weigh(0)
                    have_low(dve, CH_MG + 1 + s, 0, i2)
                    weigh(1)
                    scores(2)
                    dve.wait_ge(projhi_done, i + 1)
                    nc.vector.tensor_tensor(projlo[:, s].bitcast(F32R), proj(s), projhi[:, s], ALU.subtract).then_inc(proj_split, 1)
                    weigh(2)
                    scores(3)
                    weigh(3)
                    have_low(dve, CH_MG + 1 + s, 1, i2)
                    dve.wait_ge(ga_done, i + 2)
                    dve.wait_ge(yp_full, i + 1)
                    nc.vector.scalar_tensor_tensor(ga, ga, 1.0, bank[2][:], ALU.add, ALU.mult)
                    dve.wait_ge(gb_done, i + 2)
                    dve.wait_ge(yc_full, i + 1)
                    lstep(nc.vector.scalar_tensor_tensor(gb, gb, 1.0, bank[3][:], ALU.add, ALU.mult))
                    nc.vector.tensor_tensor(merged[:, bass.ds(i * 2, 2)].rearrange("p k t -> p (k t)"), ga, gb,
                                            ALU.add).then_inc(merge_done, 1)
                    dve.wait_ge(pv_full, i * 2 + 3)
                    nc.vector.tensor_copy(oT[:, bass.ds(i, 1)].rearrange("p r t -> p (r t)"), bank[7][:, 0:T]).then_inc(o_read, 1)
                    assert k[0] == LS * (s + 1)

            step(nc.vector.tensor_tensor(hidu[:], hidg[:], hidg[:], ALU.mult))
            step(nc.vector.tensor_scalar(hidu[:], hidu[:], 0.044715, 1.0, ALU.mult, ALU.add))
            nc.vector.tensor_tensor(hidu[:], hidu[:], hidg[:], ALU.mult).then_inc(gelu_in, 1)
            dve.wait_ge(tanh_done, 1)
            for g in range(KVG):
                c = slice(g * NCMP, (g + 1) * NCMP)
                ins = nc.vector.scalar_tensor_tensor(hidT[:, :, g, 0:NCMP], hidu[:, :, c], 1.0, hidg[:, :, c], ALU.add, ALU.mult)
            ins.then_inc(hidT_done, 1)
            have_low(dve, CH_M0B, 0)
            dve.wait_ge(kc_full, 1)
            nc.vector.tensor_scalar(kcT[:, 0:16], bank[4][:, 0:16], 0.5, None, ALU.mult)
            for r in range(REP):
                ins = nc.vector.tensor_scalar(vbd[32 * r:32 * r + 32, :, r * HD:(r + 1) * HD],
                                              bank[4][32 * r:32 * r + 32, 64:64 + KVG * HD].rearrange("p (g d) -> p g d", g=KVG),
                                              0.5, None, ALU.mult)
            ins.then_inc(kc_done, 1)
            dve.wait_ge(merge_done, N_MG + 1)
            dve.wait_ge(yp_full, N_MG)
            step(nc.vector.memset(pc, 0.0))
            have_low(dve, CH_M0B, 1)
            have_low(dve, CH_NSA, 0)
            dve.wait_ge(sc_full, 1)
            step(nc.vector.tensor_tensor(pcx, bank[6][:].rearrange("p (a c) -> p a c", c=32)[:, :, 0:16], cbias, ALU.add))
            step(nc.vector.tensor_reduce(pcs[:, 0], pcx, AX.X, ALU.max))
            nc.vector.tensor_tensor(pcx, pcx, pcs[:, 0].unsqueeze(2).to_broadcast([P, NT * HEADS, 16]),
                                    ALU.subtract).then_inc(csub_done, 1)
            dve.wait_ge(cexp_done, 1)
            step(nc.vector.tensor_reduce(pcs[:, 1], pcx, AX.X, ALU.add))
            step(nc.vector.reciprocal(pcs[:, 2], pcs[:, 1]))
            step(nc.vector.tensor_tensor(pcs[:, 3].rearrange("p (t a) -> p t a", t=NT), pcs[:, 2].rearrange("p (t a) -> p t a", t=NT),
                                         gts[:].rearrange("p t (a c) -> p t a c", c=3)[:, :, :, 0], ALU.mult))
            step(nc.vector.tensor_tensor(pcx, pcx, pcs[:, 3].unsqueeze(2).to_broadcast([P, NT * HEADS, 16]), ALU.mult))
            for t in range(NT):
                a = slice(t * HEADS, (t + 1) * HEADS)
                ins = nc.vector.tensor_tensor(pc[:, a, 0:16], pcx[:, a], cmask[:, t].unsqueeze(1).to_broadcast([P, HEADS, 16]), ALU.mult)
            ins.then_inc(pc_done, 1)
            have_low(dve, CH_NSA, 1)
            have_low(dve, CH_WO, 0)
            dve.wait_ge(o_read, N_MG + 1)
            for n in range(2):
                dve.wait_ge(oc_full, n + 1)
                o = flat(oT[:, 2 * n:2 * n + 2])
                nc.vector.tensor_tensor(o, o, bank[4 + n][:], ALU.add).then_inc(o_done, 1)
            for n in range(2):
                dve.wait_ge(ohi_done, n + 1)
                nc.vector.scalar_tensor_tensor(flat(olo[:, 2 * n:2 * n + 2]).bitcast(F32R), flat(oT[:, 2 * n:2 * n + 2]), 0.5,
                                               flat(ohi[:, 2 * n:2 * n + 2]), ALU.mult, ALU.subtract).then_inc(oT_done, 1)
            have_low(dve, CH_WO, 1)

            def merge(n):
                dve.wait_ge(m0_done, n + 1)
                dve.wait_ge(yn_full, n + 1)
                step(nc.vector.scalar_tensor_tensor(gates[n], gates[n], 1.0, bank[(4, 5, 0, 1)[n]][:], ALU.add, ALU.mult))
                m = flat(merged[:, 2 * n:2 * n + 2])
                nc.vector.tensor_tensor(m, m, gates[n], ALU.add).then_inc(merged_done, 1)

            def merged_low(n):
                m = flat(merged[:, 2 * n:2 * n + 2])
                dve.wait_ge(mhi_done, n + 1)
                nc.vector.tensor_tensor(flat(mlo[:, 2 * n:2 * n + 2]).bitcast(F32R), m, flat(mhi[n // 2][:, 2 * (n % 2):2 * (n % 2) + 2]),
                                        ALU.subtract).then_inc(mlo_done, 1)

            for n in range(4):
                merge(n)
                if n > 0:
                    merged_low(n - 1)
            merged_low(3)
            have_low(dve, CH_WO + 1, 0)
            have_low(dve, CH_WO + 1, 1)
            for n in range(4):
                t, half = n % 2, n // 2
                dve.wait_ge(wo_full, n + 1)
                hv = h[:, t, half * 512:(half + 1) * 512]
                nc.vector.tensor_tensor(hv, hv, bank[(2, 3, 6, 7)[n]][:], ALU.add).then_inc(h_done, 1)

            dve.wait_ge(rstd_done, 2)
            for t in range(NT):
                nc.vector.tensor_scalar(diag[:, t], ident, stat[:, 26 + t:27 + t], None, ALU.mult).then_inc(diag_done, 1)
            for k in (2, 3, 6, 7):
                dve.wait_ge(xn2T_full, k // 2 + 1)
                nc.vector.tensor_scalar(xn2T[:, k], bank[4 + k // 2][:, (k % 2) * T:(k % 2 + 1) * T],
                                        prm[:, PR_G2 + k:PR_G2 + k + 1], None, ALU.mult).then_inc(xn2T_done, 1)
            dve.wait_ge(vec_in, 16)
            for t in range(NT):
                dve.wait_ge(h_done, 4)
                nc.vector.scalar_tensor_tensor(xn2[:, t], h[:, t], stat[:, 26 + t:27 + t], g2b, ALU.mult, ALU.mult).then_inc(xn2_done, 1)
            dve.wait_ge(logit_full, 1)
            dve.wait_ge(small_in, 64)
            step(nc.vector.tensor_tensor(lg, bank[3][:, 0:NT * (GROUPS + NE)].rearrange("p (t e) -> p t e", t=NT),
                                         rb[:].unsqueeze(1).to_broadcast([P, NT, GROUPS + NE]), ALU.add))
            G = lg[:, :, 0:GROUPS]
            E4 = lg[:, :, GROUPS:].rearrange("p t (g e) -> p t g e", g=GROUPS)

            step(nc.vector.tensor_reduce(one(2), G, AX.X, ALU.max))
            nc.vector.tensor_tensor(rt[:, 0, :, 0:GROUPS], G, wide(one(2), GROUPS), ALU.subtract).then_inc(sub_done, 1)

            def first_largest(out_row, vals, top, n, scratch):
                v = rt[:, scratch, :, 0:n]
                step(nc.vector.tensor_tensor(v, vals, wide(top, n), ALU.is_equal))
                step(nc.vector.tensor_tensor(v, v, rk8[:, 0:n].unsqueeze(1).to_broadcast([P, NT, n]), ALU.mult))
                step(nc.vector.tensor_reduce(one(scratch + 1), v, AX.X, ALU.max))
                step(nc.vector.tensor_tensor(rt[:, out_row, :, 0:n], v, wide(one(scratch + 1), n), ALU.is_equal))

            first_largest(3, G, one(2), GROUPS, 4)
            et = etmp.rearrange("p t (g e) -> p t g e", g=GROUPS)
            for t in range(NT):
                ins = nc.vector.tensor_tensor(et[:, t], E4[:, t], rt[:, 3, t, 0:GROUPS].unsqueeze(2).to_broadcast([P, GROUPS, PER_GROUP]), ALU.mult)
            step(ins)
            step(nc.vector.tensor_reduce(rt[:, 6], etmp.rearrange("p t (g e) -> p t e g", g=GROUPS), AX.X, ALU.add))
            step(nc.vector.tensor_reduce(one(7), rt[:, 6], AX.X, ALU.max))
            first_largest(10, rt[:, 6], one(7), PER_GROUP, 4)
            step(nc.vector.scalar_tensor_tensor(rt[:, 11], rt[:, 10], NEG, rt[:, 6], ALU.mult, ALU.add))
            step(nc.vector.tensor_reduce(one(12), rt[:, 11], AX.X, ALU.max))
            first_largest(13, rt[:, 11], one(12), PER_GROUP, 4)
            nc.vector.tensor_tensor(one(8), one(12), one(7), ALU.subtract).then_inc(sub_done, 1)
            step(nc.vector.tensor_tensor(rt[:, 14], rt[:, 10], rt[:, 13], ALU.add))
            for t in range(NT):
                ins = nc.vector.tensor_tensor(mask[:, t].rearrange("p (g e) -> p g e", g=GROUPS),
                                              rt[:, 3, t, 0:GROUPS].unsqueeze(2).to_broadcast([P, GROUPS, PER_GROUP]),
                                              rt[:, 14, t].unsqueeze(1).to_broadcast([P, GROUPS, PER_GROUP]), ALU.mult)
            ins.then_inc(mask_done, 1)
            dve.wait_ge(exp_done, 1)
            step(nc.vector.tensor_reduce(one(4), rt[:, 1, :, 0:GROUPS], AX.X, ALU.add))
            dve.wait_ge(exp_done, 2)
            step(nc.vector.tensor_scalar(one(5), one(9), 1.0, None, ALU.add))
            step(nc.vector.tensor_tensor(one(4), one(4), one(5), ALU.mult))
            nc.vector.reciprocal(one(5), one(4)).then_inc(comb_in, 1)
            dve.wait_ge(count_full, 1)
            step(nc.vector.tensor_reduce(pcnt[:, 0:1], bank[2][:, 0:NE], AX.X, ALU.max))
            step(nc.vector.tensor_scalar(pcnt[:, 8:8 + MAXPASS], steps_of_cap, pcnt[:, 0:1], None, ALU.is_lt))
            step(nc.vector.tensor_reduce(pcnt[:, 1:2], pcnt[:, 8:8 + MAXPASS], AX.X, ALU.add))
            nc.vector.tensor_copy(npass[:], pcnt[:, 1:2]).then_inc(passes_done, 1)
            dve.wait_ge(rank_full, 1)
            step(nc.vector.scalar_tensor_tensor(rank, bank[1][:, 0:NT * NE].rearrange("p (t e) -> p t e", t=NT), 1.0, mask, ALU.add, ALU.mult))
            dve.wait_ge(passes_done, 1)
            passes = dve.value_load(npass[0:1, 0:1], min_val=1, max_val=MAXPASS)
            with dve.Fori(0, passes) as rnd:
                with dve.Fori(0, NB) as bb:
                    b = rnd * NB + bb
                    dve.wait_ge(xg_full, b * 2 + 1)
                    for t in range(NT):
                        ins = nc.vector.tensor_tensor(sel[:, t], iota.unsqueeze(1).to_broadcast([P, EB, CAP]),
                                                      rank[:, t, bass.ds(bb * EB, EB)].unsqueeze(2).to_broadcast([P, EB, CAP]),
                                                      ALU.is_equal)
                    ins.then_inc(sel_step, 1)
                    dve.wait_ge(sel_step, b + 1)
                    dve.wait_ge(comb_ready, NT)
                    for t in range(NT):
                        ins = nc.vector.tensor_tensor(selw[:, t], sel[:, t],
                                                      comb[:, t, bass.ds(bb * EB, EB)].unsqueeze(2).to_broadcast([P, EB, CAP]),
                                                      ALU.mult)
                    ins.then_inc(sel_done, 1)
                    dve.wait_ge(xg_full, b * 2 + 2 + 1)
                    nc.vector.tensor_copy(flat(xgT[:, 4:8]), bank[3][:]).then_inc(xg_done, 1)
                    dve.wait_ge(cmb_full, b + 1)
                    nc.vector.tensor_copy(cmbT, bank[1][:, 0:T]).then_inc(cmb_done, 1)
                    dve.wait_ge(silu_done, b + 1)
                    nc.vector.tensor_tensor(hN, sl1, bank[0][:, HID:2 * HID], ALU.mult).then_inc(hn_done, 1)
                    for half in range(2):
                        for t in range(NT):
                            dve.wait_ge(comb_done, b * 4 + (2 * half + t + 1))
                            hv = h[:, t, half * 512:(half + 1) * 512]
                            nc.vector.tensor_tensor(hv, hv, bank[6 + t][:], ALU.add).then_inc(add_done, 1)
                nc.vector.tensor_scalar(rank, rank, float(CAP), None, ALU.subtract).then_inc(rank_done, 1)
                dve.wait_ge(rank_done, rnd + 1)
            dve.wait_ge(vec_in, 32)
            dve.wait_ge(add_done, passes * (4 * NB) + 3)
            nc.vector.tensor_tensor(fin[:, 1], h[:, 1], g2b, ALU.mult).then_inc(gained, 1)
            dve.wait_ge(rstd_done, 3)
            nc.vector.scalar_tensor_tensor(fin[:, 0], h[:, 0], stat[:, 30:31], g2b, ALU.mult, ALU.mult).then_inc(dve_fin, 1)

        @block.tensor
        def _(pe):
            mm = nc.tensor.matmul
            for s1 in (s_full, pT_full, pv_full, xg_full):
                pe.sem_inc(s1, 1)

            def turned(banks, full):
                for k in range(KT):
                    for t in range(NT):
                        ins = mm(bank[banks + k // 2][:, (k % 2) * T + t * P:(k % 2) * T + (t + 1) * P], h[:, t, k * P:(k + 1) * P],
                                 diag[:, t], start=True, stop=True)
                    if k % 2:
                        ins.then_inc(full, 1)

            pe.wait_ge(diag_done, NT)
            turned(0, xT_full)

            def product(dst, whi, wlo, ahi, alo, start, stop):
                mm(dst, whi, ahi, start=start, stop=False)
                mm(dst, whi, alo, start=False, stop=False)
                return mm(dst, wlo, ahi, start=False, stop=stop)

            def parts(n, half, c):
                return [w[:, 0:floats(n)].bitcast(F32R).rearrange("p (k c) -> p k c", c=c) for w in (high(n, half), low(n, half))]

            def split(n, half, more=0):
                pe.wait_ge(split_done, more * 4 + 2 * SPLITS.index(n) + half + 1)

            XH, XL = xhi[:].bitcast(F32R), xlo[:].bitcast(F32R)

            def channels(dst, w, c0, k_tiles=KT, ahi=XH, alo=XL):
                for k in range(k_tiles):
                    ins = product(dst, w[0][:, k, c0:c0 + P], w[1][:, k, c0:c0 + P], ahi[:, k], alo[:, k], k == 0, k == k_tiles - 1)
                return ins

            def pair(dst, n, half, full, more=0):
                split(n, half, more)
                for a in range(2):
                    ins = channels(dst[:, a * T:(a + 1) * T], parts(n, half, 2 * P), a * P)
                ins.then_inc(full, 1)

            split(CH_Q, 0)
            w = parts(CH_Q, 0, 2 * P)
            for a in range(2):
                for k in range(KT):
                    if a == 0:
                        pe.wait_ge(xnT_done, k + 1)
                    ins = product(bank[4][:, a * T:(a + 1) * T], w[0][:, k, a * P:(a + 1) * P], w[1][:, k, a * P:(a + 1) * P],
                                  XH[:, k], XL[:, k], k == 0, k == KT - 1)
            ins.then_inc(q_full, 1)
            pair(bank[5], CH_Q, 1, q_full)
            pair(bank[0], CH_KV, 0, kvc_full)
            pair(bank[1], CH_KV, 1, kk_full)
            for half in range(2):
                split(CH_VG, half)
            for t in range(NT):
                for k in range(KT):
                    w = parts(CH_VG, k // 4, VGC)
                    cols = slice(t * P, (t + 1) * P)
                    mm(bank[2 + t][:, 0:VGC], XH[:, k, cols], w[0][:, k % 4], start=(k == 0), stop=False)
                    mm(bank[2 + t][:, 0:VGC], XH[:, k, cols], w[1][:, k % 4], start=False, stop=False)
                    ins = mm(bank[2 + t][:, 0:VGC], XL[:, k, cols], w[0][:, k % 4], start=False, stop=(k == KT - 1))
            ins.then_inc(vg_full, 1)

            def compress(a):
                for half in range(2):
                    landed(pe, (CH_CK, CH_CV)[a], half)
                    w = raw((CH_CK, CH_CV)[a], half).rearrange("p (j c) -> p j c", j=8)
                    for j in range(8):
                        r = slice(32 * (j % 4), 32 * (j % 4) + 32)
                        ins = mm(bank[6 + a][r, 0:2 * P], fpe[:, a, 8 * half + j], w[:, j],
                                 start=(half == 0 and j < 4), stop=(half == 1 and j >= 4))
                    ins.then_inc(hidp_full, 1)

            pe.wait_ge(flat_done, 1)
            compress(0)
            pe.wait_ge(kvc_done, 1)
            pair(bank[0], CH_UH, 0, u_full)
            pe.wait_ge(kk_done, 1)
            pair(bank[1], CH_UH, 1, h_full)
            compress(1)
            pe.wait_ge(vg_done, 1)
            pair(bank[2], CH_BC, 0, b_full)
            pair(bank[3], CH_BC, 1, c_full)
            pe.wait_ge(con_in, 16)
            pe.wait_ge(hidp_done, 2)
            for a in range(2):
                for ht in range(2):
                    c = 32 * (2 * a + ht)
                    ins = mm(bank[7][:, c:c + 32], hidp[:, a, ht * P:(ht + 1) * P], fold, start=True, stop=True)
            ins.then_inc(hid_full, 1)
            pe.wait_ge(pooled_done, 1)
            pe.wait_ge(small_in, 64)
            for a in range(2):
                ins = mm(bank[6][:, a * T:(a + 1) * T], wg[:, a], pooled[:, a], start=True, stop=True)
            ins.then_inc(mix_full, 1)
            pe.wait_ge(q_done, 2)
            pe.wait_ge(u_done, 1)
            pe.wait_ge(ch_done, 1)

            with pe.Fori(0, N_MG // 2) as i2:
                for s in range(2):
                    i = i2 * 2 + s
                    n = CH_MG + s
                    wp = [w[:, s].bitcast(F32R).rearrange("p (a k c) -> p a k c", a=2, k=2) for w in (projhi, projlo)]
                    src = [w[:].bitcast(F32R).rearrange("p (a k t) -> p a k t", a=2, k=2) for w in (mixhi, mixlo)]

                    def project(dst, n):
                        for a in range(2):
                            ins = channels(dst[:, a * T:(a + 1) * T], [w[:, n] for w in wp], a * P, 2, src[0][:, n], src[1][:, n])
                        return ins

                    def s_unit(u):
                        g, b = u % 2, u // 2
                        rows = slice(g * HD, (g + 1) * HD)
                        if u == 0:
                            pe.wait_ge(qcur_done, i + 1)
                        pe.wait_ge(s_max, i * 4 + max(u - 1, 0) + 1)
                        for t in range(NT):
                            ins = mm(bank[4 + u % 2][:, t * P:(t + 1) * P + t * P],
                                     qcur[rows, t * P:(t + 1) * P],
                                     kT[rows, b, 0:(t + 1) * P], start=True, stop=True)
                        ins.then_inc(s_full, 1)

                    def t_unit(u):
                        pe.wait_ge(weighed, i * 4 + (u + 1) + 1)
                        pe.wait_ge(pT_done, i * 4 + u + 1)
                        if u == 0:
                            pe.wait_ge(poolT_done, 1)
                        for c in range(3):
                            ins = nc.tensor.transpose(bank[6][:, c * P:(c + 1) * P], sP[:, u % 2, c * P:(c + 1) * P], ident)
                        ins.then_inc(pT_full, 1)

                    def pv_units(b):
                        pe.wait_ge(pT_done, i * 4 + (2 * b + 2) + 1)
                        if b == 0:
                            pe.wait_ge(hid_done, 1)
                            pe.wait_ge(o_read, i + 1)
                        for kt in range(NT):
                            for g in range(KVG):
                                d = slice(g * HD, (g + 1) * HD)
                                q, p = (slice(0, T), slice(0, T)) if kt == 0 else (slice(P, T), slice(2 * P, 3 * P))
                                ins = mm(bank[7][d, q], vN[:, b, kt, d], sPT[:, g, p], start=(b == 0 and kt == 0), stop=(b == 1 and kt == 1))
                        ins.then_inc(pv_full, 1)

                    s_unit(0)
                    s_unit(1)
                    pe.wait_ge(ga_done, i + 1)
                    pair(bank[0], n, 0, ga_full, i2)
                    t_unit(0)
                    s_unit(2)
                    pe.wait_ge(gb_done, i + 1)
                    split(n, 1, i2)
                    w = parts(n, 1, 2 * P)
                    channels(bank[1][:, 0:T], w, 0)
                    t_unit(1)
                    s_unit(3)
                    channels(bank[1][:, T:2 * T], w, P).then_inc(gb_full, 1)
                    pv_units(0)
                    t_unit(2)
                    pe.wait_ge(merge_done, i + 1)
                    pe.wait_ge(proj_split, i + 1)
                    pe.wait_ge(mix_split, 2)
                    project(bank[2], 0).then_inc(yp_full, 1)
                    t_unit(3)
                    project(bank[3], 1).then_inc(yc_full, 1)
                    pv_units(1)

            pe.wait_ge(ga_done, N_MG + 1)
            pair(bank[0], CH_M0A, 0, m0_full)
            pe.wait_ge(hidT_done, 1)
            for g in range(KVG):
                for ht in range(2):
                    mm(bank[4][g * HD:(g + 1) * HD, 0:16], cw2[:, ht], hidT[:, ht, g, 0:16], start=(ht == 0), stop=(ht == 1))
            for g in range(KVG):
                for r in range(REP):
                    for ht in range(2):
                        ins = mm(bank[4][32 * r:32 * r + 32, 64 + g * HD:64 + (g + 1) * HD], hidT[:, 2 + ht, g], cw2[:, 2 + ht],
                                 start=(ht == 0), stop=(ht == 1))
            ins.then_inc(kc_full, 1)
            pe.wait_ge(gb_done, N_MG + 1)
            pair(bank[1], CH_M0A, 1, m0_full)
            pe.wait_ge(kc_done, 1)
            pe.wait_ge(o_read, N_MG + 1)
            for g in range(KVG):
                rows = slice(g * HD, (g + 1) * HD)
                for r in range(REP):
                    ins = mm(bank[(5, 7)[g]][32 * r:32 * r + 32, 0:T], kcT[rows], qT[rows, r], start=True, stop=True)
            ins.then_inc(scT_full, 1)
            pe.wait_ge(merge_done, N_MG + 1)
            pair(bank[2], CH_M0B, 0, m0_full)
            pe.wait_ge(scT_done, 1)
            pe.wait_ge(pT_done, N_MG * 4 + 1)
            for t in range(NT):
                for g in range(KVG):
                    ins = nc.tensor.transpose(bank[6][:, (2 * t + g) * P:(2 * t + g + 1) * P], scT[:, g * T + t * P:g * T + (t + 1) * P], ident)
            ins.then_inc(sc_full, 1)
            split(CH_M0B, 1)
            w = parts(CH_M0B, 1, 2 * P)
            channels(bank[3][:, 0:T], w, 0)
            pe.wait_ge(pc_done, 1)
            for t in range(NT):
                for g in range(KVG):
                    src = pc[:, t * HEADS + g * REP:t * HEADS + (g + 1) * REP].rearrange("p a c -> p (a c)")
                    ins = nc.tensor.transpose(bank[7][:, (2 * t + g) * P:(2 * t + g + 1) * P], src, ident)
            ins.then_inc(pcT_full, 1)
            channels(bank[3][:, T:2 * T], w, P).then_inc(m0_full, 1)
            pe.wait_ge(pcT_done, 1)
            for r in range(REP):
                for g in range(KVG):
                    ins = mm(bank[4 + r // 2][g * HD:(g + 1) * HD, (r % 2) * T:(r % 2 + 1) * T], vbd[:, g, r * HD:(r + 1) * HD],
                             pcT.rearrange("p (t g) q -> p g t q", g=KVG)[:, g], start=True, stop=True)
                if r % 2:
                    ins.then_inc(oc_full, 1)
            pe.wait_ge(oT_done, 2)

            def nsa(n):
                split(CH_NSA, n // 2)
                for a in range(2):
                    ins = channels(bank[(4, 5, 0, 1)[n]][:, a * T:(a + 1) * T], parts(CH_NSA, n // 2, 4 * P), (2 * (n % 2) + a) * P, 4,
                                   ohi.bitcast(F32R), olo.bitcast(F32R))
                ins.then_inc(yn_full, 1)

            for n in range(4):
                if n > 1:
                    pe.wait_ge(m0_done, n - 1)
                nsa(n)

            def output(n, k):
                t, half = n % 2, n // 2
                whi, wlo = parts(CH_WO + k // 4, k // 2 % 2, D)
                cols, wc = slice(t * P, (t + 1) * P), slice(half * 512, (half + 1) * 512)
                mh, ml = mhi[k // 4][:, k % 4].bitcast(F32R), mlo[:, k].bitcast(F32R)
                dst = bank[(2, 3, 6, 7)[n]][:]
                mm(dst, mh[:, cols], whi[:, k % 2, wc], start=(k == 0), stop=False)
                mm(dst, mh[:, cols], wlo[:, k % 2, wc], start=False, stop=False)
                return mm(dst, ml[:, cols], whi[:, k % 2, wc], start=False, stop=(k == KT - 1))

            pe.wait_ge(m0_done, 4)
            for j in range(2):
                split(CH_WO, j)
                pe.wait_ge(mlo_done, 2)
                for n in range(4):
                    for k in (2 * j, 2 * j + 1):
                        ins = output(n, k)
                ins.then_inc(wo_used, 1)
            split(CH_WO + 1, 1)
            pe.wait_ge(mlo_done, 4)
            for n in range(4):
                for k in range(4, KT):
                    ins = output(n, k)
                ins.then_inc(wo_full, 1)
            pe.wait_ge(diag_done, 2 * NT)
            turned(4, xn2T_full)
            pe.wait_ge(small_in, 64)
            for k in range(KT):
                pe.wait_ge(xn2T_done, KT)
                ins = mm(bank[0][HD * (k % 2):HD * (k % 2) + HD, 0:T], rw[:, k], xn2T[:, k], start=(k < 2), stop=(k >= KT - 2))
            ins.then_inc(lgT_full, 1)
            pe.wait_ge(lgT_done, 1)
            for t in range(NT):
                c = t * (GROUPS + NE)
                ins = mm(bank[3][:, c:c + GROUPS + NE], lgT[:, t * P:(t + 1) * P], fold2, start=True, stop=True)
            ins.then_inc(logit_full, 1)
            pe.wait_ge(mask_done, 1)
            for t in range(NT):
                ins = mm(bank[2][:, 0:NE], ones, mask[:, t], start=(t == 0), stop=(t == NT - 1))
            ins.then_inc(count_full, 1)
            mm(bank[1][:, 0:NE], tri, mask[:, 0], start=True, stop=True)
            mm(bank[1][:, NE:2 * NE], tri, mask[:, 1], start=True, stop=False)
            mm(bank[1][:, NE:2 * NE], ones, mask[:, 0], start=False, stop=True).then_inc(rank_full, 1)

            pe.wait_ge(passes_done, 1)
            passes = pe.value_load(npass[0:1, 0:1], min_val=1, max_val=MAXPASS)

            def expert(j, q, e):
                return ring[:, (j * NQ + q) % SLOTS, e * 512:(e + 1) * 512]

            def have_expert(j, q):
                c = j * NQ + q
                pe.wait_ge(expert_in[c % SLOTS], bb * (16 * ROUND * NQ // SLOTS) + 16 * (c // SLOTS + 1))

            with pe.Fori(0, passes * (NB // ROUND)) as bb:
                for j in range(ROUND):
                    b = bb * ROUND + j
                    pe.wait_ge(sel_step, b + 1)
                    for half in range(2):
                        for k in range(4):
                            for t in range(NT):
                                ins = mm(bank[2 + half][:, k * P:(k + 1) * P], xn2[:, t, (4 * half + k) * P:(4 * half + k + 1) * P],
                                         flat(sel[:, t]), start=(t == 0), stop=(t == NT - 1))
                        ins.then_inc(xg_full, 1)
                    pe.wait_ge(sel_done, b + 1)
                    pe.wait_ge(hT_done, b + 1)
                    for t in range(NT):
                        ins = nc.tensor.transpose(bank[1][:, t * P:(t + 1) * P], flat(selw[:, t]), ident)
                    ins.then_inc(cmb_full, 1)
                    pe.wait_ge(xg_done, b * 2 + 2)
                    pe.wait_ge(hn_done, b + 1)
                    for q in range(NQ1):
                        have_expert(j, q)
                        for e in range(EB):
                            ins = mm(bank[0][CAP * e:CAP * (e + 1)], xgT[:, q, CAP * e:CAP * (e + 1)],
                                     expert(j, q, e), start=(q == 0), stop=(q == NQ1 - 1))
                        if q == NQ1 - 1:
                            ins.then_inc(hid1_full, 1)
                        else:
                            ins.then_inc(expert_used, 1)
                    pe.wait_ge(hn_done, b + 2)
                    pe.wait_ge(cmb_done, b + 1)
                    pe.sem_inc(expert_used, 1)
                    for k in range(HT):
                        ins = nc.tensor.transpose(bank[1][:, k * P:(k + 1) * P], hN[:, k * P:(k + 1) * P], ident)
                    ins.then_inc(hT_full, 1)
                    pe.wait_ge(hT_done, b + 2)

                    def second(half, ht):
                        q = NQ1 + HT * half + ht
                        if ht == 0:
                            pe.wait_ge(yn_done, b * 2 + half + 1)
                        have_expert(j, q)
                        for e in range(EB):
                            ins = mm(bank[4 + half][CAP * e:CAP * (e + 1)], hT[:, ht, CAP * e:CAP * (e + 1)],
                                     expert(j, q, e), start=(ht == 0), stop=(ht == HT - 1))
                        return ins

                    def combine(half):
                        pe.wait_ge(yn_done, b * 2 + (half + 1) + 1)
                        for t in range(NT):
                            pe.wait_ge(add_done, b * 4 + max(2 * half + t - 1, 0) + 3)
                            mm(bank[6 + t][:], cmbT[:, t * P:(t + 1) * P], yN[:, half * 512:(half + 1) * 512],
                               start=True, stop=True).then_inc(comb_done, 1)

                    second(0, 0).then_inc(expert_used, 1)
                    second(0, 1).then_inc(y_full, 1)
                    combine(0)
                    second(1, 0).then_inc(expert_used, 2)
                    second(1, 1).then_inc(y_full, 1)
                    combine(1)
                    pe.sem_inc(expert_used, 1)


def constants():
    import numpy as np
    c = np.zeros((P, K_N), np.float32)
    q = np.arange(P)[:, None]
    far = np.float32(-1e34)
    c[:, K_ID:K_ID + P] = np.eye(P)
    key = np.arange(P)[None, :]
    c[:, K_DIST:K_DIST + P] = np.where(key <= q, key - q, far)
    key = np.arange(2 * P)[None, :]
    c[:, K_DIST + P:K_DIST + 3 * P] = np.where(key <= q + P, key - (q + P), far)
    c[:, K_TRI:K_TRI + P] = q < np.arange(P)[None, :]
    c[:, K_ONE:K_ONE + P] = 1.0
    c[:, K_IOTA:K_IOTA + CAP] = np.arange(1, CAP + 1)
    slopes = 2.0 ** (-8.0 * np.arange(1, HEADS + 1) / HEADS)
    for t in range(NT):
        d = t * P + q - (np.arange(16)[None, :] * CMP_STRIDE + CMP_LEN - 1)
        ok = (d >= 0) & (np.arange(16)[None, :] < NCMP)
        c[:, K_CM + t * 16:K_CM + (t + 1) * 16] = ok
        for hd in range(HEADS):
            o = K_CB + (t * HEADS + hd) * 16
            c[:, o:o + 16] = np.where(ok, -slopes[hd] * d, far)
    tt = np.arange(T)
    for a in range(2):
        for g in range(2):
            c[g * HD:(g + 1) * HD, K_IC + a * T:K_IC + (a + 1) * T] = 1.0 / np.minimum(tt + 1, POOL_WINDOWS[2 * a + g])
    c[:, K_SL:K_SL + HEADS] = slopes
    c[:, K_FOLD:K_FOLD + 32] = q % 32 == np.arange(32)[None, :]
    c[:, K_FOLD2:K_N] = q % HD == np.arange(GROUPS + NE)[None, :]
    c[:, K_CAP:K_CAP + MAXPASS] = CAP * np.arange(MAXPASS)
    c[:, K_RK:K_RK + PER_GROUP] = PER_GROUP - np.arange(PER_GROUP)
    return c


def kernel(**inputs):
    import numpy as np
    import concourse.bacc as bacc
    from concourse.bass_utils import run_bass_kernel_spmd as run

    a = {k: np.asarray(v) for k, v in inputs.items()}

    def tiles(w):
        return w.reshape(-1, P, w.shape[1]).transpose(1, 0, 2).reshape(P, -1)

    w_in = a["w_in"][0]
    o_kv, o_gate = HEADS * HD, HEADS * HD + 6 * KVG * HD
    o_u = o_gate + GATES
    o_m = o_u + 4 * 256
    wq = w_in[:, 0:o_kv].reshape(D, KVG, REP, HD).transpose(0, 2, 1, 3).reshape(D, HEADS * HD)
    front = np.zeros((N_CHUNKS, 2, P, SLOT), np.float32)

    def put(n, w, by_columns=True):
        for half, part in enumerate(np.split(w, 2, axis=1 if by_columns else 0)):
            part = tiles(part)
            front[n, half, :, 0:part.shape[1]] = part

    def gate(i, c0, n):
        return w_in[:, o_m + i * D + c0:o_m + i * D + c0 + n]

    k_cmp, v_cmp, k_slc, v_slc, k_win, v_win = (w_in[:, o_kv + P * i:o_kv + P * (i + 1)] for i in range(6))
    put(CH_Q, wq)
    put(CH_KV, np.concatenate([k_cmp, v_cmp, k_slc, k_win], axis=1))
    put(CH_VG, np.concatenate([v_slc, v_win, w_in[:, o_gate:o_u]], axis=1), False)
    put(CH_UH, w_in[:, o_u:o_u + 512])
    put(CH_BC, w_in[:, o_u + 512:o_m])
    put(CH_CK, a["cmp_w1"][0, 0], False)
    put(CH_CV, a["cmp_w1"][0, 1], False)
    for i in range(N_MG):
        put(CH_MG + i, np.concatenate([gate(1, 256 * i, 256), gate(2, 256 * i, 256)], axis=1))
    projs = np.stack([np.concatenate([tiles(a[w][0][:, 256 * i:256 * i + 256]) for w in ("w_pool_proj", "w_conv_proj")], axis=1)
                      for i in range(N_MG)])
    put(CH_M0A, gate(0, 0, 512))
    put(CH_M0B, gate(0, 512, 512))
    put(CH_NSA, a["w_nsa_proj"][0].reshape(KVG, REP, HD, D).transpose(1, 0, 2, 3).reshape(HEADS * HD, D))
    for i in range(2):
        put(CH_WO + i, a["w_o"][0][512 * i:512 * i + 512], False)

    params = np.concatenate([
        a["norm1_g"][0].reshape(KT, P), a["pool_scale"][0].reshape(2, P), a["conv_w"][0].reshape(2 * CONV_K, P),
        a["cmp_pe"][0].reshape(CMP_LEN, P), a["norm2_g"][0].reshape(KT, P)]).T
    wgrp = np.zeros((P, 2, P), np.float32)
    for g in range(4):
        o = (g % 2) * HD
        wgrp[o:o + HD, g // 2, o:o + HD] = a["pool_w"][0, g]

    w1 = a["expert_w1"][0].reshape(NB, EB, NQ1, P, HID)
    w3 = a["expert_w3"][0].reshape(NB, EB, NQ1, P, HID)
    w2 = a["expert_w2"][0].reshape(NB, EB, HT, P, 2, 512)
    experts = np.concatenate([
        np.concatenate([w1, w3], axis=4).transpose(0, 2, 3, 1, 4).reshape(NB, NQ1, P, ECHUNK),
        w2.transpose(0, 4, 2, 3, 1, 5).reshape(NB, NQ2, P, ECHUNK)], axis=1)

    arrays = {
        "x": a["x"][0],
        "params": params,
        "consts": constants(),
        "front": front,
        "projs": projs,
        "small": tiles(a["cmp_w2"][0].reshape(2 * HID, HD)),
        "wgrp": wgrp.reshape(P, 2 * P),
        "vecs": np.stack([a["norm2_g"][0], a["final_norm_g"]]),
        "routerw": tiles(np.pad(np.concatenate([a["router_group_w"][0], a["router_expert_w"][0]], axis=1),
                                ((0, 0), (0, HD - GROUPS - NE)))),
        "routerb": np.concatenate([a["router_group_b"][0], a["router_expert_b"][0]])[None],
        "experts": experts,
    }
    nc = bacc.Bacc("TRN2", target_bir_lowering=False, num_devices=1)
    args, feed = [], {}
    for name, v in arrays.items():
        feed[f"in_{name}"] = np.ascontiguousarray(v)
        args.append(nc.dram_tensor(f"in_{name}", v.shape, F32, kind="ExternalInput").ap())
    args.append(nc.dram_tensor("out_y", (T, D), F32, kind="ExternalOutput").ap())
    build(nc, *args)
    r = run(nc, [feed], core_ids=[0])
    return r.results[0]["out_y"].reshape(1, T, D)
```
